# Optimizing a Trainium2 kernel written in Bass

```python
import math
import jax
import jax.numpy as jnp
from jax import lax
import numpy as np

D_MODEL = 1024
BATCH = 1
SEQ = 1024
DEPTH = 1
DEC_BATCH = 8
DEC_SEQ = 4
PAST_LEN = 1024
PAGE_SIZE = 128

NSA_HEADS = 8
NSA_KV_HEADS = 2
NSA_GROUP = NSA_HEADS // NSA_KV_HEADS
HEAD_DIM = 64
NSA_WIDTH = NSA_HEADS * HEAD_DIM
NSA_KV_WIDTH = NSA_KV_HEADS * HEAD_DIM
CMP_BLOCK = 32
CMP_STRIDE = 16
CMP_HIDDEN = 64
SEL_BLOCK = 64
N_SEL = 16
WINDOW = 512
Q_BLOCK = 128

GDN_HEADS = 8
GDN_DK = 64
GDN_DV = 64
GDN_QK_WIDTH = GDN_HEADS * GDN_DK
GDN_WIDTH = GDN_HEADS * GDN_DV
CONV_W = 4
CONV_DIM = 2 * GDN_QK_WIDTH + GDN_WIDTH
GDN_CHUNK = 64

IN_SIZES = (NSA_WIDTH, 6 * NSA_KV_WIDTH, 3 * NSA_HEADS, NSA_WIDTH, CONV_DIM, GDN_HEADS, GDN_HEADS, GDN_WIDTH, 2 * D_MODEL)
IN_WIDTH = NSA_WIDTH + 6 * NSA_KV_WIDTH + 3 * NSA_HEADS + NSA_WIDTH + CONV_DIM + 2 * GDN_HEADS + GDN_WIDTH + 2 * D_MODEL
EPS = 1e-6

kernel_name = 'hybrid_nsa_gdn_step'

def _rmsnorm(x, g):
    xf = x.astype(jnp.float32)
    y = xf * lax.rsqrt(jnp.mean(xf * xf, axis=-1, keepdims=True) + EPS)
    return (y * g.astype(jnp.float32)).astype(x.dtype)

def _l2norm(x):
    xf = x.astype(jnp.float32)
    return xf * lax.rsqrt(jnp.sum(xf * xf, axis=-1, keepdims=True) + EPS)

def _alibi_slopes():
    h = np.arange(1, NSA_HEADS + 1, dtype=np.float32)
    s = np.power(np.float32(2.0), -np.float32(8.0) * h / np.float32(NSA_HEADS))
    return jnp.asarray(s, dtype=jnp.float32).reshape(NSA_KV_HEADS, NSA_GROUP)

def _masked_softmax(s, mask):
    s = jnp.where(mask, s, -jnp.inf)
    m = jnp.max(s, axis=-1, keepdims=True)
    m = jnp.where(jnp.isfinite(m), m, 0.0)
    p = jnp.exp(s - m)
    return p / jnp.maximum(jnp.sum(p, axis=-1, keepdims=True), 1e-30)

def _to_groups(a):
    B, T = a.shape[:2]
    return a.reshape(B, T, NSA_KV_HEADS, NSA_GROUP, -1).transpose(0, 2, 3, 1, 4)

def _compress(rows, pe, w1, w2):
    B, L, G, dk = rows.shape
    r_cnt = CMP_BLOCK // CMP_STRIDE
    n16 = L // CMP_STRIDE
    n_cmp = n16 - r_cnt + 1
    ch = rows[:, :n16 * CMP_STRIDE].reshape(B, n16, CMP_STRIDE, G, dk)
    w1r = w1.reshape(r_cnt, CMP_STRIDE, dk, CMP_HIDDEN)
    pre = jnp.einsum('sd,sde->e', pe, w1)
    for r in range(r_cnt):
        pre = pre + jnp.einsum('bnsgd,sde->bnge', ch[:, r:r + n_cmp], w1r[r])
    return jnp.einsum('bnge,ed->bngd', jax.nn.silu(pre), w2)

def _cmp_to_sel(n_cmp, n_blk):
    i = np.arange(n_cmp)[:, None] * CMP_STRIDE
    j = np.arange(n_blk)[None, :] * SEL_BLOCK
    ov = np.minimum(i + CMP_BLOCK, j + SEL_BLOCK) - np.maximum(i, j)
    return jnp.asarray(np.clip(ov, 0, None).astype(np.float32) / np.float32(CMP_BLOCK))

def _cmp_attend(q, kc, vc, t, slopes):
    n_cmp = kc.shape[1]
    end = jnp.arange(n_cmp) * CMP_STRIDE + (CMP_BLOCK - 1)
    dist = t[:, None] - end[None, :]
    s = jnp.einsum('bghqd,bcgd->bghqc', q, kc).astype(jnp.float32)
    s = s - slopes[:, :, None, None] * dist.astype(jnp.float32)
    p = _masked_softmax(s, dist >= 0)
    return jnp.einsum('bghqc,bcgd->bghqd', p, vc.astype(jnp.float32)), p

def _select_blocks(p, t, sel_map):
    n_blk = sel_map.shape[1]
    imp = jnp.einsum('bghqc,cn->bgqn', p, sel_map)
    j = jnp.arange(n_blk)[None, :]
    cur = (t // SEL_BLOCK)[:, None]
    valid = j <= cur
    forced = valid & ((j == 0) | (j == cur) | (j == cur - 1))
    score = jnp.where(forced, jnp.inf, jnp.where(valid, imp, -jnp.inf))
    return lax.top_k(score, min(N_SEL, n_blk))[1]

def _sel_attend(q, rows, idx, t, slopes):
    B, G, Q, K = idx.shape
    pos = (idx[..., None] * SEL_BLOCK + jnp.arange(SEL_BLOCK)).reshape(B, G, Q, K * SEL_BLOCK)
    ks = rows[..., 0, :].reshape(B, G, Q, K * SEL_BLOCK, HEAD_DIM)
    vs = rows[..., 1, :].reshape(B, G, Q, K * SEL_BLOCK, HEAD_DIM)
    dist = t[:, None] - pos
    s = jnp.einsum('bghqd,bgqkd->bghqk', q, ks).astype(jnp.float32)
    s = s - slopes[:, :, None, None] * dist[:, :, None].astype(jnp.float32)
    p = _masked_softmax(s, dist[:, :, None] >= 0)
    return jnp.einsum('bghqk,bgqkd->bghqd', p, vs.astype(jnp.float32))

def _win_attend(q, kv, kpos, t, slopes):
    dist = t[:, None] - kpos[None, :]
    mask = (dist >= 0) & (dist < WINDOW) & (kpos >= 0)[None, :]
    s = jnp.einsum('bghqd,bsgd->bghqs', q, kv[:, :, 0]).astype(jnp.float32)
    s = s - slopes[:, :, None, None] * dist.astype(jnp.float32)
    p = _masked_softmax(s, mask)
    return jnp.einsum('bghqs,bsgd->bghqd', p, kv[:, :, 1].astype(jnp.float32))

def _combine(g, o_c, o_s, o_w):
    return g[..., 0:1] * o_c + g[..., 1:2] * o_s + g[..., 2:3] * o_w

def _nsa_prompt(q, kv_cmp, kv_sel, kv_win, gates, cmpk, cmpv):
    B, T = q.shape[:2]
    slopes = _alibi_slopes()
    qg = _to_groups(q.reshape(B, T, NSA_HEADS, HEAD_DIM)) * HEAD_DIM ** -0.5
    gg = _to_groups(jax.nn.sigmoid(gates.reshape(B, T, NSA_HEADS, 3)))
    kc = _compress(kv_cmp[:, :, 0], *cmpk)
    vc = _compress(kv_cmp[:, :, 1], *cmpv)
    n_blk = -(-T // SEL_BLOCK)
    sel_map = _cmp_to_sel(kc.shape[1], n_blk)
    zpad = ((0, 0), (0, 0), (0, 0))
    sel = jnp.pad(kv_sel, ((0, 0), (0, n_blk * SEL_BLOCK - T)) + zpad)
    sel = sel.reshape(B, n_blk, SEL_BLOCK, 2, NSA_KV_HEADS, HEAD_DIM).transpose(0, 4, 1, 2, 3, 5)
    win = jnp.pad(kv_win, ((0, 0), (WINDOW, 0)) + zpad)

    def block(i):
        q0 = i * Q_BLOCK
        t = q0 + jnp.arange(Q_BLOCK)
        qb = lax.dynamic_slice_in_dim(qg, q0, Q_BLOCK, axis=3)
        gb = lax.dynamic_slice_in_dim(gg, q0, Q_BLOCK, axis=3)
        o_c, p = _cmp_attend(qb, kc, vc, t, slopes)
        idx = _select_blocks(p, t, sel_map)
        rows = jax.vmap(jax.vmap(lambda sb, ix: sb[ix]))(sel, idx)
        o_s = _sel_attend(qb, rows, idx, t, slopes)
        wb = lax.dynamic_slice_in_dim(win, q0, WINDOW + Q_BLOCK, axis=1)
        kpos = q0 - WINDOW + jnp.arange(WINDOW + Q_BLOCK)
        o_w = _win_attend(qb, wb, kpos, t, slopes)
        return _combine(gb, o_c, o_s, o_w)

    o = lax.map(block, jnp.arange(T // Q_BLOCK))
    return o.transpose(1, 0, 4, 2, 3, 5).reshape(B, T, NSA_WIDTH)

def _nsa_sample(q, kv_cmp, kv_sel, kv_win, gates, cache_cmp, cache_sel, cache_win, page_table, layer, cmpk, cmpv):
    Bd, Tn = q.shape[:2]
    L = PAST_LEN + Tn
    t = PAST_LEN + jnp.arange(Tn)
    slopes = _alibi_slopes()
    qg = _to_groups(q.reshape(Bd, Tn, NSA_HEADS, HEAD_DIM)) * HEAD_DIM ** -0.5
    gg = _to_groups(jax.nn.sigmoid(gates.reshape(Bd, Tn, NSA_HEADS, 3)))
    past = cache_cmp[layer, page_table].reshape(Bd, PAST_LEN, 2, NSA_KV_HEADS, HEAD_DIM)
    full = jnp.concatenate([past, kv_cmp], axis=1)
    kc = _compress(full[:, :, 0], *cmpk)
    vc = _compress(full[:, :, 1], *cmpv)
    o_c, p = _cmp_attend(qg, kc, vc, t, slopes)
    n_blk = -(-L // SEL_BLOCK)
    idx = _select_blocks(p, t, _cmp_to_sel(kc.shape[1], n_blk))
    n_past_blk = PAST_LEN // SEL_BLOCK
    n_new_blk = n_blk - n_past_blk
    per_page = PAGE_SIZE // SEL_BLOCK
    off = jnp.arange(SEL_BLOCK)
    b_ix = jnp.arange(Bd)[:, None, None, None]
    g_ix = jnp.arange(NSA_KV_HEADS)[None, :, None, None, None]
    jp = jnp.minimum(idx, n_past_blk - 1)
    phys = page_table[b_ix, jp // per_page]
    in_page = ((jp % per_page) * SEL_BLOCK)[..., None] + off
    past_rows = cache_sel[layer, phys[..., None], in_page, :, g_ix]
    new = jnp.pad(kv_sel, ((0, 0), (0, n_new_blk * SEL_BLOCK - Tn), (0, 0), (0, 0), (0, 0)))
    jn = jnp.clip(idx - n_past_blk, 0, n_new_blk - 1)
    new_rows = new[b_ix[..., None], (jn * SEL_BLOCK)[..., None] + off, :, g_ix]
    rows = jnp.where((idx < n_past_blk)[..., None, None, None], past_rows, new_rows.astype(past_rows.dtype))
    o_s = _sel_attend(qg, rows, idx, t, slopes)
    kw = jnp.concatenate([cache_win, kv_win.astype(cache_win.dtype)], axis=1)
    nbuf = cache_win.shape[1]
    kpos = PAST_LEN - nbuf + jnp.arange(nbuf + Tn)
    o_w = _win_attend(qg, kw, kpos, t, slopes)
    o = _combine(gg, o_c, o_s, o_w)
    keep = min(WINDOW, nbuf + Tn)
    return o.transpose(0, 3, 1, 2, 4).reshape(Bd, Tn, NSA_WIDTH), kw[:, nbuf + Tn - keep:]

def _short_conv(u, buf, w, b):
    T = u.shape[1]
    ext = jnp.concatenate([buf.astype(u.dtype), u], axis=1)
    y = b
    for i in range(CONV_W):
        y = y + ext[:, i:i + T] * w[i]
    return jax.nn.silu(y), ext[:, T:]

def _gated_delta(q, k, v, g, beta, s0):
    B, T, H, dk = k.shape
    dv = v.shape[-1]
    C = min(GDN_CHUNK, T)
    n = -(-T // C)
    pad = n * C - T

    def ch4(a):
        a = jnp.pad(a.astype(jnp.float32), ((0, 0), (0, pad), (0, 0), (0, 0)))
        return a.reshape(B, n, C, H, a.shape[-1]).transpose(1, 0, 3, 2, 4)

    def ch3(a):
        a = jnp.pad(a.astype(jnp.float32), ((0, 0), (0, pad), (0, 0)))
        return a.reshape(B, n, C, H).transpose(1, 0, 3, 2)

    qc = ch4(q) * dk ** -0.5
    kc = ch4(k)
    vc = ch4(v)
    bc = ch3(beta)
    gc = jnp.cumsum(ch3(g), axis=-1)
    i = jnp.arange(C)
    tri = i[:, None] >= i[None, :]
    strict = i[:, None] > i[None, :]
    decay = jnp.exp(jnp.where(tri, gc[..., :, None] - gc[..., None, :], -jnp.inf))
    kb = kc * bc[..., None]
    lmat = jnp.where(strict, jnp.einsum('...id,...jd->...ij', kb, kc) * decay, 0.0)
    eye = jnp.broadcast_to(jnp.eye(C, dtype=jnp.float32), lmat.shape)
    tmat = lax.linalg.triangular_solve(eye + lmat, eye, left_side=True, lower=True)
    u = tmat @ (vc * bc[..., None])
    w = tmat @ (kb * jnp.exp(gc)[..., None])
    a_intra = jnp.where(tri, jnp.einsum('...id,...jd->...ij', qc, kc) * decay, 0.0)

    def step(s, xs):
        q_, k_, u_, w_, g_, a_ = xs
        v_new = u_ - w_ @ s
        o = (q_ * jnp.exp(g_)[..., None]) @ s + a_ @ v_new
        g_last = g_[..., -1:]
        s = s * jnp.exp(g_last)[..., None] + jnp.einsum('bhcd,bhce->bhde', k_ * jnp.exp(g_last - g_)[..., None], v_new)
        return s, o

    s, o = lax.scan(step, s0.astype(jnp.float32), (qc, kc, u, w, gc, a_intra))
    o = o.transpose(1, 0, 3, 2, 4).reshape(B, n * C, H, dv)[:, :T]
    return o, s

def _gdn(qkv, a, b, z, conv_buf, s0, conv_w, conv_b, a_log, dt_bias, gnorm):
    B, T, _ = qkv.shape
    u, conv_new = _short_conv(qkv, conv_buf, conv_w, conv_b)
    q, k, v = jnp.split(u, [GDN_QK_WIDTH, 2 * GDN_QK_WIDTH], axis=-1)
    q = _l2norm(q.reshape(B, T, GDN_HEADS, GDN_DK))
    k = _l2norm(k.reshape(B, T, GDN_HEADS, GDN_DK))
    v = v.reshape(B, T, GDN_HEADS, GDN_DV)
    beta = jax.nn.sigmoid(b.astype(jnp.float32))
    g = -jnp.exp(a_log.astype(jnp.float32)) * jax.nn.softplus(a.astype(jnp.float32) + dt_bias.astype(jnp.float32))
    o, s_new = _gated_delta(q, k, v, g, beta, s0)
    o = _rmsnorm(o, gnorm).reshape(B, T, GDN_WIDTH) * jax.nn.silu(z)
    return o, conv_new, s_new

def _mix_in(x, c, norm_g, w_ada, b_ada, w_in):
    ada = jax.nn.silu(c) @ w_ada + b_ada
    shift, scale, gate = jnp.split(ada, 3, axis=-1)
    h = _rmsnorm(x, norm_g) * (1.0 + scale[:, None]) + shift[:, None]
    split_pts = np.cumsum(np.array(IN_SIZES))[:-1].tolist()
    return jnp.split(h @ w_in, split_pts, axis=-1), gate

def _mix_out(x, gate, o_a, o_b, gm, w_o_nsa, w_o_gdn, w_out):
    gm_a, gm_b = jnp.split(jax.nn.sigmoid(gm), 2, axis=-1)
    m = gm_a * (o_a @ w_o_nsa) + gm_b * (o_b @ w_o_gdn)
    return x + gate[:, None] * (m @ w_out)

def _layer_prompt(x, c, lw):
    norm_g, w_ada, b_ada, w_in, cmpk, cmpv, conv_w, conv_b, a_log, dt_bias, gnorm, w_o_nsa, w_o_gdn, w_out = lw
    B, T, _ = x.shape
    (q_a, kv_a, g_a, z_a, qkv_b, a_b, b_b, z_b, gm), gate = _mix_in(x, c, norm_g, w_ada, b_ada, w_in)
    kv_a = kv_a.reshape(B, T, 3, 2, NSA_KV_HEADS, HEAD_DIM)
    o_a = _nsa_prompt(q_a, kv_a[:, :, 0], kv_a[:, :, 1], kv_a[:, :, 2], g_a, cmpk, cmpv) * jax.nn.silu(z_a)
    conv0 = jnp.zeros((B, CONV_W - 1, CONV_DIM), qkv_b.dtype)
    s0 = jnp.zeros((B, GDN_HEADS, GDN_DK, GDN_DV), jnp.float32)
    o_b, conv_new, s_new = _gdn(qkv_b, a_b, b_b, z_b, conv0, s0, conv_w, conv_b, a_log, dt_bias, gnorm)
    y = _mix_out(x, gate, o_a, o_b, gm, w_o_nsa, w_o_gdn, w_out)
    return y, (kv_a[:, :, 0], kv_a[:, :, 1], kv_a[:, T - min(WINDOW, T):, 2], conv_new, s_new)

def _layer_sample(x, c, cache_cmp, cache_sel, cache_win, conv_buf, s0, page_table, layer, lw):
    norm_g, w_ada, b_ada, w_in, cmpk, cmpv, conv_w, conv_b, a_log, dt_bias, gnorm, w_o_nsa, w_o_gdn, w_out = lw
    B, T, _ = x.shape
    (q_a, kv_a, g_a, z_a, qkv_b, a_b, b_b, z_b, gm), gate = _mix_in(x, c, norm_g, w_ada, b_ada, w_in)
    kv_a = kv_a.reshape(B, T, 3, 2, NSA_KV_HEADS, HEAD_DIM)
    o_a, win_new = _nsa_sample(q_a, kv_a[:, :, 0], kv_a[:, :, 1], kv_a[:, :, 2], g_a, cache_cmp, cache_sel, cache_win, page_table, layer, cmpk, cmpv)
    o_a = o_a * jax.nn.silu(z_a)
    o_b, conv_new, s_new = _gdn(qkv_b, a_b, b_b, z_b, conv_buf, s0, conv_w, conv_b, a_log, dt_bias, gnorm)
    y = _mix_out(x, gate, o_a, o_b, gm, w_o_nsa, w_o_gdn, w_out)
    return y, (kv_a[:, :, 0], kv_a[:, :, 1], win_new, conv_new, s_new)

def setup_inputs(seed: int = 0) -> dict:
    key = jax.random.key(seed)
    ks = iter(jax.random.split(key, 40))

    def nrm(shape, s):
        return jax.random.normal(next(ks), shape, jnp.float32) * s

    n_pages = PAST_LEN // PAGE_SIZE
    n_pool = (DEC_BATCH * n_pages * 5) // 4
    win_buf = min(WINDOW, PAST_LEN)
    kv_row = (2, NSA_KV_HEADS, HEAD_DIM)
    perm = jax.random.permutation(next(ks), n_pool)
    page_table = perm[:DEC_BATCH * n_pages].reshape(DEC_BATCH, n_pages).astype(jnp.int32)
    dt = jnp.exp(jax.random.uniform(next(ks), (DEPTH, GDN_HEADS), jnp.float32, math.log(1e-3), math.log(1e-1)))
    dt_bias = dt + jnp.log(-jnp.expm1(-dt))
    a_log = jnp.log(jax.random.uniform(next(ks), (DEPTH, GDN_HEADS), jnp.float32, 1.0, 16.0))
    return {
        'x_prompt': nrm((BATCH, SEQ, D_MODEL), 1.0),
        'x_sample': nrm((DEC_BATCH, DEC_SEQ, D_MODEL), 1.0),
        'cache_cmp_kv': nrm((DEPTH, n_pool, PAGE_SIZE) + kv_row, 1.0),
        'cache_sel_kv': nrm((DEPTH, n_pool, PAGE_SIZE) + kv_row, 1.0),
        'cache_win_kv': nrm((DEPTH, DEC_BATCH, win_buf) + kv_row, 1.0),
        'state_conv': nrm((DEPTH, DEC_BATCH, CONV_W - 1, CONV_DIM), 1.0),
        'state_gdn': nrm((DEPTH, DEC_BATCH, GDN_HEADS, GDN_DK, GDN_DV), 0.3),
        'page_table': page_table,
        'c_prompt': nrm((BATCH, D_MODEL), 1.0),
        'c_sample': nrm((DEC_BATCH, D_MODEL), 1.0),
        'norm_g': 1.0 + nrm((DEPTH, D_MODEL), 0.02),
        'w_ada': nrm((DEPTH, D_MODEL, 3 * D_MODEL), 0.5 * D_MODEL ** -0.5),
        'b_ada': nrm((DEPTH, 3 * D_MODEL), 0.02),
        'w_in': nrm((DEPTH, D_MODEL, IN_WIDTH), D_MODEL ** -0.5),
        'cmp_pe_k': nrm((DEPTH, CMP_BLOCK, HEAD_DIM), 0.1),
        'cmp_w1_k': nrm((DEPTH, CMP_BLOCK, HEAD_DIM, CMP_HIDDEN), (CMP_BLOCK * HEAD_DIM) ** -0.5),
        'cmp_w2_k': nrm((DEPTH, CMP_HIDDEN, HEAD_DIM), CMP_HIDDEN ** -0.5),
        'cmp_pe_v': nrm((DEPTH, CMP_BLOCK, HEAD_DIM), 0.1),
        'cmp_w1_v': nrm((DEPTH, CMP_BLOCK, HEAD_DIM, CMP_HIDDEN), (CMP_BLOCK * HEAD_DIM) ** -0.5),
        'cmp_w2_v': nrm((DEPTH, CMP_HIDDEN, HEAD_DIM), CMP_HIDDEN ** -0.5),
        'conv_w': nrm((DEPTH, CONV_W, CONV_DIM), CONV_W ** -0.5),
        'conv_b': nrm((DEPTH, CONV_DIM), 0.02),
        'gdn_a_log': a_log,
        'gdn_dt_bias': dt_bias,
        'gdn_norm_g': 1.0 + nrm((DEPTH, GDN_DV), 0.02),
        'w_o_nsa': nrm((DEPTH, NSA_WIDTH, D_MODEL), NSA_WIDTH ** -0.5),
        'w_o_gdn': nrm((DEPTH, GDN_WIDTH, D_MODEL), GDN_WIDTH ** -0.5),
        'w_out': nrm((DEPTH, D_MODEL, D_MODEL), D_MODEL ** -0.5),
        'final_g': 1.0 + nrm((D_MODEL,), 0.02),
    }

def reference(x_prompt, x_sample, cache_cmp_kv, cache_sel_kv, cache_win_kv, state_conv, state_gdn, page_table,
              c_prompt, c_sample, norm_g, w_ada, b_ada, w_in, cmp_pe_k, cmp_w1_k, cmp_w2_k, cmp_pe_v, cmp_w1_v,
              cmp_w2_v, conv_w, conv_b, gdn_a_log, gdn_dt_bias, gdn_norm_g, w_o_nsa, w_o_gdn, w_out, final_g):
    xp = x_prompt
    xs = x_sample
    sp = []
    ss = []
    for l in range(DEPTH):
        lw = (norm_g[l], w_ada[l], b_ada[l], w_in[l],
              (cmp_pe_k[l], cmp_w1_k[l], cmp_w2_k[l]), (cmp_pe_v[l], cmp_w1_v[l], cmp_w2_v[l]),
              conv_w[l], conv_b[l], gdn_a_log[l], gdn_dt_bias[l], gdn_norm_g[l],
              w_o_nsa[l], w_o_gdn[l], w_out[l])
        xp, st_p = _layer_prompt(xp, c_prompt, lw)
        sp.append(st_p)
        xs, st_s = _layer_sample(xs, c_sample, cache_cmp_kv, cache_sel_kv, cache_win_kv[l], state_conv[l],
                                 state_gdn[l], page_table, l, lw)
        ss.append(st_s)
    y_prompt = _rmsnorm(xp, final_g)
    y_sample = _rmsnorm(xs, final_g)
    new_cmp_kv_prompt = jnp.stack([s[0] for s in sp])
    new_sel_kv_prompt = jnp.stack([s[1] for s in sp])
    new_win_kv_prompt = jnp.stack([s[2] for s in sp])
    new_conv_prompt = jnp.stack([s[3] for s in sp])
    new_gdn_prompt = jnp.stack([s[4] for s in sp])
    new_cmp_kv_sample = jnp.stack([s[0] for s in ss])
    new_sel_kv_sample = jnp.stack([s[1] for s in ss])
    new_win_kv_sample = jnp.stack([s[2] for s in ss])
    new_conv_sample = jnp.stack([s[3] for s in ss])
    new_gdn_sample = jnp.stack([s[4] for s in ss])
    return (y_prompt, y_sample, new_cmp_kv_prompt, new_sel_kv_prompt, new_win_kv_prompt, new_conv_prompt,
            new_gdn_prompt, new_cmp_kv_sample, new_sel_kv_sample, new_win_kv_sample, new_conv_sample,
            new_gdn_sample)


_drawn_inputs = setup_inputs


def setup_inputs(seed=0):
    import zlib

    import numpy as np

    out = dict(_drawn_inputs(seed))
    spreads = {}
    factors = {'cache_sel_kv': 4.241,
     'cmp_pe_k': 8.0,
     'cmp_w1_k': 8.0,
     'cmp_w2_k': 8.0,
     'cmp_pe_v': 8.0,
     'gdn_norm_g': 8.0,
     'final_g': 2.741}
    for name, (base, spread) in spreads.items():
        noise = np.random.default_rng([zlib.crc32(name.encode()), seed]).standard_normal(out[name].shape)
        drawn = base * np.exp(spread * noise) if base else spread * noise
        out[name] = jnp.asarray(drawn.astype(out[name].dtype))
    for name, factor in factors.items():
        out[name] = (out[name] * factor).astype(out[name].dtype)
    return out
```

```python
from contextlib import ExitStack

import numpy as np

import concourse.bass as bass
from concourse import mybir

F32 = mybir.dt.float32
I32 = mybir.dt.int32
ALU = mybir.AluOpType
ACT = mybir.ActivationFunctionType
AX = mybir.AxisListType.X

P = 128
D_MODEL = 1024
SEQ = 1024
NB, NT = 8, 4
NS = NB * NT
TOK = SEQ + NS
KT = D_MODEL // P
TB = TOK // 3
QT = SEQ // P
H, HD = 8, 64
NJ = H // 2
PAGE = 128
NPAGE = 1024 // PAGE
NPOOL = NB * NPAGE * 5 // 4
NCMP = 63
NSEQ = NB + 1
WIN = 512
KVG = 6 * P + 24 + 16
KVH = KVG // 2
A_OFF, B_OFF = 6 * P + 24, 6 * P + 32
RS = 32
NEG = -1.0e30
GUARD = 1.0e25
TINY = 1.17549435e-38
EPS = 1e-6
CW = 1083


def stage_input(nc, T):
    with ExitStack() as ctx:
        sb = lambda n, s, d=F32: ctx.enter_context(nc.sbuf_tensor(n, s, d))
        sem = lambda n: ctx.enter_context(nc.semaphore(n))
        cT = sb("cT", [P, KT, 9])
        wa = [sb(f"wa{i}", [P, KT, 512]) for i in range(3)]
        bada = sb("bada", [9, 3072])
        gT = sb("gT", [P, KT])
        sq = [sb(f"sq{i}", [P, TOK]) for i in range(2)]
        rstd = sb("rstd", [P, TOK])
        modA = sb("modA", [P, KT, 9])
        modB = sb("modB", [P, KT, 9])
        adaP = ctx.enter_context(nc.psum_tensor("adaP", [P, 2, 512], F32))
        sumP = ctx.enter_context(nc.psum_tensor("sumP", [P, 3, 512], F32))
        trP = ctx.enter_context(nc.psum_tensor("trP", [P, 512], F32))
        ld_c, ld_x, ld_b = sem("ld_c"), sem("ld_x"), sem("ld_b")
        ld_wa = [sem(f"ld_wa{i}") for i in range(3)]
        silu_ready, sq_ready, sq_used = sem("silu_ready"), sem("sq_ready"), sem("sq_used")
        ada_prod, ada_ready, ada_t, mod_ready = sem("ada_prod"), sem("ada_ready"), sem("ada_t"), sem("mod_ready")
        inv_ready, rstd_ready, dve_step = sem("inv_ready"), sem("rstd_ready"), sem("dve_step")
        shsc = sb("shsc", [9, 2 * D_MODEL])
        hT, gate, ones, ident = T["hT"], T["gate"], T["ones"], T["ident"]
        ada = [(shsc, n * 512) for n in range(4)] + [(gate, n * 512) for n in range(2)]

        with nc.Block() as block:
            @block.sync
            def _(sp):
                sp.dma_start(cT[:], T["in"]["cT"]).then_inc(ld_c, 16)
                sp.dma_start(ident[:], T["in"]["ident"]).then_inc(ld_b, 16)
                sp.dma_start(bada[:], T["in"]["b_ada"]).then_inc(ld_b, 16)
                sp.dma_start(gT[:], T["in"]["norm_gT"]).then_inc(ld_b, 16)
                for n in range(6):
                    if n >= 3:
                        sp.wait_ge(ada_prod, n - 2)
                    sp.dma_start(wa[n % 3][:], T["in"]["w_ada"][n].rearrange("p (k n) -> p k n", k=KT)).then_inc(ld_wa[n % 3], 16)
                sp.wait_ge(ld_b, 48)

            @block.scalar
            def _(act):
                for k in range(KT):
                    act.dma_start(hT[:, k, :], T["in"]["xT"][:, k, :]).then_inc(ld_x, 16)
                act.wait_ge(ld_c, 16)
                act.activation(cT[:], cT[:], ACT.Silu).then_inc(silu_ready, 1)
                act.wait_ge(ld_x, 16 * KT)
                for k in range(KT):
                    if k >= 2:
                        act.wait_ge(sq_used, k - 1)
                    act.activation(sq[k % 2][:], hT[:, k, :], ACT.Square).then_inc(sq_ready, 1)
                act.wait_ge(inv_ready, 1)
                act.activation(rstd[:], rstd[:], ACT.Sqrt).then_inc(rstd_ready, 1)

            @block.tensor
            def _(pe):
                pe.wait_ge(dve_step, 1)
                for k in range(KT):
                    pe.wait_ge(sq_ready, k + 1)
                    for b in range(3):
                        mm = pe.matmul(sumP[:, b, 0:TB], ones[:], sq[k % 2][:, b * TB:(b + 1) * TB],
                                       start=(k == 0), stop=(k == KT - 1))
                    mm.then_inc(sq_used, 1)
                pe.wait_ge(silu_ready, 1)
                for n in range(6):
                    pe.wait_ge(ld_wa[n % 3], 16 * (n // 3 + 1))
                    if n >= 2:
                        pe.wait_ge(ada_ready, n - 1)
                    for k in range(KT):
                        mm = pe.matmul(adaP[0:9, n % 2, :], cT[:, k, :], wa[n % 3][:, k, :],
                                       start=(k == 0), stop=(k == KT - 1))
                    mm.then_inc(ada_prod, 1)
                pe.wait_ge(ada_ready, 4)
                pe.wait_ge(ld_b, 48)
                for k in range(16):
                    mm = pe.transpose(trP[:, k * 9:k * 9 + 9], shsc[:, k * P:(k + 1) * P], ident[0:9, 0:9])
                mm.then_inc(ada_t, 1)

            @block.vector
            def _(dve):
                dve.memset(ones[:], 1.0).then_inc(dve_step, 1)
                dve.wait_ge(sq_used, KT)
                dve.tensor_scalar(rstd[:].rearrange("p (b t) -> p b t", b=3), sumP[:, :, 0:TB], 1.0 / D_MODEL, EPS, ALU.mult, ALU.add).then_inc(dve_step, 1)
                dve.wait_ge(dve_step, 2)
                dve.reciprocal(rstd[:], rstd[:]).then_inc(inv_ready, 1)
                dve.wait_ge(ld_b, 48)
                for n in range(6):
                    dve.wait_ge(ada_prod, n + 1)
                    dst, at = ada[n]
                    dve.tensor_tensor(dst[:, at:at + 512], adaP[0:9, n % 2, :],
                                      bada[:, n * 512:(n + 1) * 512], ALU.add).then_inc(ada_ready, 1)
                dve.wait_ge(ada_t, 1)
                dve.tensor_copy(modB[:], trP[:, 0:72].rearrange("p (k r) -> p k r", k=KT)).then_inc(mod_ready, 1)
                dve.tensor_scalar(modA[:], trP[:, 72:144].rearrange("p (k r) -> p k r", k=KT), 1.0, None, ALU.add).then_inc(mod_ready, 1)
                dve.wait_ge(mod_ready, 2)
                dve.tensor_tensor(modA[:], modA[:], gT[:].unsqueeze(2).to_broadcast([P, KT, 9]), ALU.mult).then_inc(mod_ready, 1)
                dve.wait_ge(rstd_ready, 1)
                dve.wait_ge(mod_ready, 3)
                for k in range(KT):
                    dve.tensor_tensor(hT[:, k, :], hT[:, k, :], rstd[:], ALU.mult).then_inc(dve_step, 1)
                dve.wait_ge(dve_step, 2 + KT)
                for k in range(KT):
                    dve.tensor_scalar(hT[:, k, 0:SEQ], hT[:, k, 0:SEQ], modA[:, k, 8:9], modB[:, k, 8:9], ALU.mult, ALU.add)
                    hs = hT[:, k, SEQ:TOK].rearrange("p (b t) -> p b t", b=NB)
                    dve.tensor_tensor(hs, hs, modA[:, k, 0:NB].unsqueeze(2).to_broadcast([P, NB, NT]), ALU.mult).then_inc(dve_step, 1)
                dve.wait_ge(dve_step, 2 + 2 * KT)
                for k in range(KT):
                    hs = hT[:, k, SEQ:TOK].rearrange("p (b t) -> p b t", b=NB)
                    dve.tensor_tensor(hs, hs, modB[:, k, 0:NB].unsqueeze(2).to_broadcast([P, NB, NT]), ALU.add)


def product_features(pe, out, w, x, ft, first_wait=None):
    for k in range(KT):
        for b in range(3):
            mm = pe.matmul(out[:, b, 0:TB], w[:, k, ft * P:(ft + 1) * P], x[:, k, b * TB:(b + 1) * TB],
                           start=(k == 0), stop=(k == KT - 1))
    return mm


def stage_nsa_project(nc, T):
    with ExitStack() as ctx:
        sb = lambda n, s, d=F32: ctx.enter_context(nc.sbuf_tensor(n, s, d))
        sem = lambda n: ctx.enter_context(nc.semaphore(n))
        w = [sb(f"w{i}", [P, KT, 256]) for i in range(2)]
        wt = [sb(f"wt{i}", [P, KT, KVH]) for i in range(2)]
        featP = [ctx.enter_context(nc.psum_tensor(f"featP{i}", [P, 3, 512], F32)) for i in range(2)]
        tokP = ctx.enter_context(nc.psum_tensor("tokP", [P, 2, 512], F32))
        ld_w = [sem(f"ld_w{i}") for i in range(2)]
        ld_wt, feat_prod, feat_out = sem("ld_wt"), sem("feat_prod"), sem("feat_out")
        tok_prod, tok_out, ab_clear = sem("tok_prod"), sem("tok_out"), sem("ab_clear")
        hT, kvt = T["hT"], T["kvt"]
        dests = [(2 * blk + n, dst, 2 * n, fn, scale) for blk, dst, fn, scale in
                 ((0, T["qT"], ACT.Copy, HD ** -0.5), (1, T["zaT"], ACT.Silu, 1.0), (5, T["zbT"], ACT.Silu, 1.0)) for n in range(2)]
        tiles = [(t, h) for t in range(QT + 1) for h in range(2)]

        with nc.Block() as block:
            @block.sync
            def _(sp):
                for n in range(2):
                    sp.dma_start(wt[n][:], T["in"]["w_tok"][n].rearrange("p (k n) -> p k n", k=KT)).then_inc(ld_wt, 16)
                for n, (blk, _, _, _, _) in enumerate(dests):
                    if n >= 2:
                        sp.wait_ge(feat_prod, 2 * (n - 1))
                    sp.dma_start(w[n % 2][:], T["in"]["w_feat"][blk].rearrange("p (k n) -> p k n", k=KT)).then_inc(ld_w[n % 2], 16)

            @block.tensor
            def _(pe):
                pe.wait_ge(ld_wt, 32)
                for n, (t, h) in enumerate(tiles):
                    m = P if t < QT else NS
                    if n >= 2:
                        pe.wait_ge(tok_out, n - 1)
                    for k in range(KT):
                        mm = pe.matmul(tokP[0:m, n % 2, 0:KVH], hT[:, k, t * P:t * P + m], wt[h][:, k, :],
                                       start=(k == 0), stop=(k == KT - 1))
                    mm.then_inc(tok_prod, 1)
                for n in range(len(dests)):
                    pe.wait_ge(ld_w[n % 2], 16 * (n // 2 + 1))
                    for ft in range(2):
                        u = 2 * n + ft
                        if u >= 2:
                            pe.wait_ge(feat_out, u - 1)
                        mm = product_features(pe, featP[u % 2], w[n % 2], hT, ft)
                        mm.then_inc(feat_prod, 1)

            @block.vector
            def _(dve):
                for n, (t, h) in enumerate(tiles):
                    m = P if t < QT else NS
                    dve.wait_ge(tok_prod, n + 1)
                    dve.tensor_copy(kvt[0:m, t, h * KVH:(h + 1) * KVH], tokP[0:m, n % 2, 0:KVH]).then_inc(tok_out, 1)
                dve.memset(T["ab_t"][:], 0.0).then_inc(ab_clear, 1)
                dve.wait_ge(ab_clear, 1)
                dve.wait_ge(tok_out, len(tiles))
                dve.tensor_copy(T["ab_t"][:, 0:QT, :], kvt[:, 0:QT, A_OFF:KVG])
                dve.tensor_copy(T["ab_t"][0:NS, QT, :], kvt[0:NS, QT, A_OFF:KVG])

            @block.scalar
            def _(act):
                for n, (_, dst, at, fn, scale) in enumerate(dests):
                    for ft in range(2):
                        u = 2 * n + ft
                        act.wait_ge(feat_prod, u + 1)
                        act.activation(dst[:, at + ft, :].rearrange("p (b t) -> p b t", b=3), featP[u % 2][:, :, 0:TB],
                                       fn, scale=scale).then_inc(feat_out, 1)


def stage_compress(nc, T):
    with ExitStack() as ctx:
        sb = lambda n, s, d=F32: ctx.enter_context(nc.sbuf_tensor(n, s, d))
        sem = lambda n: ctx.enter_context(nc.semaphore(n))
        w1 = sb("cw1", [P, 2, RS, P])
        pe2 = sb("pe2", [P, 2, RS])
        w2 = sb("cw2", [P, 2, P])
        bias = sb("bias", [P, 2])
        xc = [sb(f"xc{i}", [P, NPAGE, 2, 16, 8]) for i in range(2)]
        hs = [sb(f"hs{i}", [P, 2, NCMP]) for i in range(2)]
        pages = sb("pages", [1, NB * NPAGE], I32)
        cmpT = sb("cmpT", [P, 2, SEQ])
        trP = ctx.enter_context(nc.psum_tensor("trP2", [P, 2, 512], F32))
        biasP = ctx.enter_context(nc.psum_tensor("biasP", [P, 512], F32))
        preP = ctx.enter_context(nc.psum_tensor("preP", [P, 2, 512], F32))
        kvP = ctx.enter_context(nc.psum_tensor("kvP", [P, 2, 512], F32))
        w_zero, ld_w, ld_pg = sem("w_zero"), sem("ld_cw"), sem("ld_pg")
        ld_x = [sem(f"ld_xc{i}") for i in range(2)]
        kv_t, kv_copied, bias_prod, bias_ready = sem("kv_t"), sem("kv_copied"), sem("bias_prod"), sem("bias_ready")
        pre_prod, hs_ready, cmp_prod, cmp_ready, st_kv = sem("pre_prod"), sem("hs_ready"), sem("cmp_prod"), sem("cmp_ready"), sem("st_kv")
        kvt, kvT, kcT, vc, ident = T["kvt"], T["kvT"], T["kcT"], T["vc"], T["ident"]
        pool = T["in"]["cmp_pool"]
        BLK = [0, 1, 2, 4]

        with nc.Block() as block:
            @block.sync
            def _(sp):
                sp.dma_start(pages[:], T["in"]["pages"]).then_inc(ld_pg, 16)
                sp.dma_start(pe2[:], T["in"]["cmp_pe"]).then_inc(ld_w, 16)
                sp.wait_ge(w_zero, 2)
                for g in range(2):
                    sp.dma_start(w1[g * HD:(g + 1) * HD, :, :, g * HD:(g + 1) * HD], T["in"]["cmp_w1"]).then_inc(ld_w, 16)
                    sp.dma_start(w2[g * HD:(g + 1) * HD, :, g * HD:(g + 1) * HD], T["in"]["cmp_w2"]).then_inc(ld_w, 16)
                sp.wait_ge(ld_pg, 16)

                def load_sequence(b, half):
                    for p in range(NPAGE):
                        page = sp.value_load(pages[0:1, bass.ds(b * NPAGE + p, 1)], min_val=0, max_val=NPOOL - 1)
                        sp.dma_start(xc[half][:, p], pool[bass.ds(page, 1)].rearrange("a p (k s n) -> (a p) k s n", k=2, s=16)).then_inc(ld_x[half], 16)

                for half in range(2):
                    load_sequence(half, half)
                with sp.Fori(1, NB // 2) as i:
                    for half in range(2):
                        sp.wait_ge(pre_prod, i * 2 + (half - 1))
                        load_sequence(i * 2 + half, half)

            @block.gpsimd
            def _(pool_e):
                pool_e.memset(w1[:], 0.0).then_inc(w_zero, 1)
                pool_e.memset(w2[:], 0.0).then_inc(w_zero, 1)
                o, sel = T["out"], lambda c: slice(c * 2 * P, (c + 1) * 2 * P)
                rows = lambda ap: ap.rearrange("a b t k g d -> (a b t) (k g d)")
                pool_e.dma_start(rows(o["cmp_p"]).rearrange("(n p) c -> p n c", p=P), kvt[:, 0:QT, sel(0)]).then_inc(st_kv, 16)
                pool_e.dma_start(rows(o["sel_p"]).rearrange("(n p) c -> p n c", p=P), kvt[:, 0:QT, sel(1)]).then_inc(st_kv, 16)
                pool_e.dma_start(rows(o["win_p"]).rearrange("(n p) c -> p n c", p=P), kvt[:, QT // 2:QT, sel(2)]).then_inc(st_kv, 16)
                pool_e.dma_start(rows(o["cmp_s"]), kvt[0:NS, QT, sel(0)]).then_inc(st_kv, 16)
                pool_e.dma_start(rows(o["sel_s"]), kvt[0:NS, QT, sel(1)]).then_inc(st_kv, 16)
                win = o["win_s"].rearrange("a b t k g d -> (a b) t (k g d)")
                for b in range(NB):
                    pool_e.dma_start(win[b, WIN - NT:WIN, :], kvt[b * NT:(b + 1) * NT, QT, sel(2)]).then_inc(st_kv, 16)
                pool_e.dma_start(win[:, 0:WIN - NT, :], T["in"]["cache_win"][:, NT:WIN, :]).then_inc(st_kv, 16)
                pool_e.wait_ge(st_kv, 16 * (6 + NB))

            @block.tensor
            def _(pe):
                for t in range(QT + 1):
                    m = P if t < QT else NS
                    if t >= 2:
                        pe.wait_ge(kv_copied, t - 1)
                    for n, c in list(enumerate(BLK))[0 if t < QT else 2:]:
                        mm = pe.transpose(trP[:, t % 2, n * P:n * P + m], kvt[0:m, t, c * P:(c + 1) * P], ident[0:m, 0:m])
                    mm.then_inc(kv_t, 1)
                pe.wait_ge(ld_w, 80)
                for kv in range(2):
                    for rs in range(RS):
                        mm = pe.matmul(biasP[:, kv:kv + 1], w1[:, kv, rs, :], pe2[:, kv, rs:rs + 1], start=(rs == 0), stop=(rs == RS - 1))
                mm.then_inc(bias_prod, 1)

                def conv(src, s):
                    for kv in range(2):
                        for r in range(2):
                            for t in range(16):
                                mm = pe.matmul(preP[:, s, kv * 128 + 1 - r:kv * 128 + 65 - r], w1[:, kv, r * 16 + t, :], src(kv, t),
                                               start=(r == 0 and t == 0), stop=(r == 1 and t == 15), skip_group_check=True)
                    return mm

                def up(s):
                    pe.matmul(kvP[:, s, 0:NCMP], w2[:, 0, :], hs[s][:, 0, :])
                    return pe.matmul(kvP[0:NCMP, s, 128:256], hs[s][:, 1, :], w2[:, 1, :])

                with pe.Fori(0, NB // 2) as i:
                    for half in range(2):
                        pe.wait_ge(ld_x[half], i * (16 * NPAGE) + 16 * NPAGE)
                        conv(lambda kv, t: xc[half][:, :, kv, t, :], half).then_inc(pre_prod, 1)
                    for half in range(2):
                        pe.wait_ge(hs_ready, i * 2 + half + 1)
                        up(half).then_inc(cmp_prod, 1)
                    pe.wait_ge(cmp_ready, i * 2 + 2)
                pe.wait_ge(kv_copied, QT + 1)
                conv(lambda kv, t: cmpT[:, kv, t:SEQ:16], 0).then_inc(pre_prod, 1)
                pe.wait_ge(hs_ready, NB + 1)
                up(0).then_inc(cmp_prod, 1)

            @block.scalar
            def _(act):
                def silus(s):
                    for kv in range(2):
                        ins = act.activation(hs[s][:, kv, :], preP[:, s, kv * 128 + 1:kv * 128 + 64], ACT.Silu, bias=bias[:, kv:kv + 1])
                    return ins
                act.wait_ge(bias_ready, 1)
                with act.Fori(0, NB // 2) as i:
                    for half in range(2):
                        act.wait_ge(pre_prod, i * 2 + half + 1)
                        silus(half).then_inc(hs_ready, 1)
                act.wait_ge(pre_prod, NB + 1)
                silus(0).then_inc(hs_ready, 1)

            @block.vector
            def _(dve):
                for t in range(QT + 1):
                    m = P if t < QT else NS
                    dve.wait_ge(kv_t, t + 1)
                    tr = trP[:, t % 2, :].rearrange("p (n t) -> p n t", n=4)
                    if t < QT:
                        dve.tensor_copy(cmpT[:, :, t * P:t * P + m], tr[:, 0:2, :])
                    dve.tensor_copy(kvT[:, :, t * P:t * P + m], tr[:, 2:4, 0:m]).then_inc(kv_copied, 1)
                dve.wait_ge(bias_prod, 1)
                dve.tensor_copy(bias[:], biasP[:, 0:2]).then_inc(bias_ready, 1)
                with dve.Fori(0, NB // 2) as i:
                    for half in range(2):
                        dve.wait_ge(cmp_prod, i * 2 + half + 1)
                        dve.tensor_copy(kcT[:, bass.ds(i * 2 + half, 1), 0:NCMP], kvP[:, half, 0:NCMP])
                        dve.tensor_copy(vc[:, bass.ds(i * 2 + half, 1), :], kvP[0:NCMP, half, 128:256]).then_inc(cmp_ready, 1)
                dve.wait_ge(cmp_prod, NB + 1)
                dve.tensor_copy(kcT[:, NB, 0:NCMP], kvP[:, 0, 0:NCMP])
                dve.tensor_copy(vc[:, NB, :], kvP[0:NCMP, 0, 128:256]).then_inc(cmp_ready, 1)


def stage_sample_attention(nc, T):
    NG, SG = 2, 4
    NK = PAGE * NPAGE
    VG = 18
    with ExitStack() as ctx:
        sb = lambda n, s, d=F32: ctx.enter_context(nc.sbuf_tensor(n, s, d))
        sem = lambda n: ctx.enter_context(nc.semaphore(n))
        qs = sb("qs", [P, NB, 2, NJ, NT])
        tab = sb("tab", [P, 1840])
        sel = sb("sel", [NS, 2, P])
        pages = sb("pages2", [1, NB * NPAGE], I32)
        kS = sb("kS", [P, SG, NPAGE, PAGE])
        vS = sb("vS", [P, SG, NPAGE, P])
        kW = sb("kW", [P, SG, WIN])
        vW = sb("vW", [P, SG, 4, P])
        sc = sb("sc", [P, 63 + 1056 + 544])
        pT = sb("pT", [P, 15, P])
        sm = sb("sm", [P, 64])
        gts = sb("gts", [NS, 24])
        g3 = sb("g3", [P, 3, H])
        imp_r = sb("imp_r", [P, 16])
        drop = sb("drop", [P, 3, 16])
        oz = sb("oz", [P, 2, HD])
        half_o = sb("half_o", [P, SG, NJ, NT])
        scoreP = ctx.enter_context(nc.psum_tensor("scoreP", [P, 4, 512], F32))
        ptP = ctx.enter_context(nc.psum_tensor("ptP", [P, 2, 512], F32))
        oP = ctx.enter_context(nc.psum_tensor("oP", [P, 512], F32))
        miscP = ctx.enter_context(nc.psum_tensor("miscP", [P, 512], F32))
        qs_zero, qs_ready, ld_t, ld_pg = sem("qs_zero"), sem("qs_ready"), sem("ld_tab"), sem("ld_pg2")
        ld_k, ld_v = sem("ld_k"), sem("ld_v")
        gate_sig, gate_row, cmp_s, sel_s = sem("gate_sig"), sem("gate_row"), sem("cmp_s"), sem("sel_s")
        v, e, pt_ready, pt_out, o_done, imp_p = sem("v"), sem("e"), sem("pt_ready"), sem("pt_out"), sem("o_done"), sem("imp_p")
        dve_step = sem("dve_step2")
        ident, kvt, kvT, kcT, vc, zaT = T["ident"], T["kvt"], T["kvT"], T["kcT"], T["vc"], T["zaT"]
        qTs = T["qT"]
        c_cmp, c_sel, c_win, c_new, c_map, c_agg, c_hm, c_io, c_m = 0, 63, 1087, 1599, 1663, 1679, 1807, 1815, 1831
        C, S0, S1, W0, W1 = 0, 63, 63 + 1024, 63 + 1056, 63 + 1056 + 512
        END = W1 + 32

        with nc.Block() as block:
            @block.sync
            def _(sp):
                sp.dma_start(tab[:], T["in"]["sample_tab"]).then_inc(ld_t, 16)
                sp.dma_start(sel[:], T["in"]["token_sel"]).then_inc(ld_t, 16)
                sp.dma_start(pages[:], T["in"]["pages"]).then_inc(ld_pg, 16)
                sp.wait_ge(ld_pg, 16)
                for G in range(NG):
                    if G:
                        sp.wait_ge(o_done, 1)
                    with sp.Fori(0, SG * NPAGE) as i:
                        page = sp.value_load(pages[0:1, bass.ds(i + G * SG * NPAGE, 1)], min_val=0, max_val=NPOOL - 1)
                        sp.dma_start(kS[:].rearrange("p b n t -> p (b n) t")[:, bass.ds(i, 1), :], T["in"]["sel_k"][bass.ds(page, 1)].rearrange("a p t -> p a t")).then_inc(ld_k, 16)
                        sp.dma_start(vS[:].rearrange("p b n t -> p (b n) t")[:, bass.ds(i, 1), :], T["in"]["sel_v"][bass.ds(page, 1)].rearrange("a p t -> p a t")).then_inc(ld_v, 16)
                    sp.dma_start(kW[:], T["in"]["win_k"][G].rearrange("p (b t) -> p b t", b=SG)).then_inc(ld_k, 16)
                    sp.dma_start(vW[:], T["in"]["win_v"][G].rearrange("p (b n c) -> p b n c", b=SG, n=4)).then_inc(ld_v, 16)
                sp.wait_ge(ld_t, 32)

            @block.gpsimd
            def _(po):
                po.memset(qs[:], 0.0).then_inc(qs_zero, 1)
                po.wait_ge(qs_zero, 1)
                for g in range(2):
                    r = slice(g * HD, (g + 1) * HD)
                    po.tensor_copy(qs[r, :, g].rearrange("p b j t -> p j b t"), qTs[r, :, SEQ:TOK].rearrange("p j (b t) -> p j b t", b=NB)).then_inc(qs_ready, 1)

            @block.tensor
            def _(pe):
                npt = 0
                pe.wait_ge(qs_ready, 2)
                pe.wait_ge(ld_t, 32)
                for G in range(NG):
                    lhs = lambda b: qs[:, G * SG + b].rearrange("p g j t -> p (g j t)")
                    lhs_all = qs[:, G * SG:(G + 1) * SG].rearrange("p b g j t -> p (b g j t)")
                    pe.wait_ge(gate_sig, 1)
                    pe.matmul(miscP[:, 0:24], sel[:, G, :], gts[:, :]).then_inc(gate_row, 1)
                    for b in range(SG):
                        pe.matmul(scoreP[32 * b:32 * b + 32, 0, 0:NCMP], lhs(b), kcT[:, G * SG + b, 0:NCMP])
                    pe.matmul(scoreP[:, 0, 64:96], lhs_all, kvT[:, 0, SEQ:TOK])
                    pe.matmul(scoreP[:, 0, 96:128], lhs_all, kvT[:, 1, SEQ:TOK]).then_inc(cmp_s, 1)
                    pe.wait_ge(ld_k, (G + 1) * 16 * (SG * NPAGE + 1))
                    for b in range(SG):
                        for n in range(2):
                            pe.matmul(scoreP[32 * b:32 * b + 32, 1 + n, :], lhs(b), kS[:, b, 4 * n:4 * n + 4, :].rearrange("p n t -> p (n t)"))
                        mm = pe.matmul(scoreP[32 * b:32 * b + 32, 3, :], lhs(b), kW[:, b, :])
                    mm.then_inc(sel_s, 1)
                    pe.wait_ge(v, VG * G + 3)
                    pe.transpose(ptP[0:NCMP, 0, 0:P], sc[:, C:C + NCMP], ident[:]).then_inc(pt_ready, 1)
                    pe.wait_ge(pt_out, 5 * G + 1)
                    for b in range(SG):
                        pe.matmul(oP[32 * b:32 * b + 32, 0:P], pT[0:NCMP, 0, 32 * b:32 * b + 32], vc[:, G * SG + b, :])
                    pe.matmul(miscP[:, 32:48], pT[0:NCMP, 0, :], tab[0:NCMP, c_map:c_map + 16]).then_inc(imp_p, 1)
                    pe.wait_ge(v, VG * G + 4)
                    pe.matmul(miscP[:, 64:80], tab[:, c_agg:c_agg + P], imp_r[:]).then_inc(imp_p, 1)
                    pe.wait_ge(e, 3 * G + 2)
                    for grp in range(2):
                        for n in range(4):
                            mm = pe.transpose(ptP[:, 1 - grp, n * P:(n + 1) * P], sc[:, S0 + (4 * grp + n) * P:S0 + (4 * grp + n + 1) * P], ident[:])
                        mm.then_inc(pt_ready, 1)
                    pe.wait_ge(pt_out, 5 * G + 2)
                    pe.wait_ge(e, 3 * G + 3)
                    for n in range(4):
                        mm = pe.transpose(ptP[:, 1, n * P:(n + 1) * P], sc[:, W0 + n * P:W0 + (n + 1) * P], ident[:])
                    mm.then_inc(pt_ready, 1)
                    pe.wait_ge(pt_out, 5 * G + 3)
                    pe.transpose(ptP[0:NS, 0, 0:P], sc[:, S1:S1 + NS], ident[:])
                    pe.transpose(ptP[0:NS, 0, P:2 * P], sc[:, W1:W1 + NS], ident[:]).then_inc(pt_ready, 1)
                    pe.wait_ge(pt_out, 5 * G + 5)
                    pe.wait_ge(ld_v, (G + 1) * 16 * (SG * NPAGE + 1))
                    for b in range(SG):
                        c = slice(32 * b, 32 * b + 32)
                        for n in range(8):
                            pe.matmul(oP[c, P:2 * P], pT[:, 1 + n, c], vS[:, b, n, :], start=(n == 0), stop=False, skip_group_check=True)
                        pe.matmul(oP[c, P:2 * P], pT[0:NS, 9, c], kvt[0:NS, QT, 3 * P:4 * P], start=False, stop=True, skip_group_check=True)
                        for n in range(4):
                            pe.matmul(oP[c, 2 * P:3 * P], pT[:, 10 + n, c], vW[:, b, n, :], start=(n == 0), stop=False, skip_group_check=True)
                        mm = pe.matmul(oP[c, 2 * P:3 * P], pT[0:NS, 14, c], kvt[0:NS, QT, 5 * P:6 * P], start=False, stop=True, skip_group_check=True)
                    mm.then_inc(o_done, 1)
                    pe.wait_ge(v, VG * G + 17)
                    pe.transpose(miscP[:, P:2 * P], oz[:].rearrange("p g d -> p (g d)"), ident[:]).then_inc(o_done, 1)
                    pe.wait_ge(v, VG * G + 18)

            @block.scalar
            def _(act):
                act.activation(gts[:], kvt[0:NS, QT, 6 * P:6 * P + 24], ACT.Sigmoid).then_inc(gate_sig, 1)
                for G in range(NG):
                    act.wait_ge(v, VG * G + 1)
                    act.activation(sc[:, C:C + NCMP], sc[:, C:C + NCMP], ACT.Exp, bias=sm[:, 0:1], accum_out=sm[:, 1:2]).then_inc(e, 1)
                    act.wait_ge(v, VG * G + 5)
                    act.activation(sc[:, S0:W0], sc[:, S0:W0], ACT.Exp, bias=sm[:, 2:3], accum_out=sm[:, 3:4]).then_inc(e, 1)
                    act.wait_ge(v, VG * G + 6)
                    act.activation(sc[:, W0:END], sc[:, W0:END], ACT.Exp, bias=sm[:, 4:5], accum_out=sm[:, 5:6]).then_inc(e, 1)
                    for k, (m, dst, src) in enumerate([
                            (P, pT[:, 1:5, :], ptP[:, 1, :].rearrange("p (n t) -> p n t", n=4)),
                            (P, pT[:, 5:9, :], ptP[:, 0, :].rearrange("p (n t) -> p n t", n=4)),
                            (P, pT[:, 10:14, :], ptP[:, 1, :].rearrange("p (n t) -> p n t", n=4)),
                            (NS, pT[0:NS, 9:15:5, :], ptP[0:NS, 0, 0:2 * P].rearrange("p (n t) -> p n t", n=2))]):
                        act.wait_ge(pt_ready, 5 * G + 2 + k)
                        act.activation(dst, src, ACT.Copy).then_inc(pt_out, 1)

            @block.vector
            def _(dve):
                linked = [0]
                def link(ins, wait=True):
                    ins.then_inc(dve_step, 1)
                    linked[0] += 1
                    if wait:
                        dve.wait_ge(dve_step, linked[0])
                dve.wait_ge(ld_t, 32)
                for G in range(NG):
                    n_v = [VG * G]
                    def done(ins):
                        ins.then_inc(v, 1)
                        n_v[0] += 1
                    def settle():
                        dve.wait_ge(v, n_v[0])
                    dve.wait_ge(cmp_s, G + 1)
                    dve.wait_ge(gate_row, G + 1)
                    link(dve.tensor_tensor(sc[:, C:C + NCMP], scoreP[:, 0, 0:NCMP], tab[:, c_cmp:c_cmp + NCMP], ALU.add))
                    done(dve.tensor_reduce(sm[:, 0:1], sc[:, C:C + NCMP], AX, ALU.max, negate=True))
                    link(dve.tensor_tensor(g3[:], miscP[:, 0:24].rearrange("p (h c) -> p c h", c=3), tab[:, c_hm:c_hm + H].unsqueeze(1).to_broadcast([P, 3, H]), ALU.mult))
                    link(dve.tensor_reduce(sm[:, 10:13], g3[:], AX, ALU.add))
                    dve.wait_ge(e, 3 * G + 1)
                    done(dve.reciprocal(sm[:, 6:7], sm[:, 1:2]))
                    settle()
                    link(dve.tensor_scalar(sc[:, C:C + NCMP], sc[:, C:C + NCMP], sm[:, 6:7], None, ALU.mult))
                    done(dve.scalar_tensor_tensor(sc[:, C:C + NCMP], sc[:, C:C + NCMP], TINY, sc[:, C:C + NCMP], ALU.is_ge, ALU.mult))
                    dve.wait_ge(pt_ready, 5 * G + 1)
                    dve.tensor_copy(pT[0:NCMP, 0, :], ptP[0:NCMP, 0, 0:P]).then_inc(pt_out, 1)
                    dve.wait_ge(imp_p, 2 * G + 1)
                    done(dve.tensor_copy(imp_r[:], miscP[:, 32:48]))
                    dve.wait_ge(imp_p, 2 * G + 2)
                    imp = miscP[:, 65:79]
                    link(dve.tensor_reduce(sm[:, 7:8], imp, AX, ALU.min))
                    link(dve.scalar_tensor_tensor(drop[:, 0, 0:14], imp, sm[:, 7:8], tab[:, c_io + 1:c_io + 15], ALU.is_equal, ALU.mult))
                    link(dve.tensor_reduce(sm[:, 8:9], drop[:, 0, 0:14], AX, ALU.max))
                    link(dve.tensor_scalar(drop[:, 1, :], tab[:, c_io:c_io + 16], sm[:, 8:9], NEG, ALU.is_equal, ALU.mult))
                    dve.wait_ge(sel_s, G + 1)
                    link(dve.tensor_tensor(sc[:, S0:S1].rearrange("p (b n) -> p b n", b=2), scoreP[:, 1:3, :], tab[:, c_sel:c_sel + NK].rearrange("p (b n) -> p b n", b=2), ALU.add), wait=False)
                    link(dve.tensor_tensor(sc[:, S1:W0], scoreP[:, 0, 64:96], tab[:, c_new + 32 * G:c_new + 32 * G + 32], ALU.add))
                    s3 = sc[:, S0:S1].rearrange("p (b n) -> p b n", b=16)
                    link(dve.tensor_tensor(s3, s3, drop[:, 1, :].unsqueeze(2).to_broadcast([P, 16, 64]), ALU.add))
                    done(dve.tensor_reduce(sm[:, 2:3], sc[:, S0:W0], AX, ALU.max, negate=True))
                    link(dve.tensor_tensor(sc[:, W0:W1], scoreP[:, 3, :], tab[:, c_win:c_win + WIN], ALU.add), wait=False)
                    link(dve.tensor_tensor(sc[:, W1:END], scoreP[:, 0, 96:128], tab[:, c_new + 32 * G:c_new + 32 * G + 32], ALU.add))
                    done(dve.tensor_reduce(sm[:, 4:5], sc[:, W0:END], AX, ALU.max, negate=True))
                    dve.wait_ge(e, 3 * G + 3)
                    done(dve.reciprocal(sm[:, 13:14], sm[:, 3:4]))
                    done(dve.reciprocal(sm[:, 14:15], sm[:, 5:6]))
                    settle()
                    done(dve.tensor_tensor(sm[:, 11:13], sm[:, 11:13], sm[:, 13:15], ALU.mult))
                    settle()
                    done(dve.tensor_scalar(sm[:, 16:19], sm[:, 10:13], tab[:, c_m:c_m + 1], None, ALU.mult))
                    done(dve.tensor_scalar(sm[:, 19:22], sm[:, 10:13], tab[:, c_m + 1:c_m + 2], None, ALU.mult))
                    settle()
                    dve.wait_ge(o_done, 2 * G + 1)
                    for c in range(3):
                        for g in range(2):
                            src, k = oP[:, c * P + g * HD:c * P + (g + 1) * HD], sm[:, 16 + 3 * g + c:17 + 3 * g + c]
                            if c == 0:
                                done(dve.tensor_scalar(oz[:, g, :], src, k, None, ALU.mult))
                            else:
                                done(dve.scalar_tensor_tensor(oz[:, g, :], src, k, oz[:, g, :], ALU.mult, ALU.add))
                        if c < 2:
                            settle()
                    dve.wait_ge(o_done, 2 * G + 2)
                    ot = miscP[:, P:2 * P].rearrange("p (b g j t) -> p g b j t", b=SG, g=2, j=NJ)
                    link(dve.tensor_copy(half_o[:], ot[:, 0]))
                    link(dve.tensor_tensor(half_o[:], half_o[:], ot[:, 1], ALU.add))
                    zs = zaT[:, :, SEQ + G * SG * NT:SEQ + (G + 1) * SG * NT].rearrange("p j (b t) -> p b j t", b=SG)
                    done(dve.tensor_tensor(zs, zs, half_o[:], ALU.mult))
                    assert n_v[0] == VG * (G + 1)
                    settle()


def stage_prompt_attention(nc, T):
    NPAIR = 2
    UN = 4 * NPAIR
    W_MAX = WIN + P

    def width(i):
        return min((i + 1) * P, W_MAX)

    def slots(i, kind):
        if kind == 0:
            return [(0, n * P, P, n) for n in range(i + 1)]
        k0 = (i + 1) - width(i) // P
        return [(1, n * P, P, k0 + n) for n in range(width(i) // P)] + [(2, W_MAX, NCMP, None)]

    def groups(i, kind):
        s = slots(i, kind)
        cut = 3 if len(s) == 5 and kind else 4
        return [x for x in (s[:cut], s[cut:8], s[8:]) if x]

    def each_step(eng, i, body):
        if i == 0:
            for s in range(2):
                body(s)
        else:
            with eng.Fori(0, 2) as s:
                body(s)

    def wait(eng, sem, count):
        if not isinstance(count, int) or count > 0:
            eng.wait_ge(sem, count)

    unit_kind = [0, 0, 1, 1] * NPAIR
    unit_g = [0, 1, 0, 1] * NPAIR
    with ExitStack() as ctx:
        sb = lambda n, s, d=F32: ctx.enter_context(nc.sbuf_tensor(n, s, d))
        sem = lambda n: ctx.enter_context(nc.semaphore(n))
        dist = sb("dist", [P, SEQ])
        dist_w = sb("dist_w", [P, P])
        dist_c = sb("dist_c", [P, QT, 64])
        slope = sb("slope", [P, H])
        gates = sb("gates", [P, QT, NJ, 2, 3])
        qb = [sb(f"qb{i}", [P, P]) for i in range(NPAIR)]
        ss = [sb(f"ss{i}", [P, SEQ]) for i in range(4)]
        pT = [sb(f"ppT{i}", [P, 4, P]) for i in range(4)]
        nm = sb("nm", [P, 4, 2])
        sums = [sb(f"sums{i}", [P, 6]) for i in range(NPAIR)]
        coef = sb("coef", [P, 6])
        tmp = sb("otmp", [P, 6, HD])
        ot = sb("ot", [P, NJ, P])
        sP = [ctx.enter_context(nc.psum_tensor(f"sP{i}", [P, 2, 512], F32)) for i in range(2)]
        tP = ctx.enter_context(nc.psum_tensor("tP", [P, 2, 512], F32))
        oP = ctx.enter_context(nc.psum_tensor("poP", [P, 2, 512], F32))
        ld_t, gate_ready, q_ready = sem("ld_d"), sem("gate_ready"), sem("q_ready")
        score_prod, score_read, max_ready, p_ready = sem("score_prod"), sem("score_read"), sem("max_ready"), sem("p_ready")
        pt_ready, pt_out, pv_done = sem("ppt_ready"), sem("ppt_out"), sem("pv_done")
        o_read, o_ready, o_turned, z_done, dve_step = sem("o_read"), sem("o_ready"), sem("o_turned"), sem("z_done"), sem("dve_step3")
        kvt, kvT, kcT, vc, qT, zaT, ident = T["kvt"], T["kvT"], T["kcT"], T["vc"], T["qT"], T["zaT"], T["ident"]
        NPT = [sum(len(groups(i, k)) for k in unit_kind) for i in range(QT)]
        G0 = [2 * sum(NPT[:i]) for i in range(QT)]
        U0 = [2 * UN * i for i in range(QT)]

        with nc.Block() as block:
            @block.sync
            def _(sp):
                sp.dma_start(dist[:], T["in"]["dist"]).then_inc(ld_t, 16)
                sp.dma_start(dist_w[:], T["in"]["dist_w"]).then_inc(ld_t, 16)
                sp.dma_start(dist_c[:], T["in"]["dist_c"]).then_inc(ld_t, 16)
                sp.dma_start(slope[:], T["in"]["slope"]).then_inc(ld_t, 16)
                sp.wait_ge(ld_t, 64)

            @block.gpsimd
            def _(po):
                for i in range(QT):
                    def body(s, i=i):
                        for j in range(NPAIR):
                            wait(po, score_prod, s * UN + (U0[i] - UN + 4 * j + 4))
                            po.tensor_copy(qb[j][:], qT[:, bass.ds(s * NPAIR + j, 1), i * P:(i + 1) * P]).then_inc(q_ready, 1)
                    each_step(po, i, body)

            @block.tensor
            def _(pe):
                for i in range(QT):
                    def body(s, i=i):
                        def at(base):
                            return s * UN + base

                        def scores(u):
                            g, j, dst = unit_g[u], u // 4, sP[u % 2]
                            r = slice(g * HD, (g + 1) * HD)
                            if u % 4 == 0:
                                pe.wait_ge(q_ready, s * NPAIR + 2 * NPAIR * i + j + 1)
                            wait(pe, score_read, at(U0[i] + u - 1))
                            n = (i + 1) * P if unit_kind[u] == 0 else width(i)
                            k0 = (i + 1) * P - n
                            for c in range(0, n, 512):
                                m = min(512, n - c)
                                mm = pe.matmul(dst[:, c // 512, 0:m], qb[j][r, :], kvT[r, unit_kind[u], k0 + c:k0 + c + m])
                            if unit_kind[u]:
                                mm = pe.matmul(dst[:, 1, P:P + NCMP], qb[j][r, :], kcT[r, NB, 0:NCMP])
                            mm.then_inc(score_prod, 1)

                        flat = [(u, n, grp) for u in range(UN) for n, grp in enumerate(groups(i, unit_kind[u]))]

                        def turn(k):
                            u, n, grp = flat[k]
                            if n == 0:
                                pe.wait_ge(p_ready, at(U0[i] + u + 1))
                            wait(pe, pt_out, s * NPT[i] + (G0[i] + k - 1))
                            for m, (_, c, keys, _) in enumerate(grp):
                                mm = pe.transpose(tP[0:keys, k % 2, m * P:(m + 1) * P], ss[u % 4][:, c:c + keys], ident[:])
                            mm.then_inc(pt_ready, 1)

                        def values(k):
                            u, n, grp = flat[k]
                            g, j = unit_g[u], u // 4
                            pe.wait_ge(pt_out, s * NPT[i] + (G0[i] + k + 1))
                            if u % 4 == 0 and n == 0:
                                wait(pe, o_read, s * NPAIR + (2 * NPAIR * i - NPAIR + j + 1))
                                if j == 0:
                                    wait(pe, z_done, i)
                            for m, (br, c, keys, tile) in enumerate(grp):
                                v = vc[:, NB, g * HD:(g + 1) * HD] if br == 2 else kvt[:, tile, (3 + 2 * br) * P + g * HD:(3 + 2 * br) * P + (g + 1) * HD]
                                first = br == 2 or c == 0
                                last = br == 2 or c == ((i + 1) * P if br == 0 else width(i)) - P
                                mm = pe.matmul(oP[:, j, (g * 3 + br) * HD:(g * 3 + br + 1) * HD], pT[k % 4][0:keys, m, :], v, start=first, stop=last)
                            mm.then_inc(pv_done, 1)

                        scores(0)
                        scores(1)
                        for k, (u, n, grp) in enumerate(flat):
                            turn(k)
                            if k:
                                values(k - 1)
                            if n == len(groups(i, unit_kind[u])) - 1 and u + 2 < UN:
                                scores(u + 2)
                        values(len(flat) - 1)
                    each_step(pe, i, body)
                    pe.wait_ge(o_ready, 4 * (i + 1))
                    for j in range(NJ):
                        mm = pe.transpose(oP[:, 0, j * P:(j + 1) * P], ot[:, j, :], ident[:])
                    mm.then_inc(o_turned, 1)
                pe.wait_ge(z_done, QT)

            @block.scalar
            def _(act):
                for i in range(QT):
                    src = kvt[:, i, 6 * P:6 * P + 24].rearrange("p (g j c) -> p g j c", g=2, j=NJ)
                    dst = gates[:, i].rearrange("p j g c -> p g j c")
                    act.activation(dst[:, :, :, 2], src[:, :, :, 0], ACT.Sigmoid)
                    act.activation(dst[:, :, :, 0:2], src[:, :, :, 1:3], ACT.Sigmoid).then_inc(gate_ready, 1)
                for i in range(QT):
                    def body(s, i=i):
                        def exps(u):
                            g, j = unit_g[u], u // 4
                            act.wait_ge(max_ready, s * UN + (U0[i] + u + 1))
                            n = (i + 1) * P if unit_kind[u] == 0 else width(i)
                            b = unit_kind[u]
                            x = act.activation(ss[u % 4][:, 0:n], ss[u % 4][:, 0:n], ACT.Exp, bias=nm[:, u % 4, 0:1], accum_out=sums[j][:, g * 3 + b:g * 3 + b + 1])
                            if b:
                                c = slice(W_MAX, W_MAX + NCMP)
                                x = act.activation(ss[u % 4][:, c], ss[u % 4][:, c], ACT.Exp, bias=nm[:, u % 4, 1:2], accum_out=sums[j][:, g * 3 + 2:g * 3 + 3])
                            x.then_inc(p_ready, 1)

                        exps(0)
                        k = 0
                        for u in range(UN):
                            if u + 1 < UN:
                                exps(u + 1)
                            for grp in groups(i, unit_kind[u]):
                                act.wait_ge(pt_ready, s * NPT[i] + (G0[i] + k + 1))
                                wait(act, pv_done, s * NPT[i] + (G0[i] + k - 3))
                                full = [x for x in grp if x[0] != 2]
                                if full:
                                    x = act.activation(pT[k % 4][:, 0:len(full), :], tP[:, k % 2, 0:len(full) * P].rearrange("p (n t) -> p n t", t=P), ACT.Copy)
                                if len(full) < len(grp):
                                    m = len(full)
                                    x = act.activation(pT[k % 4][0:NCMP, m, :], tP[0:NCMP, k % 2, m * P:(m + 1) * P], ACT.Copy)
                                x.then_inc(pt_out, 1)
                                k += 1
                    each_step(act, i, body)

            @block.vector
            def _(dve):
                LN = UN // 2 + 3 * NPAIR
                ends = lambda i: [sum(len(groups(i, unit_kind[u])) for u in range(n + 1)) for n in range(UN)]
                dve.wait_ge(ld_t, 64)
                dve.wait_ge(gate_ready, QT)
                for i in range(QT):
                    def body(s, i=i):
                        linked = [0]

                        def link(ins, wait=True):
                            linked[0] += 1
                            ins.then_inc(dve_step, 1)
                            if wait:
                                dve.wait_ge(dve_step, s * LN + (2 * LN * i + linked[0]))

                        def biased(u):
                            g, j, src, dst = unit_g[u], u // 4, sP[u % 2], ss[u % 4]
                            U = U0[i] + u
                            dve.wait_ge(score_prod, s * UN + (U + 1))
                            if u >= 4:
                                wait(dve, pt_ready, s * NPT[i] + (G0[i] + ends(i)[u - 4]))
                            elif i == 0:
                                wait(dve, pt_ready, s * ends(i)[u + 4])
                            else:
                                gone = G0[i] - NPT[i - 1] + ends(i - 1)[u + 4]
                                dve.wait_ge(pt_ready, s * (G0[i] + ends(i)[u + 4] - gone) + gone)
                            k = slope[:, bass.ds(s * (2 * NPAIR) + (2 * j + g), 1)]
                            n = (i + 1) * P if unit_kind[u] == 0 else width(i)
                            flat = src[:].rearrange("p a b -> p (a b)")
                            first = P if unit_kind[u] and i >= 4 else 0
                            if first:
                                dve.scalar_tensor_tensor(dst[:, 0:P], dist_w[:], k, flat[:, 0:P], ALU.mult, ALU.add)
                            if unit_kind[u]:
                                dve.scalar_tensor_tensor(dst[:, W_MAX:W_MAX + NCMP], dist_c[:, i, 0:NCMP], k, flat[:, W_MAX:W_MAX + NCMP], ALU.mult, ALU.add)
                            dve.scalar_tensor_tensor(dst[:, first:n], dist[:, SEQ - n + first:SEQ], k, flat[:, first:n], ALU.mult, ALU.add).then_inc(score_read, 1)
                            dve.wait_ge(score_read, s * UN + (U + 1))
                            if unit_kind[u]:
                                link(dve.tensor_reduce(nm[:, u % 4, 1:2], dst[:, W_MAX:W_MAX + NCMP], AX, ALU.max, negate=True))
                                dve.tensor_scalar(nm[:, u % 4, 1:2], nm[:, u % 4, 1:2], GUARD, None, ALU.min)
                            dve.tensor_reduce(nm[:, u % 4, 0:1], dst[:, 0:n], AX, ALU.max, negate=True).then_inc(max_ready, 1)

                        def combine(j):
                            last = sum(len(groups(i, unit_kind[u])) for u in range(4 * j + 4))
                            dve.wait_ge(pv_done, s * NPT[i] + (G0[i] + last))
                            link(dve.tensor_scalar(coef[:], sums[j][:], 1e-30, None, ALU.max))
                            link(dve.reciprocal(coef[:], coef[:]))
                            link(dve.tensor_tensor(coef[:], coef[:], gates[:, i].rearrange("p j g c -> p j (g c)")[:, bass.ds(s * NPAIR + j, 1), :], ALU.mult))
                            dve.tensor_tensor(tmp[:], oP[:, j, 0:6 * HD].rearrange("p (c d) -> p c d", d=HD), coef[:].unsqueeze(2).to_broadcast([P, 6, HD]), ALU.mult).then_inc(o_read, 1)
                            dve.wait_ge(o_read, s * NPAIR + (2 * NPAIR * i + j + 1))
                            dve.tensor_reduce(ot[:, bass.ds(s * NPAIR + j, 1), :].rearrange("p a (g d) -> p (a g) d", g=2), tmp[:].rearrange("p (g b) d -> p g d b", g=2), AX, ALU.add).then_inc(o_ready, 1)

                        for u in range(UN):
                            biased(u)
                            if u == 5:
                                combine(0)
                        combine(1)
                        assert linked[0] == LN
                    each_step(dve, i, body)
                    dve.wait_ge(o_turned, i + 1)
                    z = zaT[:, :, i * P:(i + 1) * P]
                    dve.tensor_tensor(z, z, oP[:, 0, :].rearrange("p (j t) -> p j t", j=NJ), ALU.mult).then_inc(z_done, 1)


def stage_gdn_project(nc, T):
    with ExitStack() as ctx:
        sb = lambda n, s, d=F32: ctx.enter_context(nc.sbuf_tensor(n, s, d))
        sem = lambda n: ctx.enter_context(nc.semaphore(n))
        w = [sb(f"gw{i}", [P, KT, 256]) for i in range(2)]
        raw = [sb(f"raw{i}", [P, CW]) for i in range(2)]
        st = sb("cst", [P, 12, NB, 3])
        cwt = sb("cwt", [P, 12, 5])
        tail = sb("ctail", [P, 12, 3 + 3 * NB])
        fP = [ctx.enter_context(nc.psum_tensor(f"gfP{i}", [P, 3, 512], F32)) for i in range(2)]
        ld_w = [sem(f"gld_w{i}") for i in range(2)]
        ld_c, prod, raw_ready, st_ready = sem("gld_c"), sem("gprod"), sem("raw_ready"), sem("gst_ready")
        taps, conv_ready, tail_ready, st_out = sem("taps"), sem("conv_ready"), sem("tail_ready"), sem("gst_out")
        hT, uT = T["hT"], T["uT"]
        NF = 12
        samples = lambda r: r[:, SEQ + 3:CW].rearrange("p (b t) -> p b t", b=NB)

        with nc.Block() as block:
            @block.sync
            def _(sp):
                sp.dma_start(st[:], T["in"]["conv_state"]).then_inc(ld_c, 16)
                sp.dma_start(cwt[:], T["in"]["conv_w"]).then_inc(ld_c, 16)
                for n in range(NF // 2):
                    if n >= 2:
                        sp.wait_ge(prod, 2 * (n - 1))
                    sp.dma_start(w[n % 2][:], T["in"]["w_feat"][4 + n].rearrange("p (k n) -> p k n", k=KT)).then_inc(ld_w[n % 2], 16)
                sp.wait_ge(tail_ready, NF)
                sp.dma_start(T["out"]["conv_p"], tail[:, :, 0:3]).then_inc(st_out, 16)
                sp.dma_start(T["out"]["conv_s"], tail[:, :, 3:].rearrange("p f (b t) -> p f b t", b=NB)).then_inc(st_out, 16)
                sp.wait_ge(st_out, 32)

            @block.tensor
            def _(pe):
                for f in range(NF):
                    if f % 2 == 0:
                        pe.wait_ge(ld_w[f // 2 % 2], 16 * (f // 4 + 1))
                    if f >= 2:
                        pe.wait_ge(raw_ready, f - 1)
                    product_features(pe, fP[f % 2], w[f // 2 % 2], hT, f % 2).then_inc(prod, 1)

            @block.gpsimd
            def _(po):
                for r in raw:
                    po.memset(r[:, 0:3], 0.0)
                po.wait_ge(ld_c, 32)
                for f in range(NF):
                    if f >= 2:
                        po.wait_ge(conv_ready, f - 1)
                    po.tensor_copy(samples(raw[f % 2])[:, :, 0:3], st[:, f]).then_inc(st_ready, 1)
                    po.wait_ge(raw_ready, f + 1)
                    po.tensor_copy(tail[:, f, 0:3], raw[f % 2][:, SEQ:SEQ + 3])
                    po.tensor_copy(tail[:, f, 3:].rearrange("p (b t) -> p b t", b=NB), samples(raw[f % 2])[:, :, 4:7]).then_inc(tail_ready, 1)

            @block.scalar
            def _(act):
                def silu(f):
                    act.wait_ge(conv_ready, f + 1)
                    act.activation(uT[:, f, :], uT[:, f, :], ACT.Silu)
                for f in range(NF):
                    act.wait_ge(prod, f + 1)
                    if f >= 2:
                        act.wait_ge(conv_ready, f - 1)
                        act.wait_ge(tail_ready, f - 1)
                    r, p = raw[f % 2], fP[f % 2]
                    act.activation(r[:, 3:3 + 2 * TB].rearrange("p (b t) -> p b t", b=2), p[:, 0:2, 0:TB], ACT.Copy)
                    act.activation(r[:, 3 + 2 * TB:3 + SEQ], p[:, 2, 0:SEQ - 2 * TB], ACT.Copy)
                    act.activation(samples(r)[:, :, 3:7], p[:, 2, SEQ - 2 * TB:TB].rearrange("p (b t) -> p b t", b=NB), ACT.Copy).then_inc(raw_ready, 1)
                    if f:
                        silu(f - 1)
                silu(NF - 1)

            @block.vector
            def _(dve):
                dve.wait_ge(ld_c, 32)
                for f in range(NF):
                    dve.wait_ge(raw_ready, f + 1)
                    dve.wait_ge(st_ready, f + 1)
                    r, o = raw[f % 2], uT[:, f, :]
                    so, sr = o[:, SEQ:TOK].rearrange("p (b t) -> p b t", b=NB), samples(r)
                    for i in range(4):
                        if i == 0:
                            dve.tensor_scalar(o[:, 0:SEQ], r[:, 0:SEQ], cwt[:, f, 0:1], cwt[:, f, 4:5], ALU.mult, ALU.add)
                            x = dve.tensor_scalar(so, sr[:, :, 0:4], cwt[:, f, 0:1], cwt[:, f, 4:5], ALU.mult, ALU.add)
                        else:
                            k = cwt[:, f, i:i + 1]
                            dve.scalar_tensor_tensor(o[:, 0:SEQ], r[:, i:SEQ + i], k, o[:, 0:SEQ], ALU.mult, ALU.add)
                            x = dve.scalar_tensor_tensor(so, sr[:, :, i:i + 4], k, so, ALU.mult, ALU.add)
                        if i < 3:
                            x.then_inc(taps, 1)
                            dve.wait_ge(taps, 3 * f + i + 1)
                    x.then_inc(conv_ready, 1)


def stage_gdn_tokens(nc, T):
    with ExitStack() as ctx:
        sb = lambda n, s, d=F32: ctx.enter_context(nc.sbuf_tensor(n, s, d))
        sem = lambda n: ctx.enter_context(nc.semaphore(n))
        NTI = QT + 1
        sq = [sb(f"gsq{i}", [P, 2, 512]) for i in range(2)]
        ss = sb("gss", [P, NTI, 16])
        ab = sb("gab", [P, 2, H])
        ga = sb("ga", [P, 3, NTI, H])
        qP = [ctx.enter_context(nc.psum_tensor(f"gqP{i}", [P, 3, 512], F32)) for i in range(2)]
        ld, turned, copied, sq_ready, ss_ready, rt_ready = sem("gld"), sem("gturned"), sem("gcopied"), sem("gsq_ready"), sem("gss_ready"), sem("grt_ready")
        e, step, clear = sem("ge"), sem("gstep"), sem("gclear")
        uT, ident, qkv, ab_t = T["uT"], T["ident"], T["qkv"], T["ab_t"]
        rows = lambda t: P if t < QT else NS

        with nc.Block() as block:
            @block.sync
            def _(sp):
                sp.dma_start(ab[:], T["in"]["gdn_ab"]).then_inc(ld, 16)
                sp.wait_ge(ld, 16)

            @block.tensor
            def _(pe):
                for t in range(NTI):
                    m = rows(t)
                    if t >= 2:
                        pe.wait_ge(copied, t - 1)
                    for f in range(12):
                        mm = pe.transpose(qP[t % 2][0:m, f // 4, f % 4 * P:(f % 4 + 1) * P], uT[:, f, t * P:t * P + m], ident[:])
                    mm.then_inc(turned, 1)

            @block.scalar
            def _(act):
                for t in range(NTI):
                    m = rows(t)
                    act.wait_ge(copied, t + 1)
                    if t >= 2:
                        act.wait_ge(ss_ready, t - 1)
                    act.activation(sq[t % 2][0:m], qkv[0:m, t, 0:2], ACT.Square).then_inc(sq_ready, 1)
                act.wait_ge(step, 2)
                act.activation(ss[:], ss[:], ACT.Sqrt).then_inc(rt_ready, 1)
                act.wait_ge(ld, 16)
                act.activation(ab_t[:, :, H:2 * H], ab_t[:, :, H:2 * H], ACT.Sigmoid).then_inc(e, 1)
                act.activation(ab[:, 1, :], ab[:, 1, :], ACT.Exp).then_inc(e, 1)
                act.wait_ge(step, 3)
                act.activation(ga[:, 1], ga[:, 0], ACT.Abs).then_inc(e, 1)
                act.wait_ge(e, 3)
                act.activation(ga[:, 1], ga[:, 1], ACT.Exp, scale=-1.0).then_inc(e, 1)
                act.wait_ge(step, 4)
                act.activation(ga[:, 1], ga[:, 1], ACT.Ln).then_inc(e, 1)

            @block.vector
            def _(dve):
                dve.memset(ss[:], 1.0).then_inc(clear, 1)
                dve.wait_ge(clear, 1)
                for t in range(NTI):
                    m = rows(t)
                    dve.wait_ge(turned, t + 1)
                    dve.tensor_copy(qkv[0:m, t], qP[t % 2][0:m]).then_inc(copied, 1)
                    dve.wait_ge(sq_ready, t + 1)
                    dve.tensor_reduce(ss[0:m, t, :], sq[t % 2][0:m].rearrange("p a (h d) -> p (a h) d", d=HD), AX, ALU.add).then_inc(ss_ready, 1)
                dve.wait_ge(ss_ready, NTI)
                dve.tensor_scalar(ss[:], ss[:], EPS, None, ALU.add).then_inc(step, 1)
                dve.wait_ge(step, 1)
                dve.reciprocal(ss[:], ss[:]).then_inc(step, 1)
                dve.wait_ge(ld, 16)
                dve.tensor_tensor(ga[:, 0], ab_t[:, :, 0:H], ab[:, 0, :].unsqueeze(1).to_broadcast([P, NTI, H]), ALU.add).then_inc(step, 1)
                dve.wait_ge(e, 4)
                dve.tensor_scalar(ga[:, 1], ga[:, 1], 1.0, None, ALU.add).then_inc(step, 1)
                dve.tensor_scalar(ga[:, 2], ga[:, 0], 0.0, None, ALU.max).then_inc(step, 1)
                dve.wait_ge(e, 5)
                dve.wait_ge(step, 5)
                dve.tensor_tensor(ga[:, 2], ga[:, 2], ga[:, 1], ALU.add).then_inc(step, 1)
                dve.wait_ge(step, 6)
                dve.scalar_tensor_tensor(ab_t[:, :, 0:H], ga[:, 2], -1.0, ab[:, 1, :].unsqueeze(1).to_broadcast([P, NTI, H]), ALU.mult, ALU.mult)
                dve.wait_ge(rt_ready, 1)
                dve.tensor_scalar(ss[:, :, 0:H], ss[:, :, 0:H], HD ** -0.5, None, ALU.mult).then_inc(step, 1)
                dve.wait_ge(step, 7)
                for t in range(NTI):
                    m = rows(t)
                    x = qkv[0:m, t, 0:2].rearrange("p a (h d) -> p (a h) d", d=HD)
                    dve.tensor_tensor(x, x, ss[0:m, t].unsqueeze(2).to_broadcast([m, 16, HD]), ALU.mult)


def stage_gdn_scan(nc, T):
    with ExitStack() as ctx:
        sb = lambda n, s, d=F32: ctx.enter_context(nc.sbuf_tensor(n, s, d))
        sem = lambda n: ctx.enter_context(nc.semaphore(n))
        ps = lambda n, b: ctx.enter_context(nc.psum_tensor(n, [P, b, 512], F32))
        NTI = QT + 1
        tri = sb("tri", [P, 2, P])
        tot = sb("tot", [NS, P])
        seq = sb("seq", [NS, NB])
        msk = sb("msk", [P, 2, P])
        lvl = sb("lvl", [P, 7, P])
        src = sb("src", [P, 2, 512])
        ags = sb("ags", [P, 16])
        gst = sb("gst", [P, 24])
        gex = sb("gex", [P, 4, H])
        dec = sb("dec", [P, H, P])
        kb = sb("kb", [P, 4, 512])
        vb = sb("vb", [P, 512])
        kz = sb("kz", [P, H, P])
        kq = sb("kq", [P, NJ, 2, P])
        ke = sb("ke", [P, 2, NJ, P])
        lt = sb("lt", [P, H, P])
        at = sb("at", [P, H, P])
        x = sb("x", [P, H, P])
        xt = sb("xt", [P, H, P])
        yy = sb("yy", [P, H, P])
        vz = sb("vz", [P, NJ * 256 + P])
        r = sb("r", [P, 512])
        S = sb("S", [P, NJ, P])
        egl = sb("egl", [P, NJ])
        SS = sb("SS", [P, NJ, NB, P])
        eglS = sb("eglS", [P, NJ, NB])
        A, Bk = ps("psA", 4), ps("psB", 4)
        ld, clear, st_out = sem("sld"), sem("sclear"), sem("sst_out")
        g_prod, g_read, exp_ready, dec_in, dec_ready, row_prod = sem("g_prod"), sem("g_read"), sem("exp_ready"), sem("dec_in"), sem("dec_ready"), sem("row_prod")
        scaled, t_done, t_out, kk_done, lt_ready = sem("scaled"), sem("t_done"), sem("t_out"), sem("kk_done"), sem("lt_ready")
        mm_done, xt_out, dv_out, chain_mm, chain_ev, tile_done, step = (sem(n) for n in ("mm_done", "xt_out", "dv_out", "chain_mm", "chain_ev", "tile_done", "sstep"))
        src_ready, og_out, state_done = sem("src_ready"), sem("og_out"), sem("state_done")
        qkv, ab_t, ident, ones, og = T["qkv"], T["ab_t"], T["ident"], T["ones"], T["og"]
        pair_rows = [slice(0, HD), slice(HD, P)]
        heads3 = lambda ap: ap.rearrange("p (h d) -> p h d", d=HD)

        NL = 6
        LNK = 12

        def levels_of(smp):
            return 1 if smp else NL

        def tiles(eng, body):
            body(0, 0, P)
            with eng.Fori(1, QT) as t:
                body(t, 0, P)
            body(QT, 1, NS)

        with nc.Block() as block:
            @block.sync
            def _(sp):
                for dst, name in ((tri, "tri"), (tot, "tot"), (seq, "seq"), (msk, "msk"), (lvl, "lvl")):
                    sp.dma_start(dst[:], T["in"][name]).then_inc(ld, 16)
                sp.wait_ge(clear, 4)
                for h2 in range(2):
                    for j in range(NJ):
                        sp.dma_start(SS[pair_rows[h2], j, :, h2 * HD:(h2 + 1) * HD], T["in"]["gdn_state"][pair_rows[h2], j]).then_inc(ld, 16)
                sp.wait_ge(tile_done, NTI)
                for h2 in range(2):
                    sp.dma_start(T["out"]["gdn_p"][pair_rows[h2]], S[pair_rows[h2], :, h2 * HD:(h2 + 1) * HD]).then_inc(st_out, 16)
                    for j in range(NJ):
                        sp.dma_start(T["out"]["gdn_s"][pair_rows[h2], j], SS[pair_rows[h2], j, :, h2 * HD:(h2 + 1) * HD]).then_inc(st_out, 16)
                sp.wait_ge(st_out, 16 * (2 + 2 * NJ))

            @block.gpsimd
            def _(po):
                for t_ in (SS, S, kz, vz):
                    po.memset(t_[:], 0.0).then_inc(clear, 1)
                def body(t, smp, m):
                    bc = lambda ap: ap.unsqueeze(2).to_broadcast([m, H, HD])
                    if not (isinstance(t, int) and t == 0):
                        po.wait_ge(tile_done, t)
                    at_t = bass.ds(t, 1)
                    po.tensor_copy(ags[0:m], ab_t[0:m, at_t, :]).then_inc(src_ready, 1)
                    po.tensor_copy(src[0:m], qkv[0:m, at_t, 0:2, :]).then_inc(src_ready, 1)
                    po.wait_ge(exp_ready, t + 1)
                    po.wait_ge(src_ready, t * 2 + 2)
                    q, k = (heads3(src[0:m, c]) for c in range(2))
                    v = qkv[0:m, at_t, 2, :].rearrange("p a (h d) -> p (a h) d", d=HD)
                    po.tensor_tensor(heads3(kb[0:m, 0]), k, bc(ags[0:m, H:2 * H]), ALU.mult).then_inc(scaled, 1)
                    po.tensor_tensor(heads3(vb[0:m]), v, bc(ags[0:m, H:2 * H]), ALU.mult).then_inc(scaled, 1)
                    po.tensor_tensor(heads3(kb[0:m, 2]), q, bc(gex[0:m, 0, :]), ALU.mult).then_inc(scaled, 1)
                    po.tensor_tensor(heads3(kb[0:m, 3]), k, bc(gex[0:m, 1, :]), ALU.mult).then_inc(scaled, 1)
                    po.wait_ge(scaled, t * 5 + 4)
                    po.tensor_tensor(heads3(kb[0:m, 1]), heads3(kb[0:m, 0]), bc(gex[0:m, 0, :]), ALU.mult).then_inc(scaled, 1)
                tiles(po, body)

            @block.tensor
            def _(pe):
                pe.wait_ge(ld, 16 * (5 + 2 * NJ))
                pe.wait_ge(clear, 4)
                def body(t, smp, m):
                    g = ags[0:m, 0:H]
                    if not (isinstance(t, int) and t == 0):
                        pe.wait_ge(tile_done, t)
                    pe.wait_ge(src_ready, t * 2 + 2)
                    pe.matmul(A[0:m, 0, 0:H], tri[0:m, smp, 0:m], g)
                    pe.matmul(A[0:m, 0, 8:16], tot[:, 0:m] if smp else ones[:], g)
                    for h in range(H):
                        mm = pe.matmul(Bk[0:m, h // 4, h % 4 * P:h % 4 * P + m], ags[0:m, h:h + 1].to_broadcast([m, m]), tri[0:m, smp, 0:m])
                    if smp:
                        for h in range(H):
                            mm = pe.matmul(A[:, 0, 16 + 8 * h:24 + 8 * h], ags[0:m, h:h + 1].to_broadcast([m, P]), seq[:, :])
                    mm.then_inc(g_prod, 1)
                    pe.wait_ge(scaled, t * 5 + 5)
                    pe.wait_ge(g_read, t + 1)
                    from_ = [src[0:m, 1], kb[0:m, 0], src[0:m, 0], kb[0:m, 1], kb[0:m, 2]]
                    for n, s in enumerate(from_):
                        if n == 4:
                            pe.wait_ge(t_out, t * 5 + 1)
                        for j in range(NJ):
                            mm = pe.transpose(A[:, n % 4, j * P:j * P + m], s[:, j * P:(j + 1) * P], ident[0:m, 0:m])
                        mm.then_inc(t_done, 1)
                    pe.wait_ge(t_out, t * 5 + 5)
                    pe.wait_ge(dec_in, t + 1)
                    for h in range(H):
                        mm = pe.matmul(Bk[0:m, h // 2 % 4, h % 2 * 256:h % 2 * 256 + 2 * m], kz[:, h, 0:m], kq[:, h // 2, :, 0:m])
                        if h % 4 == 3:
                            mm.then_inc(kk_done, 1)
                    hh = lambda a: range(4 * a, 4 * a + 4)
                    for a in range(2):
                        pe.wait_ge(lt_ready, t * 4 + 3 + a)
                        for h in hh(a):
                            mm = pe.transpose(A[0:m, a, h % 4 * P:h % 4 * P + m], xt[0:m, h, 0:m], ident[0:m, 0:m])
                        mm.then_inc(mm_done, 1)
                    nl = levels_of(smp)
                    for li in range(nl):
                        for a in range(2):
                            pe.wait_ge(xt_out, t * (2 * NL) + 2 * li + a + 1)
                            for h in hh(a):
                                mm = pe.matmul(A[0:m, 2 + a, h % 4 * P:h % 4 * P + m], lt[0:m, h, 0:m], x[0:m, h, 0:m])
                            mm.then_inc(mm_done, 1)
                        for a in range(2):
                            pe.wait_ge(dv_out, t * (4 * NL) + 4 * li + a + 1)
                            for h in hh(a):
                                l_, r_ = (xt, yy) if li < nl - 1 else (yy, xt)
                                mm = pe.matmul(Bk[0:m, a, h % 4 * P:h % 4 * P + m], l_[0:m, h, 0:m], r_[0:m, h, 0:m])
                            mm.then_inc(mm_done, 1)
                        for a in range(2):
                            pe.wait_ge(dv_out, t * (4 * NL) + 4 * li + 3 + a)
                            if li < nl - 1:
                                for h in hh(a):
                                    mm = pe.transpose(A[0:m, a, h % 4 * P:h % 4 * P + m], x[0:m, h, 0:m], ident[0:m, 0:m])
                                mm.then_inc(mm_done, 1)
                    if not smp:
                        for j in range(NJ):
                            mm = pe.matmul(A[:, 0, j * P:(j + 1) * P], ke[:, 0, j], S[:, j])
                        mm.then_inc(chain_mm, 1)
                        for j in range(NJ):
                            mm = pe.matmul(A[:, 3, j * P:(j + 1) * P], ke[:, 1, j], S[:, j], start=(j == 0), stop=False, skip_group_check=True)
                    else:
                        for c in range(2):
                            for j in range(NJ):
                                if c or j >= 2:
                                    pe.wait_ge(chain_ev, 2 * QT + 4 * c + j - 1)
                                for b in range(2):
                                    mm = pe.matmul(Bk[0:m, 2 * (j % 2) + b, :], ke[:, c, j, 0:m], SS[:, j, 4 * b:4 * b + 4, :].rearrange("p b e -> p (b e)"))
                                mm.then_inc(chain_mm, 1)
                    ev = t * 2 + (8 if smp else 0)
                    pe.wait_ge(chain_ev, ev + 1)
                    for h in range(H):
                        mm = pe.matmul(A[0:m, 1 + h // 4, h % 4 * P:(h % 4 + 1) * P], xt[0:m, h, 0:m], r[0:m, h // 2 * P:(h // 2 + 1) * P])
                    mm.then_inc(chain_mm, 1)
                    pe.wait_ge(chain_ev, ev + 2)
                    for h in range(H):
                        j = h // 2
                        mm = pe.matmul(A[0:m, 3, j * P:(j + 1) * P], at[0:m, h, 0:m], vz[0:m, h * P:(h + 1) * P],
                                       start=bool(smp and h == 0), stop=True, skip_group_check=True)
                    mm.then_inc(chain_mm, 1)
                    if not smp:
                        for j in range(NJ):
                            mm = pe.matmul(A[:, 0, j * P:(j + 1) * P], kb[:, 3, j * P:(j + 1) * P],
                                           vz[:, j * 256:j * 256 + 384].rearrange("p (a b) -> p a b", a=2)[:, :, 0:HD])
                        mm.then_inc(chain_mm, 1)
                    else:
                        for j in range(NJ):
                            if j >= 2:
                                pe.wait_ge(state_done, j - 1)
                            pe.wait_ge(chain_ev, 2 * QT + 11 + j)
                            for b in range(2):
                                mm = pe.matmul(Bk[:, 2 * (j % 2) + b, :], kb[0:m, 3, j * P:(j + 1) * P], yy[0:m, 4 * b:4 * b + 4, :].rearrange("p b e -> p (b e)"))
                            mm.then_inc(chain_mm, 1)
                tiles(pe, body)
                pe.wait_ge(tile_done, NTI)

            @block.scalar
            def _(act):
                def body(t, smp, m):
                    act.wait_ge(g_read, t + 1)
                    act.activation(gex[0:m, 0, :], gst[0:m, 0:8], ACT.Exp)
                    act.activation(gex[0:m, 1, :], gst[0:m, 16:24], ACT.Exp)
                    if not smp:
                        for h2 in range(2):
                            x_ = act.activation(egl[pair_rows[h2], :], gst[pair_rows[h2], 8 + h2:16:2], ACT.Exp)
                    else:
                        for h2 in range(2):
                            x_ = act.activation(eglS[pair_rows[h2]], A[pair_rows[h2], 0, 16:80].rearrange("p (j a b) -> p j a b", a=2, b=NB)[:, :, h2, :], ACT.Exp)
                    x_.then_inc(exp_ready, 1)
                    act.wait_ge(dec_in, t + 1)
                    act.activation(dec[0:m, :, 0:m], dec[0:m, :, 0:m], ACT.Exp).then_inc(dec_ready, 1)
                    four = lambda n: A[:, n % 4, :].rearrange("p (j t) -> p j t", j=NJ)[:, :, 0:m]
                    act.wait_ge(t_done, t * 5 + 1)
                    act.activation(kz[pair_rows[0], 0:H:2, 0:m], four(0)[pair_rows[0]], ACT.Copy)
                    act.activation(kz[pair_rows[1], 1:H:2, 0:m], four(0)[pair_rows[1]], ACT.Copy).then_inc(t_out, 1)
                    for n, dst in ((1, kq[:, :, 0, 0:m]), (2, kq[:, :, 1, 0:m]), (3, ke[:, 0, :, 0:m]), (4, ke[:, 1, :, 0:m])):
                        act.wait_ge(t_done, t * 5 + (n + 1))
                        act.activation(dst, four(n), ACT.Copy).then_inc(t_out, 1)
                    for li in range(levels_of(smp)):
                        for a in range(2):
                            act.wait_ge(mm_done, t * (6 * NL) + (6 * li + a + 1))
                            act.activation((x if li == 0 else xt)[0:m, 4 * a:4 * a + 4, 0:m], A[0:m, a, :].rearrange("p (h t) -> p h t", h=4)[:, :, 0:m], ACT.Copy).then_inc(xt_out, 1)
                    if not smp:
                        act.wait_ge(chain_mm, t * 4 + 3)
                        act.activation(og[:, bass.ds(t, 1), :].rearrange("p a c -> p (a c)"), A[:, 3, :], ACT.Copy).then_inc(og_out, 1)
                tiles(act, body)

            @block.vector
            def _(dve):
                dve.wait_ge(ld, 16 * (5 + 2 * NJ))
                dve.wait_ge(clear, 4)
                def body(t, smp, m):
                    linked = [0]
                    def link(ins, wait=True):
                        ins.then_inc(step, 1)
                        linked[0] += 1
                        if wait:
                            dve.wait_ge(step, t * LNK + linked[0])
                    bch = lambda ap, n=4: ap.unsqueeze(1).to_broadcast([m, n, m])
                    dve.wait_ge(g_prod, t + 1)
                    link(dve.tensor_copy(gst[0:m, 0:16], A[0:m, 0, 0:16]))
                    dve.tensor_tensor(gst[0:m, 16:24], gst[0:m, 8:16], gst[0:m, 0:8], ALU.subtract).then_inc(g_read, 1)
                    for a in range(2):
                        p_ = Bk[0:m, a, :].rearrange("p (h t) -> p h t", h=4)[:, :, 0:m]
                        link(dve.tensor_tensor(dec[0:m, 4 * a:4 * a + 4, 0:m], p_, gst[0:m, 4 * a:4 * a + 4].unsqueeze(2).to_broadcast([m, 4, m]), ALU.subtract), wait=(a == 1))
                    dve.tensor_tensor(dec[0:m, :, 0:m], dec[0:m, :, 0:m], bch(msk[0:m, smp, 0:m], H), ALU.add).then_inc(dec_in, 1)
                    dve.wait_ge(dec_ready, t + 1)
                    for a in range(2):
                        dve.wait_ge(kk_done, t * 2 + (a + 1))
                        b4 = slice(2 * a, 2 * a + 2)
                        hs = slice(4 * a, 4 * a + 4)
                        p_ = Bk[0:m, b4, :].rearrange("p b (h c) -> p (b h) c", h=2)
                        link(dve.tensor_tensor(lt[0:m, hs, 0:m], p_[:, :, 0:m], dec[0:m, hs, 0:m], ALU.mult), wait=False)
                        dve.tensor_tensor(at[0:m, hs, 0:m], p_[:, :, m:2 * m], dec[0:m, hs, 0:m], ALU.mult).then_inc(lt_ready, 1)
                    for a in range(2):
                        hs = slice(4 * a, 4 * a + 4)
                        if a == 0:
                            dve.wait_ge(step, t * LNK + linked[0])
                        link(dve.tensor_tensor(xt[0:m, hs, 0:m], lt[0:m, hs, 0:m], bch(lvl[0:m, 0, 0:m]), ALU.mult))
                        dve.tensor_tensor(xt[0:m, hs, 0:m], bch(ident[0:m, 0:m]), xt[0:m, hs, 0:m], ALU.subtract).then_inc(lt_ready, 1)
                    nl = levels_of(smp)
                    for li in range(nl):
                        mm0 = t * (6 * NL) + 6 * li
                        for a in range(2):
                            hs = slice(4 * a, 4 * a + 4)
                            dve.wait_ge(mm_done, mm0 + 3 + a)
                            p_ = A[0:m, 2 + a, :].rearrange("p (h t) -> p h t", h=4)[:, :, 0:m]
                            dve.tensor_tensor(yy[0:m, hs, 0:m], p_, bch(lvl[0:m, 1 + li, 0:m]), ALU.mult).then_inc(dv_out, 1)
                        for a in range(2):
                            hs = slice(4 * a, 4 * a + 4)
                            dve.wait_ge(mm_done, mm0 + 5 + a)
                            p_ = Bk[0:m, a, :].rearrange("p (h t) -> p h t", h=4)[:, :, 0:m]
                            dst = x if li < nl - 1 else xt
                            dve.tensor_tensor(dst[0:m, hs, 0:m], dst[0:m, hs, 0:m], p_, ALU.subtract).then_inc(dv_out, 1)
                    if not smp:
                        dve.wait_ge(chain_mm, t * 4 + 1)
                        dve.tensor_tensor(r[:], vb[:], A[:, 0, :], ALU.subtract).then_inc(chain_ev, 1)
                        dve.wait_ge(chain_mm, t * 4 + 2)
                    else:
                        for c in range(2):
                            for j in range(NJ):
                                dve.wait_ge(chain_mm, 4 * QT + 4 * c + j + 1)
                                p_ = Bk[0:m, 2 * (j % 2):2 * (j % 2) + 2, :].rearrange("p c (b e) -> p (c b) e", b=4)
                                dve.tensor_tensor(yy[0:m, 0:NB, :], p_, seq[:, :].unsqueeze(2).to_broadcast([m, NB, P]), ALU.mult).then_inc(chain_ev, 1)
                                dve.wait_ge(chain_ev, 2 * QT + 4 * c + j + 1)
                                dst = r[0:m] if c == 0 else dec[0:m, 0:4, :].rearrange("p a b -> p (a b)")
                                link(dve.tensor_reduce(dst[:, j * P:(j + 1) * P], yy[0:m, 0:NB, :].rearrange("p b e -> p e b"), AX, ALU.add))
                        dve.tensor_tensor(r[0:m], vb[0:m], r[0:m], ALU.subtract).then_inc(chain_ev, 1)
                        dve.wait_ge(chain_mm, 4 * QT + 9)
                    for h2 in range(2):
                        for bk in range(2):
                            p_ = A[0:m, 1 + bk, :].rearrange("p (j a e) -> p j a e", j=2, a=2)[:, :, h2, h2 * HD:(h2 + 1) * HD]
                            z = dve.tensor_copy(vz[0:m, 512 * bk:512 * bk + 512].rearrange("p (j c) -> p j c", j=2)[:, :, h2 * 192:h2 * 192 + HD], p_)
                    z.then_inc(chain_ev, 1)
                    if not smp:
                        dve.wait_ge(chain_mm, t * 4 + 4)
                        for h2 in range(2):
                            q_ = S[pair_rows[h2], :, h2 * HD:(h2 + 1) * HD]
                            link(dve.tensor_tensor(q_, q_, egl[pair_rows[h2], :].unsqueeze(2).to_broadcast([HD, NJ, HD]), ALU.mult), wait=(h2 == 1))
                        dve.wait_ge(og_out, t + 1)
                        for h2 in range(2):
                            q_ = S[pair_rows[h2], :, h2 * HD:(h2 + 1) * HD]
                            z = dve.tensor_tensor(q_, q_, A[pair_rows[h2], 0, :].rearrange("p (j e) -> p j e", j=NJ)[:, :, h2 * HD:(h2 + 1) * HD], ALU.add)
                        z.then_inc(tile_done, 1)
                        assert linked[0] <= LNK
                        for _ in range(LNK - linked[0]):
                            dve.sem_inc(step, 1)
                    else:
                        dve.wait_ge(chain_mm, 4 * QT + 10)
                        link(dve.tensor_tensor(og[0:m, QT, :], dec[0:m, 0:4, :].rearrange("p a b -> p (a b)"), A[0:m, 3, :], ALU.add), wait=False)
                        for j in range(NJ):
                            if j:
                                dve.wait_ge(chain_mm, 4 * QT + 10 + j)
                            for a in range(2):
                                z = dve.tensor_tensor(yy[0:m, 0:NB, a * HD:(a + 1) * HD], vz[0:m, j * 256 + a * 192:j * 256 + a * 192 + HD].unsqueeze(1).to_broadcast([m, NB, HD]),
                                                      seq[:, :].unsqueeze(2).to_broadcast([m, NB, HD]), ALU.mult)
                            z.then_inc(chain_ev, 1)
                            for h2 in range(2):
                                q_ = SS[pair_rows[h2], j, :, h2 * HD:(h2 + 1) * HD]
                                link(dve.tensor_tensor(q_, q_, eglS[pair_rows[h2], j, :].unsqueeze(2).to_broadcast([HD, NB, HD]), ALU.mult), wait=(h2 == 1))
                            dve.wait_ge(chain_mm, 4 * QT + 11 + j)
                            for h2 in range(2):
                                q_ = SS[pair_rows[h2], j, :, h2 * HD:(h2 + 1) * HD]
                                p_ = Bk[pair_rows[h2], 2 * (j % 2):2 * (j % 2) + 2, :].rearrange("p c (b e) -> p (c b) e", b=4)[:, :, h2 * HD:(h2 + 1) * HD]
                                z = dve.tensor_tensor(q_, q_, p_, ALU.add)
                            z.then_inc(state_done, 1)
                        dve.wait_ge(state_done, NJ)
                        dve.sem_inc(tile_done, 1)
                tiles(dve, body)


def stage_gdn_norm(nc, T):
    with ExitStack() as ctx:
        sb = lambda n, s, d=F32: ctx.enter_context(nc.sbuf_tensor(n, s, d))
        sem = lambda n: ctx.enter_context(nc.semaphore(n))
        NTI = QT + 1
        sq = [sb(f"nsq{i}", [P, 512]) for i in range(2)]
        ss = sb("nss", [P, NTI, H])
        gn = sb("gn", [P, HD])
        tP = ctx.enter_context(nc.psum_tensor("ntP", [P, 2, 512], F32))
        ld, sq_ready, ss_ready, rt, sc, turned, done, step = (sem("n" + x) for x in ("ld", "sq_ready", "ss_ready", "rt", "sc", "turned", "done", "step"))
        og, zbT, ident = T["og"], T["zbT"], T["ident"]
        rows = lambda t: P if t < QT else NS
        with nc.Block() as block:
            @block.sync
            def _(sp):
                sp.dma_start(gn[:], T["in"]["gdn_norm"]).then_inc(ld, 16)
                sp.wait_ge(ld, 16)

            @block.scalar
            def _(act):
                for t in range(NTI):
                    m = rows(t)
                    if t >= 2:
                        act.wait_ge(ss_ready, t - 1)
                    act.activation(sq[t % 2][0:m], og[0:m, t, :], ACT.Square).then_inc(sq_ready, 1)
                act.wait_ge(step, 3)
                act.activation(ss[:], ss[:], ACT.Sqrt).then_inc(rt, 1)

            @block.vector
            def _(dve):
                def finish(dve, t):
                    m = rows(t)
                    dve.wait_ge(turned, t + 1)
                    z = zbT[:, :, t * P:t * P + m]
                    dve.tensor_tensor(z, z, tP[:, t % 2, :].rearrange("p (j t) -> p j t", j=NJ)[:, :, 0:m], ALU.mult).then_inc(done, 1)

                dve.memset(ss[:], 1.0).then_inc(step, 1)
                dve.wait_ge(step, 1)
                for t in range(NTI):
                    m = rows(t)
                    dve.wait_ge(sq_ready, t + 1)
                    dve.tensor_reduce(ss[0:m, t, :], sq[t % 2][0:m].rearrange("p (h d) -> p h d", d=HD), AX, ALU.add).then_inc(ss_ready, 1)
                dve.wait_ge(ss_ready, NTI)
                dve.tensor_scalar(ss[:], ss[:], 1.0 / HD, EPS, ALU.mult, ALU.add).then_inc(step, 1)
                dve.wait_ge(step, 2)
                dve.reciprocal(ss[:], ss[:]).then_inc(step, 1)
                dve.wait_ge(rt, 1)
                dve.wait_ge(ld, 16)
                for t in range(NTI):
                    m = rows(t)
                    x = og[0:m, t, :].rearrange("p (h d) -> p h d", d=HD)
                    dve.tensor_tensor(x, x, ss[0:m, t].unsqueeze(2).to_broadcast([m, H, HD]), ALU.mult).then_inc(step, 1)
                    dve.wait_ge(step, 4 + t)
                    dve.tensor_tensor(x, x, gn[0:m].unsqueeze(1).to_broadcast([m, H, HD]), ALU.mult).then_inc(sc, 1)
                    if t:
                        finish(dve, t - 1)
                finish(dve, NTI - 1)

            @block.tensor
            def _(pe):
                for t in range(NTI):
                    m = rows(t)
                    pe.wait_ge(sc, t + 1)
                    if t >= 2:
                        pe.wait_ge(done, t - 1)
                    for j in range(NJ):
                        mm = pe.transpose(tP[:, t % 2, j * P:j * P + m], og[0:m, t, j * P:(j + 1) * P], ident[0:m, 0:m])
                    mm.then_inc(turned, 1)


def stage_gdn(nc, T):
    with nc.sbuf_tensor("qkv", [P, QT + 1, 3, 512], F32) as qkv:
        T["qkv"] = qkv
        with nc.sbuf_tensor("uT", [P, 12, TOK], F32) as uT:
            T["uT"] = uT
            stage_gdn_project(nc, T)
            stage_gdn_tokens(nc, T)
        T["og"] = qkv[:, :, 0, :]
        stage_gdn_scan(nc, T)
        stage_gdn_norm(nc, T)


def stage_output(nc, T):
    with ExitStack() as ctx:
        sb = lambda n, s, d=F32: ctx.enter_context(nc.sbuf_tensor(n, s, d))
        sem = lambda n: ctx.enter_context(nc.semaphore(n))
        NTI = QT + 1
        wg = [sb(f"ow{i}", [P, KT, 256]) for i in range(2)]
        wo = [sb(f"oo{i}", [P, 2, NJ, P]) for i in range(2)]
        mT = sb("mT", [P, KT, TOK])
        sg = [sb(f"sg{i}", [P, TOK]) for i in range(2)]
        pr = sb("pr", [P, TOK])
        gP = ctx.enter_context(nc.psum_tensor("ogP", [P, 3, 512], F32))
        oP = ctx.enter_context(nc.psum_tensor("ooP", [P, 3, 512], F32))
        ld_w = [sem(f"old_w{i}") for i in range(2)]
        g_prod, g_out, o_prod, o_out, step = (sem("o" + n) for n in ("g_prod", "g_out", "o_prod", "o_out", "step"))
        hT, zaT, zbT = T["hT"], T["zaT"], T["zbT"]
        U = 2 * KT
        with nc.Block() as block:
            @block.sync
            def _(sp):
                for f in range(KT):
                    if f >= 2:
                        sp.wait_ge(o_prod, 2 * (f - 1))
                    sp.dma_start(wg[f % 2][:], T["in"]["w_gm"][f].rearrange("p (k n) -> p k n", k=KT)).then_inc(ld_w[f % 2], 16)
                    sp.dma_start(wo[f % 2][:], T["in"]["w_o"][f].rearrange("p (c k n) -> p c k n", c=2, k=NJ)).then_inc(ld_w[f % 2], 16)

            @block.tensor
            def _(pe):
                for u in range(U):
                    f, c = u // 2, u % 2
                    if c == 0:
                        pe.wait_ge(ld_w[f % 2], 32 * (f // 2 + 1))
                    if u:
                        pe.wait_ge(g_out, u)
                    product_features(pe, gP, wg[f % 2], hT, c).then_inc(g_prod, 1)
                    if u:
                        pe.wait_ge(o_out, u)
                    src = (zaT, zbT)[c]
                    for k in range(NJ):
                        for b in range(3):
                            mm = pe.matmul(oP[:, b, 0:TB], wo[f % 2][:, c, k, :], src[:, k, b * TB:(b + 1) * TB], start=(k == 0), stop=(k == NJ - 1))
                    mm.then_inc(o_prod, 1)

            @block.scalar
            def _(act):
                for u in range(U):
                    act.wait_ge(g_prod, u + 1)
                    if u >= 2:
                        act.wait_ge(o_out, u - 1)
                    act.activation(sg[u % 2][:].rearrange("p (b t) -> p b t", b=3), gP[:, :, 0:TB], ACT.Sigmoid).then_inc(g_out, 1)

            @block.vector
            def _(dve):
                for u in range(U):
                    f, c = u // 2, u % 2
                    dve.wait_ge(g_out, u + 1)
                    dve.wait_ge(o_prod, u + 1)
                    dst = mT[:, f, :] if c == 0 else pr[:]
                    dve.tensor_tensor(dst.rearrange("p (b t) -> p b t", b=3), oP[:, :, 0:TB], sg[u % 2][:].rearrange("p (b t) -> p b t", b=3), ALU.mult).then_inc(o_out, 1)
                    if c:
                        dve.wait_ge(o_out, u + 1)
                        dve.tensor_tensor(mT[:, f, :], mT[:, f, :], pr[:], ALU.add).then_inc(step, 1)
                        dve.wait_ge(step, f + 1)

        with ExitStack() as ctx2:
            sb = lambda n, s, d=F32: ctx2.enter_context(nc.sbuf_tensor(n, s, d))
            sem = lambda n: ctx2.enter_context(nc.semaphore(n))
            wf = sb("wf", [P, KT, D_MODEL])
            xr = [sb(f"xr{i}", [P, D_MODEL]) for i in range(2)]
            gt = sb("gt", [P, D_MODEL])
            gs = sb("gs", [NS, D_MODEL])
            fg = sb("fg", [P, D_MODEL])
            sel = sb("osel", [9, P + NS])
            rs = sb("ors", [P, NTI])
            ld, ld_x, y_prod, y_out, st_y, sel_p, gt_ready, st2, q_ready, root = (sem("y" + n) for n in ("ld", "ld_x", "prod", "out", "st", "sel_p", "gt_ready", "step", "sq", "root"))
            ld_xr = [ld_x, sem("yld_x1")]
            st_y = [st_y, sem("yst_1")]
            rows = lambda t: P if t < QT else NS
            y_dram = lambda t: T["out"]["y_prompt"][0, t * P:(t + 1) * P, :] if t < QT else T["out"]["y_sample"].rearrange("b t d -> (b t) d")
            bank = lambda t: (gP if t % 2 == 0 else oP)
            gate = T["gate"]
            with nc.Block() as block:
                @block.sync
                def _(sp):
                    sp.dma_start(sel[:], T["in"]["row_sel"]).then_inc(ld, 16)
                    sp.dma_start(fg[:], T["in"]["final_g"]).then_inc(ld, 16)
                    for n in range(2):
                        sp.dma_start(wf[:, :, n * 512:(n + 1) * 512], T["in"]["w_out"][n].rearrange("p (k n) -> p k n", k=KT)).then_inc(ld, 16)
                    for t in range(NTI):
                        if t >= 2:
                            sp.wait_ge(st_y[t % 2], 16 * (t // 2))
                        sp.dma_start(xr[t % 2][0:rows(t)], T["in"]["x"][t * P:t * P + rows(t), :]).then_inc(ld_xr[t % 2], 16)

                @block.scalar
                def _(act):
                    for t in range(NTI):
                        m = rows(t)
                        act.wait_ge(y_out, t + 1)
                        act.activation(pr[0:m, 0:D_MODEL], xr[t % 2][0:m], ACT.Square, accum_out=rs[0:m, t:t + 1]).then_inc(q_ready, 1)
                        act.wait_ge(st2, 4 * t + 2)
                        act.activation(rs[0:m, t:t + 1], rs[0:m, t:t + 1], ACT.Sqrt).then_inc(root, 1)
                        act.wait_ge(st2, 4 * t + 4)
                        act.dma_start(y_dram(t), xr[t % 2][0:m]).then_inc(st_y[t % 2], 16)
                    act.wait_ge(st_y[0], 16 * ((NTI + 1) // 2))
                    act.wait_ge(st_y[1], 16 * (NTI // 2))

                @block.tensor
                def _(pe):
                    pe.wait_ge(ld, 64)
                    for c in range(2):
                        pe.matmul(gP[:, c, :], sel[:, 0:P], gate[:, c * 512:(c + 1) * 512])
                        mm = pe.matmul(oP[0:NS, c, :], sel[:, P:P + NS], gate[:, c * 512:(c + 1) * 512])
                    mm.then_inc(sel_p, 1)
                    pe.wait_ge(gt_ready, 2)
                    for t in range(NTI):
                        m = rows(t)
                        if t >= 2:
                            pe.wait_ge(y_out, t - 1)
                        for c in range(2):
                            for k in range(KT):
                                mm = pe.matmul(bank(t)[0:m, c, :], mT[:, k, t * P:t * P + m], wf[:, k, c * 512:(c + 1) * 512], start=(k == 0), stop=(k == KT - 1))
                        mm.then_inc(y_prod, 1)

                @block.vector
                def _(dve):
                    dve.wait_ge(sel_p, 1)
                    dve.tensor_copy(gt[:].rearrange("p (c n) -> p c n", c=2), gP[:, 0:2, :]).then_inc(gt_ready, 1)
                    dve.tensor_copy(gs[:].rearrange("p (c n) -> p c n", c=2), oP[0:NS, 0:2, :]).then_inc(gt_ready, 1)
                    dve.wait_ge(gt_ready, 2)
                    dve.wait_ge(ld, 64)
                    for t in range(NTI):
                        m = rows(t)
                        x = xr[t % 2][0:m]
                        dve.wait_ge(y_prod, t + 1)
                        dve.wait_ge(ld_xr[t % 2], 16 * (t // 2 + 1))
                        gate_t = gt if t < QT else gs
                        tmp = sg[t % 2][0:m, 0:D_MODEL]
                        dve.tensor_tensor(tmp.rearrange("p (c n) -> p c n", c=2), bank(t)[0:m, 0:2, :], gate_t[0:m].rearrange("p (c n) -> p c n", c=2), ALU.mult).then_inc(st2, 1)
                        dve.wait_ge(st2, 4 * t + 1)
                        dve.tensor_tensor(x, x, tmp, ALU.add).then_inc(y_out, 1)
                        dve.wait_ge(q_ready, t + 1)
                        dve.tensor_scalar(rs[0:m, t:t + 1], rs[0:m, t:t + 1], 1.0 / D_MODEL, EPS, ALU.mult, ALU.add).then_inc(gt_ready, 1)
                        dve.wait_ge(gt_ready, 3 + t)
                        dve.reciprocal(rs[0:m, t:t + 1], rs[0:m, t:t + 1]).then_inc(st2, 1)
                        dve.wait_ge(root, t + 1)
                        dve.tensor_scalar(x, x, rs[0:m, t:t + 1], None, ALU.mult).then_inc(st2, 1)
                        dve.wait_ge(st2, 4 * t + 3)
                        dve.tensor_tensor(x, x, fg[0:m], ALU.mult).then_inc(st2, 1)


def build(nc, ins, outs):
    T = {"in": ins, "out": outs}
    with ExitStack() as ctx:
        def sb(name, shape, dt=F32):
            T[name] = ctx.enter_context(nc.sbuf_tensor(name, shape, dt))
        sb("hT", [P, KT, TOK])
        sb("gate", [9, D_MODEL])
        sb("ones", [P, P])
        sb("ident", [P, P])
        sb("zaT", [P, NJ, TOK])
        sb("zbT", [P, NJ, TOK])
        sb("ab_t", [P, QT + 1, 16])
        stage_input(nc, T)
        with nc.sbuf_tensor("qT", [P, NJ, TOK], F32) as qT, nc.sbuf_tensor("kvt", [P, QT + 1, KVG], F32) as kvt:
            T["qT"], T["kvt"] = qT, kvt
            stage_nsa_project(nc, T)
            with nc.sbuf_tensor("kvT", [P, 2, TOK], F32) as kvT, nc.sbuf_tensor("kcT", [P, NSEQ, 64], F32) as kcT, \
                    nc.sbuf_tensor("vc", [NCMP, NSEQ, P], F32) as vc:
                T["kvT"], T["kcT"], T["vc"] = kvT, kcT, vc
                stage_compress(nc, T)
                stage_sample_attention(nc, T)
                stage_prompt_attention(nc, T)
        stage_gdn(nc, T)
        stage_output(nc, T)


def layouts(inp):
    a = {k: np.asarray(v) for k, v in inp.items()}
    f = np.float32
    c = np.concatenate([a["c_sample"], a["c_prompt"]], 0)
    x = np.concatenate([a["x_prompt"][0], a["x_sample"].reshape(NS, D_MODEL)], 0)
    o = {}
    o["cT"] = np.ascontiguousarray(c.T.reshape(KT, P, 9).transpose(1, 0, 2))
    o["xT"] = np.ascontiguousarray(x.T.reshape(KT, P, TOK).transpose(1, 0, 2))
    o["x"] = x
    wt = lambda w, n: np.ascontiguousarray(w.reshape(-1, P, w.shape[1] // n, n).transpose(2, 1, 0, 3).reshape(w.shape[1] // n, P, -1))
    o["w_ada"] = wt(a["w_ada"][0], 512)
    o["b_ada"] = np.ascontiguousarray(np.broadcast_to(a["b_ada"][0], (9, 3072)))
    o["norm_gT"] = np.ascontiguousarray(a["norm_g"][0].reshape(KT, P).T)
    w = a["w_in"][0]
    pair = np.arange(512).reshape(2, NJ, HD).transpose(1, 0, 2).reshape(-1)
    q, kv, g = w[:, 0:512], w[:, 512:1280], w[:, 1280:1304]
    za, qkv, ab, zb, gm = w[:, 1304:1816], w[:, 1816:3352], w[:, 3352:3368], w[:, 3368:3880], w[:, 3880:5928]
    o["w_feat_full"] = np.concatenate([q[:, pair], za[:, pair], qkv, zb, gm], 1)
    o["w_tok"] = wt(np.concatenate([kv, g, ab], 1), KVH)
    o["ident"] = np.eye(P, dtype=f)
    extra_layouts(a, o, pair, f)
    return o


def extra_layouts(a, o, pair, f):
    cc = a["cache_cmp_kv"][0]
    o["cmp_pool"] = np.ascontiguousarray(cc.reshape(NPOOL, 8, 16, 2, 2, HD).transpose(0, 4, 5, 3, 2, 1).reshape(NPOOL, P, 256))
    cs = a["cache_sel_kv"][0].reshape(NPOOL, PAGE, 2, P)
    o["sel_k"] = np.ascontiguousarray(cs[:, :, 0].transpose(0, 2, 1))
    o["sel_v"] = np.ascontiguousarray(cs[:, :, 1])
    cw = a["cache_win_kv"][0].reshape(NB, WIN, 2, P)
    o["cache_win"] = cw.reshape(NB, WIN, 2 * P)
    o["win_k"] = np.ascontiguousarray(cw[:, :, 0].reshape(2, 4, WIN, P).transpose(0, 3, 1, 2).reshape(2, P, 4 * WIN))
    o["win_v"] = np.ascontiguousarray(cw[:, :, 1].reshape(2, 4, 4, P, P).transpose(0, 3, 1, 2, 4).reshape(2, P, 16 * P))
    o["pages"] = a["page_table"].reshape(1, NB * NPAGE)
    both = lambda n: np.stack([a[n + "_k"][0], a[n + "_v"][0]])
    o["cmp_w1"] = np.ascontiguousarray(both("cmp_w1").transpose(2, 0, 1, 3))
    o["cmp_w2"] = np.ascontiguousarray(both("cmp_w2").transpose(1, 0, 2))
    pe = both("cmp_pe").transpose(2, 0, 1)
    o["cmp_pe"] = np.ascontiguousarray(np.concatenate([pe, pe], 0))
    r = np.arange(P)
    g, j, t = (r // 16) % 2, (r // 4) % 4, r % 4
    h = g * NJ + j
    slope = (0.5 ** (h + 1.0))[:, None]
    end = np.arange(NCMP) * 16 + 31
    now = (1024 + t)[:, None]
    tab = np.zeros((P, 1840), f)
    tab[:, 0:63] = -slope * (now - end)
    tab[:, 63:1087] = -slope * (now - np.arange(1024))
    wpos = 512 + np.arange(512)
    tab[:, 1087:1599] = np.where(now - wpos < WIN, -slope * (now - wpos), NEG)
    for G in range(2):
        b = G * 4 + r // 32
        tok = np.arange(NS)
        ok = (tok // 4 == b[:, None]) & (tok % 4 <= t[:, None])
        tab[:, 1599 + 32 * G:1631 + 32 * G] = np.where(ok, -slope * (t[:, None] - tok % 4), NEG)
    i16, j64 = np.arange(NCMP)[:, None] * 16, np.arange(16)[None] * 64
    tab[:NCMP, 1663:1679] = np.clip(np.minimum(i16 + 32, j64 + 64) - np.maximum(i16, j64), 0, None) / 32
    same = (r[:, None] // 32 == r // 32) & (g[:, None] == g) & (t[:, None] == t)
    tab[:, 1679:1807] = same
    tab[:, 1807:1815] = h[:, None] == np.arange(H)
    tab[:, 1815:1831] = np.arange(16)
    tab[:, 1831], tab[:, 1832] = g == 0, g == 1
    o["sample_tab"] = tab
    o["token_sel"] = np.ascontiguousarray(np.stack([(np.arange(NS)[:, None] == (G * 4 + r // 32) * 4 + t) for G in range(2)], 1).astype(f))
    more_layouts(a, o, pair, f)


def more_layouts(a, o, pair, f):
    p, c = np.arange(P)[:, None], np.arange(SEQ)
    d = p - (c - (SEQ - P))
    o["dist"] = np.where(d >= 0, -d, NEG).astype(f)
    d = p - np.arange(P) + WIN
    o["dist_w"] = np.where(d < WIN, -d, NEG).astype(f)
    d = (np.arange(QT)[:, None] * P + np.arange(P))[:, :, None] - (np.arange(64) * 16 + 31)
    o["dist_c"] = np.ascontiguousarray(np.where(d >= 0, -d, NEG).astype(f).transpose(1, 0, 2))
    o["slope"] = np.ascontiguousarray(np.broadcast_to((0.5 ** (np.arange(2) * NJ + np.arange(NJ)[:, None] + 1.0)).reshape(-1), (P, H)).astype(f))
    gdn_layouts(a, o, pair, f)


def gdn_layouts(a, o, pair, f):
    w = o.pop("w_feat_full")
    wt = lambda w, n: np.ascontiguousarray(w.reshape(-1, P, w.shape[1] // n, n).transpose(2, 1, 0, 3).reshape(w.shape[1] // n, P, -1))
    o["w_feat"] = wt(w[:, 0:3072], 256)
    gm = w[:, 3072:].reshape(D_MODEL, 2, KT, P).transpose(0, 2, 1, 3).reshape(D_MODEL, 2048)
    o["w_gm"] = wt(gm, 256)
    o["conv_w"] = np.ascontiguousarray(np.concatenate([a["conv_w"][0], a["conv_b"]], 0).reshape(5, 12, P).transpose(2, 1, 0))
    o["conv_state"] = np.ascontiguousarray(a["state_conv"][0].reshape(NB, 3, 12, P).transpose(3, 2, 0, 1))
    o["gdn_state"] = np.ascontiguousarray(a["state_gdn"][0].reshape(NB, NJ, P, HD).transpose(2, 1, 0, 3))
    o["gdn_ab"] = np.ascontiguousarray(np.broadcast_to(np.stack([a["gdn_dt_bias"][0], a["gdn_a_log"][0]]), (P, 2, H)))
    o["gdn_norm"] = np.ascontiguousarray(np.broadcast_to(a["gdn_norm_g"][0], (P, HD)))
    i = np.arange(P)
    same = i[:, None] // NT == i // NT
    le = i[:, None] <= i
    o["tri"] = np.ascontiguousarray(np.stack([le, le & same], 1).astype(f))
    o["tot"] = np.ascontiguousarray(same[0:NS].astype(f))
    o["seq"] = np.ascontiguousarray((np.arange(NS)[:, None] // NT == np.arange(NB)).astype(f))
    o["msk"] = np.ascontiguousarray(np.where(np.stack([le, le & same], 1), 0, NEG).astype(f))
    m = lambda s: (i[:, None] // s == i // s + 1) & (i[:, None] // s % 2 == 1)
    o["lvl"] = np.ascontiguousarray(np.stack([m(1).T] + [m(2 ** n) for n in range(1, 7)], 1).astype(f))
    wo = np.stack([a["w_o_nsa"][0][pair], a["w_o_gdn"][0]])
    o["w_o"] = np.ascontiguousarray(wo.reshape(2, NJ, P, KT, P).transpose(3, 2, 0, 1, 4).reshape(KT, P, -1))
    o["w_out"] = wt(a["w_out"][0], 512)
    o["final_g"] = np.ascontiguousarray(np.broadcast_to(a["final_g"], (P, D_MODEL)))
    o["row_sel"] = np.ascontiguousarray(np.concatenate([np.arange(9)[:, None] == np.full(P, 8), np.arange(9)[:, None] == np.arange(NS) // NT], 1).astype(f))


OUTS = [("y_prompt", (1, SEQ, D_MODEL)), ("y_sample", (NB, NT, D_MODEL)),
        ("cmp_p", (1, 1, SEQ, 2, 2, HD)), ("sel_p", (1, 1, SEQ, 2, 2, HD)), ("win_p", (1, 1, WIN, 2, 2, HD)),
        ("conv_p", (P, 12, 3)), ("gdn_p", (P, NJ, HD)),
        ("cmp_s", (1, NB, NT, 2, 2, HD)), ("sel_s", (1, NB, NT, 2, 2, HD)), ("win_s", (1, NB, WIN, 2, 2, HD)),
        ("conv_s", (P, 12, NB, 3)), ("gdn_s", (P, NJ, NB, HD))]


def kernel(**inputs):
    import concourse.bacc as bacc
    from concourse.bass_utils import run_bass_kernel_spmd

    arrays = layouts(inputs)
    nc = bacc.Bacc("TRN2", target_bir_lowering=False, num_devices=1)
    ins = {k: nc.dram_tensor(f"in_{k}", v.shape, mybir.dt.from_np(v.dtype), kind="ExternalInput").ap() for k, v in arrays.items()}
    outs = {k: nc.dram_tensor(f"out_{k}", s, F32, kind="ExternalOutput").ap() for k, s in OUTS}
    build(nc, ins, outs)
    r = run_bass_kernel_spmd(nc, [{f"in_{k}": v for k, v in arrays.items()}], core_ids=[0]).results[0]
    y = {k: r[f"out_{k}"] for k, _ in OUTS}
    conv_p = y["conv_p"].transpose(2, 1, 0).reshape(1, 1, 3, 1536)
    conv_s = y["conv_s"].transpose(2, 3, 1, 0).reshape(1, NB, 3, 1536)
    gdn_p = y["gdn_p"].reshape(2, HD, NJ, HD).transpose(2, 0, 1, 3).reshape(1, 1, H, HD, HD)
    gdn_s = y["gdn_s"].reshape(2, HD, NJ, NB, HD).transpose(3, 2, 0, 1, 4).reshape(1, NB, H, HD, HD)
    return (y["y_prompt"], y["y_sample"], y["cmp_p"], y["sel_p"], y["win_p"], conv_p, gdn_p,
            y["cmp_s"], y["sel_s"], y["win_s"], conv_s, gdn_s)
```

```python
from contextlib import ExitStack

import numpy as np

import concourse.bass as bass
from concourse import mybir

F32 = mybir.dt.float32
I32 = mybir.dt.int32
ALU = mybir.AluOpType
ACT = mybir.ActivationFunctionType
AX = mybir.AxisListType.X

P = 128
D_MODEL = 1024
SEQ = 1024
NB, NT = 8, 4
NS = NB * NT
TOK = SEQ + NS
KT = D_MODEL // P
TB = TOK // 3
QT = SEQ // P
H, HD = 8, 64
NJ = H // 2
PAGE = 128
NPAGE = 1024 // PAGE
NPOOL = NB * NPAGE * 5 // 4
NCMP = 63
NSEQ = NB + 1
WIN = 512
KVG = 6 * P + 24 + 16
KVH = KVG // 2
A_OFF, B_OFF = 6 * P + 24, 6 * P + 32
RS = 32
NEG = -1.0e30
GUARD = 1.0e25
TINY = 1.17549435e-38
EPS = 1e-6
CW = 1083


def stage_input(nc, T):
    with ExitStack() as ctx:
        sb = lambda n, s, d=F32: ctx.enter_context(nc.sbuf_tensor(n, s, d))
        sem = lambda n: ctx.enter_context(nc.semaphore(n))
        cT = sb("cT", [P, KT, 9])
        wa = [sb(f"wa{i}", [P, KT, 512]) for i in range(3)]
        bada = sb("bada", [9, 3072])
        gT = sb("gT", [P, KT])
        sq = [sb(f"sq{i}", [P, TOK]) for i in range(2)]
        rstd = sb("rstd", [P, TOK])
        modA = sb("modA", [P, KT, 9])
        modB = sb("modB", [P, KT, 9])
        adaP = ctx.enter_context(nc.psum_tensor("adaP", [P, 2, 512], F32))
        sumP = ctx.enter_context(nc.psum_tensor("sumP", [P, 3, 512], F32))
        trP = ctx.enter_context(nc.psum_tensor("trP", [P, 512], F32))
        ld_c, ld_x, ld_b = sem("ld_c"), sem("ld_x"), sem("ld_b")
        ld_wa = [sem(f"ld_wa{i}") for i in range(3)]
        silu_ready, sq_ready, sq_used = sem("silu_ready"), sem("sq_ready"), sem("sq_used")
        ada_prod, ada_ready, ada_t, mod_ready = sem("ada_prod"), sem("ada_ready"), sem("ada_t"), sem("mod_ready")
        inv_ready, rstd_ready, dve_step = sem("inv_ready"), sem("rstd_ready"), sem("dve_step")
        shsc = sb("shsc", [9, 2 * D_MODEL])
        hT, gate, ones, ident = T["hT"], T["gate"], T["ones"], T["ident"]
        ada = [(shsc, n * 512) for n in range(4)] + [(gate, n * 512) for n in range(2)]

        with nc.Block() as block:
            @block.sync
            def _(sp):
                sp.dma_start(cT[:], T["in"]["cT"]).then_inc(ld_c, 16)
                sp.dma_start(ident[:], T["in"]["ident"]).then_inc(ld_b, 16)
                sp.dma_start(bada[:], T["in"]["b_ada"]).then_inc(ld_b, 16)
                sp.dma_start(gT[:], T["in"]["norm_gT"]).then_inc(ld_b, 16)
                for n in range(6):
                    if n >= 3:
                        sp.wait_ge(ada_prod, n - 2)
                    sp.dma_start(wa[n % 3][:], T["in"]["w_ada"][n].rearrange("p (k n) -> p k n", k=KT)).then_inc(ld_wa[n % 3], 16)
                sp.wait_ge(ld_b, 48)

            @block.scalar
            def _(act):
                for k in range(KT):
                    act.dma_start(hT[:, k, :], T["in"]["xT"][:, k, :]).then_inc(ld_x, 16)
                act.wait_ge(ld_c, 16)
                act.activation(cT[:], cT[:], ACT.Silu).then_inc(silu_ready, 1)
                act.wait_ge(ld_x, 16 * KT)
                for k in range(KT):
                    if k >= 2:
                        act.wait_ge(sq_used, k - 1)
                    act.activation(sq[k % 2][:], hT[:, k, :], ACT.Square).then_inc(sq_ready, 1)
                act.wait_ge(inv_ready, 1)
                act.activation(rstd[:], rstd[:], ACT.Sqrt).then_inc(rstd_ready, 1)

            @block.tensor
            def _(pe):
                pe.wait_ge(dve_step, 1)
                for k in range(KT):
                    pe.wait_ge(sq_ready, k + 1)
                    for b in range(3):
                        mm = pe.matmul(sumP[:, b, 0:TB], ones[:], sq[k % 2][:, b * TB:(b + 1) * TB],
                                       start=(k == 0), stop=(k == KT - 1))
                    mm.then_inc(sq_used, 1)
                pe.wait_ge(silu_ready, 1)
                for n in range(6):
                    pe.wait_ge(ld_wa[n % 3], 16 * (n // 3 + 1))
                    if n >= 2:
                        pe.wait_ge(ada_ready, n - 1)
                    for k in range(KT):
                        mm = pe.matmul(adaP[0:9, n % 2, :], cT[:, k, :], wa[n % 3][:, k, :],
                                       start=(k == 0), stop=(k == KT - 1))
                    mm.then_inc(ada_prod, 1)
                pe.wait_ge(ada_ready, 4)
                pe.wait_ge(ld_b, 48)
                for k in range(16):
                    mm = pe.transpose(trP[:, k * 9:k * 9 + 9], shsc[:, k * P:(k + 1) * P], ident[0:9, 0:9])
                mm.then_inc(ada_t, 1)

            @block.vector
            def _(dve):
                dve.memset(ones[:], 1.0).then_inc(dve_step, 1)
                dve.wait_ge(sq_used, KT)
                dve.tensor_scalar(rstd[:].rearrange("p (b t) -> p b t", b=3), sumP[:, :, 0:TB], 1.0 / D_MODEL, EPS, ALU.mult, ALU.add).then_inc(dve_step, 1)
                dve.wait_ge(dve_step, 2)
                dve.reciprocal(rstd[:], rstd[:]).then_inc(inv_ready, 1)
                dve.wait_ge(ld_b, 48)
                for n in range(6):
                    dve.wait_ge(ada_prod, n + 1)
                    dst, at = ada[n]
                    dve.tensor_tensor(dst[:, at:at + 512], adaP[0:9, n % 2, :],
                                      bada[:, n * 512:(n + 1) * 512], ALU.add).then_inc(ada_ready, 1)
                dve.wait_ge(ada_t, 1)
                dve.tensor_copy(modB[:], trP[:, 0:72].rearrange("p (k r) -> p k r", k=KT)).then_inc(mod_ready, 1)
                dve.tensor_scalar(modA[:], trP[:, 72:144].rearrange("p (k r) -> p k r", k=KT), 1.0, None, ALU.add).then_inc(mod_ready, 1)
                dve.wait_ge(mod_ready, 2)
                dve.tensor_tensor(modA[:], modA[:], gT[:].unsqueeze(2).to_broadcast([P, KT, 9]), ALU.mult).then_inc(mod_ready, 1)
                dve.wait_ge(rstd_ready, 1)
                dve.wait_ge(mod_ready, 3)
                for k in range(KT):
                    dve.tensor_tensor(hT[:, k, :], hT[:, k, :], rstd[:], ALU.mult).then_inc(dve_step, 1)
                dve.wait_ge(dve_step, 2 + KT)
                for k in range(KT):
                    dve.tensor_scalar(hT[:, k, 0:SEQ], hT[:, k, 0:SEQ], modA[:, k, 8:9], modB[:, k, 8:9], ALU.mult, ALU.add)
                    hs = hT[:, k, SEQ:TOK].rearrange("p (b t) -> p b t", b=NB)
                    dve.tensor_tensor(hs, hs, modA[:, k, 0:NB].unsqueeze(2).to_broadcast([P, NB, NT]), ALU.mult).then_inc(dve_step, 1)
                dve.wait_ge(dve_step, 2 + 2 * KT)
                for k in range(KT):
                    hs = hT[:, k, SEQ:TOK].rearrange("p (b t) -> p b t", b=NB)
                    dve.tensor_tensor(hs, hs, modB[:, k, 0:NB].unsqueeze(2).to_broadcast([P, NB, NT]), ALU.add)


def product_features(pe, out, w, x, ft, first_wait=None):
    for k in range(KT):
        for b in range(3):
            mm = pe.matmul(out[:, b, 0:TB], w[:, k, ft * P:(ft + 1) * P], x[:, k, b * TB:(b + 1) * TB],
                           start=(k == 0), stop=(k == KT - 1))
    return mm


def stage_nsa_project(nc, T):
    with ExitStack() as ctx:
        sb = lambda n, s, d=F32: ctx.enter_context(nc.sbuf_tensor(n, s, d))
        sem = lambda n: ctx.enter_context(nc.semaphore(n))
        w = [sb(f"w{i}", [P, KT, 256]) for i in range(2)]
        wt = [sb(f"wt{i}", [P, KT, KVH]) for i in range(2)]
        featP = [ctx.enter_context(nc.psum_tensor(f"featP{i}", [P, 3, 512], F32)) for i in range(2)]
        tokP = ctx.enter_context(nc.psum_tensor("tokP", [P, 2, 512], F32))
        ld_w = [sem(f"ld_w{i}") for i in range(2)]
        ld_wt, feat_prod, feat_out = sem("ld_wt"), sem("feat_prod"), sem("feat_out")
        tok_prod, tok_out, ab_clear = sem("tok_prod"), sem("tok_out"), sem("ab_clear")
        hT, kvt = T["hT"], T["kvt"]
        dests = [(2 * blk + n, dst, 2 * n, fn, scale) for blk, dst, fn, scale in
                 ((0, T["qT"], ACT.Copy, HD ** -0.5), (1, T["zaT"], ACT.Silu, 1.0), (5, T["zbT"], ACT.Silu, 1.0)) for n in range(2)]
        tiles = [(t, h) for t in range(QT + 1) for h in range(2)]

        with nc.Block() as block:
            @block.sync
            def _(sp):
                for n in range(2):
                    sp.dma_start(wt[n][:], T["in"]["w_tok"][n].rearrange("p (k n) -> p k n", k=KT)).then_inc(ld_wt, 16)
                for n, (blk, _, _, _, _) in enumerate(dests):
                    if n >= 2:
                        sp.wait_ge(feat_prod, 2 * (n - 1))
                    sp.dma_start(w[n % 2][:], T["in"]["w_feat"][blk].rearrange("p (k n) -> p k n", k=KT)).then_inc(ld_w[n % 2], 16)

            @block.tensor
            def _(pe):
                pe.wait_ge(ld_wt, 32)
                for n, (t, h) in enumerate(tiles):
                    m = P if t < QT else NS
                    if n >= 2:
                        pe.wait_ge(tok_out, n - 1)
                    for k in range(KT):
                        mm = pe.matmul(tokP[0:m, n % 2, 0:KVH], hT[:, k, t * P:t * P + m], wt[h][:, k, :],
                                       start=(k == 0), stop=(k == KT - 1))
                    mm.then_inc(tok_prod, 1)
                for n in range(len(dests)):
                    pe.wait_ge(ld_w[n % 2], 16 * (n // 2 + 1))
                    for ft in range(2):
                        u = 2 * n + ft
                        if u >= 2:
                            pe.wait_ge(feat_out, u - 1)
                        mm = product_features(pe, featP[u % 2], w[n % 2], hT, ft)
                        mm.then_inc(feat_prod, 1)

            @block.vector
            def _(dve):
                for n, (t, h) in enumerate(tiles):
                    m = P if t < QT else NS
                    dve.wait_ge(tok_prod, n + 1)
                    dve.tensor_copy(kvt[0:m, t, h * KVH:(h + 1) * KVH], tokP[0:m, n % 2, 0:KVH]).then_inc(tok_out, 1)
                dve.memset(T["ab_t"][:], 0.0).then_inc(ab_clear, 1)
                dve.wait_ge(ab_clear, 1)
                dve.wait_ge(tok_out, len(tiles))
                dve.tensor_copy(T["ab_t"][:, 0:QT, :], kvt[:, 0:QT, A_OFF:KVG])
                dve.tensor_copy(T["ab_t"][0:NS, QT, :], kvt[0:NS, QT, A_OFF:KVG])

            @block.scalar
            def _(act):
                for n, (_, dst, at, fn, scale) in enumerate(dests):
                    for ft in range(2):
                        u = 2 * n + ft
                        act.wait_ge(feat_prod, u + 1)
                        act.activation(dst[:, at + ft, :].rearrange("p (b t) -> p b t", b=3), featP[u % 2][:, :, 0:TB],
                                       fn, scale=scale).then_inc(feat_out, 1)


def stage_compress(nc, T):
    with ExitStack() as ctx:
        sb = lambda n, s, d=F32: ctx.enter_context(nc.sbuf_tensor(n, s, d))
        sem = lambda n: ctx.enter_context(nc.semaphore(n))
        w1 = sb("cw1", [P, 2, RS, P])
        pe2 = sb("pe2", [P, 2, RS])
        w2 = sb("cw2", [P, 2, P])
        bias = sb("bias", [P, 2])
        xc = [sb(f"xc{i}", [P, 2 * NPAGE, 2, 16, 8]) for i in range(2)]
        hs = [sb(f"hs{i}", [P, 2, 127]) for i in range(2)]
        pages = sb("pages", [1, NB * NPAGE], I32)
        cmpT = sb("cmpT", [P, 2, SEQ])
        trP = ctx.enter_context(nc.psum_tensor("trP2", [P, 2, 512], F32))
        biasP = ctx.enter_context(nc.psum_tensor("biasP", [P, 512], F32))
        preP = ctx.enter_context(nc.psum_tensor("preP", [P, 2, 512], F32))
        kvP = ctx.enter_context(nc.psum_tensor("kvP", [P, 2, 512], F32))
        w_zero, ld_w, ld_pg = sem("w_zero"), sem("ld_cw"), sem("ld_pg")
        ld_x = [sem(f"ld_xc{i}") for i in range(2)]
        kv_t, kv_copied, bias_prod, bias_ready = sem("kv_t"), sem("kv_copied"), sem("bias_prod"), sem("bias_ready")
        pre_prod, hs_ready, cmp_prod, cmp_ready, st_kv = sem("pre_prod"), sem("hs_ready"), sem("cmp_prod"), sem("cmp_ready"), sem("st_kv")
        kvt, kvT, kcT, vc, ident = T["kvt"], T["kvT"], T["kcT"], T["vc"], T["ident"]
        pool = T["in"]["cmp_pool"]
        BLK = [0, 1, 2, 4]

        with nc.Block() as block:
            @block.sync
            def _(sp):
                sp.dma_start(pages[:], T["in"]["pages"]).then_inc(ld_pg, 16)
                sp.wait_ge(ld_pg, 16)

                def load_pair(pair, half):
                    for p in range(2 * NPAGE):
                        page = sp.value_load(pages[0:1, bass.ds(pair * (2 * NPAGE) + p, 1)], min_val=0, max_val=NPOOL - 1)
                        sp.dma_start(xc[half][:, p], pool[bass.ds(page, 1)].rearrange("a p (k s n) -> (a p) k s n", k=2, s=16)).then_inc(ld_x[half], 16)

                for half in range(2):
                    load_pair(half, half)
                for half in range(2):
                    sp.wait_ge(pre_prod, half + 1)
                    load_pair(2 + half, half)

            @block.gpsimd
            def _(pool_e):
                pool_e.memset(w1[:], 0.0).then_inc(w_zero, 1)
                pool_e.memset(w2[:], 0.0).then_inc(w_zero, 1)
                o, sel = T["out"], lambda c: slice(c * 2 * P, (c + 1) * 2 * P)
                rows = lambda ap: ap.rearrange("a b t k g d -> (a b t) (k g d)")
                pool_e.dma_start(rows(o["cmp_p"]).rearrange("(n p) c -> p n c", p=P), kvt[:, 0:QT, sel(0)]).then_inc(st_kv, 16)
                pool_e.dma_start(rows(o["sel_p"]).rearrange("(n p) c -> p n c", p=P), kvt[:, 0:QT, sel(1)]).then_inc(st_kv, 16)
                pool_e.dma_start(rows(o["win_p"]).rearrange("(n p) c -> p n c", p=P), kvt[:, QT // 2:QT, sel(2)]).then_inc(st_kv, 16)
                pool_e.dma_start(rows(o["cmp_s"]), kvt[0:NS, QT, sel(0)]).then_inc(st_kv, 16)
                pool_e.dma_start(rows(o["sel_s"]), kvt[0:NS, QT, sel(1)]).then_inc(st_kv, 16)
                win = o["win_s"].rearrange("a b t k g d -> (a b) t (k g d)")
                for b in range(NB):
                    pool_e.dma_start(win[b, WIN - NT:WIN, :], kvt[b * NT:(b + 1) * NT, QT, sel(2)]).then_inc(st_kv, 16)
                pool_e.dma_start(win[:, 0:WIN - NT, :], T["in"]["cache_win"][:, NT:WIN, :]).then_inc(st_kv, 16)
                pool_e.wait_ge(st_kv, 16 * (6 + NB))

            @block.tensor
            def _(pe):
                for t in range(QT + 1):
                    m = P if t < QT else NS
                    if t >= 2:
                        pe.wait_ge(kv_copied, t - 1)
                    for n, c in list(enumerate(BLK))[0 if t < QT else 2:]:
                        mm = pe.transpose(trP[:, t % 2, n * P:n * P + m], kvt[0:m, t, c * P:(c + 1) * P], ident[0:m, 0:m])
                    mm.then_inc(kv_t, 1)
                pe.wait_ge(ld_w, 80)
                for kv in range(2):
                    for rs in range(RS):
                        mm = pe.matmul(biasP[:, kv:kv + 1], w1[:, kv, rs, :], pe2[:, kv, rs:rs + 1], start=(rs == 0), stop=(rs == RS - 1))
                mm.then_inc(bias_prod, 1)

                def conv(src, s, n):
                    for kv in range(2):
                        for r in range(2):
                            for t in range(16):
                                mm = pe.matmul(preP[:, s, kv * 256 + 1 - r:kv * 256 + n + 1 - r], w1[:, kv, r * 16 + t, :], src(kv, t),
                                               start=(r == 0 and t == 0), stop=(r == 1 and t == 15), skip_group_check=True)
                    return mm

                def up(s, seqs):
                    n = 64 * seqs - 1
                    pe.matmul(kvP[:, s, 0:n], w2[:, 0, :], hs[s][:, 0, 0:n])
                    for a in range(seqs):
                        mm = pe.matmul(kvP[0:NCMP, s, (a + 1) * 128:(a + 2) * 128], hs[s][:, 1, a * 64:a * 64 + NCMP], w2[:, 1, :])
                    return mm

                with pe.Fori(0, NB // 4) as i:
                    for half in range(2):
                        pe.wait_ge(ld_x[half], i * (32 * NPAGE) + 32 * NPAGE)
                        conv(lambda kv, t: xc[half][:, :, kv, t, :], half, 128).then_inc(pre_prod, 1)
                    for half in range(2):
                        pe.wait_ge(hs_ready, i * 2 + half + 1)
                        up(half, 2).then_inc(cmp_prod, 1)
                    pe.wait_ge(cmp_ready, i * 2 + 2)
                pe.wait_ge(kv_copied, QT + 1)
                conv(lambda kv, t: cmpT[:, kv, t:SEQ:16], 0, 64).then_inc(pre_prod, 1)
                pe.wait_ge(hs_ready, NB // 2 + 1)
                up(0, 1).then_inc(cmp_prod, 1)

            @block.scalar
            def _(act):
                act.dma_start(pe2[:], T["in"]["cmp_pe"]).then_inc(ld_w, 16)
                act.wait_ge(w_zero, 2)
                for g in range(2):
                    act.dma_start(w1[g * HD:(g + 1) * HD, :, :, g * HD:(g + 1) * HD], T["in"]["cmp_w1"]).then_inc(ld_w, 16)
                    act.dma_start(w2[g * HD:(g + 1) * HD, :, g * HD:(g + 1) * HD], T["in"]["cmp_w2"]).then_inc(ld_w, 16)

                def silus(s, seqs):
                    n = 64 * seqs - 1
                    for kv in range(2):
                        ins = act.activation(hs[s][:, kv, 0:n], preP[:, s, kv * 256 + 1:kv * 256 + 1 + n], ACT.Silu, bias=bias[:, kv:kv + 1])
                    return ins
                act.wait_ge(bias_ready, 1)
                with act.Fori(0, NB // 4) as i:
                    for half in range(2):
                        act.wait_ge(pre_prod, i * 2 + half + 1)
                        silus(half, 2).then_inc(hs_ready, 1)
                act.wait_ge(pre_prod, NB // 2 + 1)
                silus(0, 1).then_inc(hs_ready, 1)

            @block.vector
            def _(dve):
                for t in range(QT + 1):
                    m = P if t < QT else NS
                    dve.wait_ge(kv_t, t + 1)
                    tr = trP[:, t % 2, :].rearrange("p (n t) -> p n t", n=4)
                    if t < QT:
                        dve.tensor_copy(cmpT[:, :, t * P:t * P + m], tr[:, 0:2, :])
                    dve.tensor_copy(kvT[:, :, t * P:t * P + m], tr[:, 2:4, 0:m]).then_inc(kv_copied, 1)
                dve.wait_ge(bias_prod, 1)
                dve.tensor_copy(bias[:], biasP[:, 0:2]).then_inc(bias_ready, 1)
                with dve.Fori(0, NB // 4) as i:
                    for half in range(2):
                        dve.wait_ge(cmp_prod, i * 2 + half + 1)
                        b = i * 4 + 2 * half
                        dve.tensor_copy(kcT[:, bass.ds(b, 2), 0:NCMP], kvP[:, half, 0:128].rearrange("p (a n) -> p a n", a=2)[:, :, 0:NCMP])
                        dve.tensor_copy(vc[:, bass.ds(b, 2), :], kvP[0:NCMP, half, 128:384].rearrange("p (a n) -> p a n", a=2)).then_inc(cmp_ready, 1)
                dve.wait_ge(cmp_prod, NB // 2 + 1)
                dve.tensor_copy(kcT[:, NB, 0:NCMP], kvP[:, 0, 0:NCMP])
                dve.tensor_copy(vc[:, NB, :], kvP[0:NCMP, 0, 128:256]).then_inc(cmp_ready, 1)


def stage_sample_attention(nc, T):
    NG, SG = 2, 4
    NK = PAGE * NPAGE
    VG = 18
    with ExitStack() as ctx:
        sb = lambda n, s, d=F32: ctx.enter_context(nc.sbuf_tensor(n, s, d))
        sem = lambda n: ctx.enter_context(nc.semaphore(n))
        qs = sb("qs", [P, NB, 2, NJ, NT])
        tab = sb("tab", [P, 1840])
        sel = sb("sel", [NS, 2, P])
        pages = sb("pages2", [1, NB * NPAGE], I32)
        kS = sb("kS", [P, SG, NPAGE, PAGE])
        vS = sb("vS", [P, SG, NPAGE, P])
        kW = sb("kW", [P, SG, WIN])
        vW = sb("vW", [P, SG, 4, P])
        sc = sb("sc", [P, 63 + 1056 + 544])
        pT = sb("pT", [P, 15, P])
        sm = sb("sm", [P, 64])
        gts = sb("gts", [NS, 24])
        g3 = sb("g3", [P, 3, H])
        imp_r = sb("imp_r", [P, 16])
        drop = sb("drop", [P, 3, 16])
        oz = sb("oz", [P, 2, HD])
        half_o = sb("half_o", [P, SG, NJ, NT])
        scoreP = ctx.enter_context(nc.psum_tensor("scoreP", [P, 4, 512], F32))
        ptP = ctx.enter_context(nc.psum_tensor("ptP", [P, 2, 512], F32))
        oP = ctx.enter_context(nc.psum_tensor("oP", [P, 512], F32))
        miscP = ctx.enter_context(nc.psum_tensor("miscP", [P, 512], F32))
        qs_zero, qs_ready, ld_t, ld_pg = sem("qs_zero"), sem("qs_ready"), sem("ld_tab"), sem("ld_pg2")
        ld_k, ld_v = sem("ld_k"), sem("ld_v")
        gate_sig, gate_row, cmp_s, sel_s = sem("gate_sig"), sem("gate_row"), sem("cmp_s"), sem("sel_s")
        v, e, pt_ready, pt_out, o_done, imp_p = sem("v"), sem("e"), sem("pt_ready"), sem("pt_out"), sem("o_done"), sem("imp_p")
        dve_step = sem("dve_step2")
        ident, kvt, kvT, kcT, vc, zaT = T["ident"], T["kvt"], T["kvT"], T["kcT"], T["vc"], T["zaT"]
        qTs = T["qT"]
        c_cmp, c_sel, c_win, c_new, c_map, c_agg, c_hm, c_io, c_m = 0, 63, 1087, 1599, 1663, 1679, 1807, 1815, 1831
        C, S0, S1, W0, W1 = 0, 63, 63 + 1024, 63 + 1056, 63 + 1056 + 512
        END = W1 + 32

        def load_pages(eng, G, dst, pool, loaded):
            with eng.Fori(0, SG * NPAGE) as i:
                page = eng.value_load(pages[0:1, bass.ds(i + G * SG * NPAGE, 1)], min_val=0, max_val=NPOOL - 1)
                eng.dma_start(dst[:].rearrange("p b n t -> p (b n) t")[:, bass.ds(i, 1), :], pool[bass.ds(page, 1)].rearrange("a p t -> p a t")).then_inc(loaded, 16)

        with nc.Block() as block:
            @block.sync
            def _(sp):
                sp.dma_start(pages[:], T["in"]["pages"]).then_inc(ld_pg, 16)
                sp.dma_start(sel[:], T["in"]["token_sel"]).then_inc(ld_t, 16)
                sp.dma_start(tab[:], T["in"]["sample_tab"]).then_inc(ld_t, 16)
                sp.wait_ge(ld_pg, 16)
                for G in range(NG):
                    if G:
                        sp.wait_ge(sel_s, 1)
                    load_pages(sp, G, kS, T["in"]["sel_k"], ld_k)
                    sp.dma_start(kW[:], T["in"]["win_k"][G].rearrange("p (b t) -> p b t", b=SG)).then_inc(ld_k, 16)
                sp.wait_ge(ld_t, 32)

            @block.gpsimd
            def _(po):
                po.memset(qs[:], 0.0).then_inc(qs_zero, 1)
                po.wait_ge(qs_zero, 1)
                for g in range(2):
                    r = slice(g * HD, (g + 1) * HD)
                    po.tensor_copy(qs[r, :, g].rearrange("p b j t -> p j b t"), qTs[r, :, SEQ:TOK].rearrange("p j (b t) -> p j b t", b=NB)).then_inc(qs_ready, 1)
                po.wait_ge(ld_pg, 16)
                for G in range(NG):
                    if G:
                        po.wait_ge(o_done, 1)
                    po.dma_start(vW[:], T["in"]["win_v"][G].rearrange("p (b n c) -> p b n c", b=SG, n=4)).then_inc(ld_v, 16)
                    load_pages(po, G, vS, T["in"]["sel_v"], ld_v)

            @block.tensor
            def _(pe):
                npt = 0
                pe.wait_ge(qs_ready, 2)
                pe.wait_ge(ld_t, 32)
                for G in range(NG):
                    lhs = lambda b: qs[:, G * SG + b].rearrange("p g j t -> p (g j t)")
                    lhs_all = qs[:, G * SG:(G + 1) * SG].rearrange("p b g j t -> p (b g j t)")
                    pe.wait_ge(gate_sig, 1)
                    pe.matmul(miscP[:, 0:24], sel[:, G, :], gts[:, :]).then_inc(gate_row, 1)
                    for b in range(SG):
                        pe.matmul(scoreP[32 * b:32 * b + 32, 0, 0:NCMP], lhs(b), kcT[:, G * SG + b, 0:NCMP])
                    pe.matmul(scoreP[:, 0, 64:96], lhs_all, kvT[:, 0, SEQ:TOK])
                    pe.matmul(scoreP[:, 0, 96:128], lhs_all, kvT[:, 1, SEQ:TOK]).then_inc(cmp_s, 1)
                    pe.wait_ge(ld_k, (G + 1) * 16 * (SG * NPAGE + 1))
                    for b in range(SG):
                        for n in range(2):
                            pe.matmul(scoreP[32 * b:32 * b + 32, 1 + n, :], lhs(b), kS[:, b, 4 * n:4 * n + 4, :].rearrange("p n t -> p (n t)"))
                        mm = pe.matmul(scoreP[32 * b:32 * b + 32, 3, :], lhs(b), kW[:, b, :])
                    mm.then_inc(sel_s, 1)
                    pe.wait_ge(v, VG * G + 3)
                    pe.transpose(ptP[0:NCMP, 0, 0:P], sc[:, C:C + NCMP], ident[:]).then_inc(pt_ready, 1)
                    pe.wait_ge(pt_out, 5 * G + 1)
                    for b in range(SG):
                        pe.matmul(oP[32 * b:32 * b + 32, 0:P], pT[0:NCMP, 0, 32 * b:32 * b + 32], vc[:, G * SG + b, :])
                    pe.matmul(miscP[:, 32:48], pT[0:NCMP, 0, :], tab[0:NCMP, c_map:c_map + 16]).then_inc(imp_p, 1)
                    pe.wait_ge(v, VG * G + 4)
                    pe.matmul(miscP[:, 64:80], tab[:, c_agg:c_agg + P], imp_r[:]).then_inc(imp_p, 1)
                    pe.wait_ge(e, 3 * G + 2)
                    for grp in range(2):
                        for n in range(4):
                            mm = pe.transpose(ptP[:, 1 - grp, n * P:(n + 1) * P], sc[:, S0 + (4 * grp + n) * P:S0 + (4 * grp + n + 1) * P], ident[:])
                        mm.then_inc(pt_ready, 1)
                    pe.wait_ge(pt_out, 5 * G + 2)
                    pe.wait_ge(e, 3 * G + 3)
                    for n in range(4):
                        mm = pe.transpose(ptP[:, 1, n * P:(n + 1) * P], sc[:, W0 + n * P:W0 + (n + 1) * P], ident[:])
                    mm.then_inc(pt_ready, 1)
                    pe.wait_ge(pt_out, 5 * G + 3)
                    pe.transpose(ptP[0:NS, 0, 0:P], sc[:, S1:S1 + NS], ident[:])
                    pe.transpose(ptP[0:NS, 0, P:2 * P], sc[:, W1:W1 + NS], ident[:]).then_inc(pt_ready, 1)
                    pe.wait_ge(pt_out, 5 * G + 5)
                    pe.wait_ge(ld_v, (G + 1) * 16 * (SG * NPAGE + 1))
                    for b in range(SG):
                        c = slice(32 * b, 32 * b + 32)
                        for n in range(8):
                            pe.matmul(oP[c, P:2 * P], pT[:, 1 + n, c], vS[:, b, n, :], start=(n == 0), stop=False, skip_group_check=True)
                        pe.matmul(oP[c, P:2 * P], pT[0:NS, 9, c], kvt[0:NS, QT, 3 * P:4 * P], start=False, stop=True, skip_group_check=True)
                        for n in range(4):
                            pe.matmul(oP[c, 2 * P:3 * P], pT[:, 10 + n, c], vW[:, b, n, :], start=(n == 0), stop=False, skip_group_check=True)
                        mm = pe.matmul(oP[c, 2 * P:3 * P], pT[0:NS, 14, c], kvt[0:NS, QT, 5 * P:6 * P], start=False, stop=True, skip_group_check=True)
                    mm.then_inc(o_done, 1)
                    pe.wait_ge(v, VG * G + 17)
                    pe.transpose(miscP[:, P:2 * P], oz[:].rearrange("p g d -> p (g d)"), ident[:]).then_inc(o_done, 1)
                    pe.wait_ge(v, VG * G + 18)

            @block.scalar
            def _(act):
                act.activation(gts[:], kvt[0:NS, QT, 6 * P:6 * P + 24], ACT.Sigmoid).then_inc(gate_sig, 1)
                for G in range(NG):
                    act.wait_ge(v, VG * G + 1)
                    act.activation(sc[:, C:C + NCMP], sc[:, C:C + NCMP], ACT.Exp, bias=sm[:, 0:1], accum_out=sm[:, 1:2]).then_inc(e, 1)
                    act.wait_ge(v, VG * G + 5)
                    act.activation(sc[:, S0:W0], sc[:, S0:W0], ACT.Exp, bias=sm[:, 2:3], accum_out=sm[:, 3:4]).then_inc(e, 1)
                    act.wait_ge(v, VG * G + 6)
                    act.activation(sc[:, W0:END], sc[:, W0:END], ACT.Exp, bias=sm[:, 4:5], accum_out=sm[:, 5:6]).then_inc(e, 1)
                    for k, (m, dst, src) in enumerate([
                            (P, pT[:, 1:5, :], ptP[:, 1, :].rearrange("p (n t) -> p n t", n=4)),
                            (P, pT[:, 5:9, :], ptP[:, 0, :].rearrange("p (n t) -> p n t", n=4)),
                            (P, pT[:, 10:14, :], ptP[:, 1, :].rearrange("p (n t) -> p n t", n=4)),
                            (NS, pT[0:NS, 9:15:5, :], ptP[0:NS, 0, 0:2 * P].rearrange("p (n t) -> p n t", n=2))]):
                        act.wait_ge(pt_ready, 5 * G + 2 + k)
                        act.activation(dst, src, ACT.Copy).then_inc(pt_out, 1)

            @block.vector
            def _(dve):
                linked = [0]
                def link(ins, wait=True):
                    ins.then_inc(dve_step, 1)
                    linked[0] += 1
                    if wait:
                        dve.wait_ge(dve_step, linked[0])
                dve.wait_ge(ld_t, 32)
                for G in range(NG):
                    n_v = [VG * G]
                    def done(ins):
                        ins.then_inc(v, 1)
                        n_v[0] += 1
                    def settle():
                        dve.wait_ge(v, n_v[0])
                    dve.wait_ge(cmp_s, G + 1)
                    dve.wait_ge(gate_row, G + 1)
                    link(dve.tensor_tensor(sc[:, C:C + NCMP], scoreP[:, 0, 0:NCMP], tab[:, c_cmp:c_cmp + NCMP], ALU.add))
                    done(dve.tensor_reduce(sm[:, 0:1], sc[:, C:C + NCMP], AX, ALU.max, negate=True))
                    link(dve.tensor_tensor(g3[:], miscP[:, 0:24].rearrange("p (h c) -> p c h", c=3), tab[:, c_hm:c_hm + H].unsqueeze(1).to_broadcast([P, 3, H]), ALU.mult))
                    link(dve.tensor_reduce(sm[:, 10:13], g3[:], AX, ALU.add))
                    dve.wait_ge(e, 3 * G + 1)
                    done(dve.reciprocal(sm[:, 6:7], sm[:, 1:2]))
                    settle()
                    link(dve.tensor_scalar(sc[:, C:C + NCMP], sc[:, C:C + NCMP], sm[:, 6:7], None, ALU.mult))
                    done(dve.scalar_tensor_tensor(sc[:, C:C + NCMP], sc[:, C:C + NCMP], TINY, sc[:, C:C + NCMP], ALU.is_ge, ALU.mult))
                    dve.wait_ge(pt_ready, 5 * G + 1)
                    dve.tensor_copy(pT[0:NCMP, 0, :], ptP[0:NCMP, 0, 0:P]).then_inc(pt_out, 1)
                    dve.wait_ge(imp_p, 2 * G + 1)
                    done(dve.tensor_copy(imp_r[:], miscP[:, 32:48]))
                    dve.wait_ge(imp_p, 2 * G + 2)
                    imp = miscP[:, 65:79]
                    link(dve.tensor_reduce(sm[:, 7:8], imp, AX, ALU.min))
                    link(dve.scalar_tensor_tensor(drop[:, 0, 0:14], imp, sm[:, 7:8], tab[:, c_io + 1:c_io + 15], ALU.is_equal, ALU.mult))
                    link(dve.tensor_reduce(sm[:, 8:9], drop[:, 0, 0:14], AX, ALU.max))
                    link(dve.tensor_scalar(drop[:, 1, :], tab[:, c_io:c_io + 16], sm[:, 8:9], NEG, ALU.is_equal, ALU.mult))
                    dve.wait_ge(sel_s, G + 1)
                    link(dve.tensor_tensor(sc[:, S0:S1].rearrange("p (b n) -> p b n", b=2), scoreP[:, 1:3, :], tab[:, c_sel:c_sel + NK].rearrange("p (b n) -> p b n", b=2), ALU.add), wait=False)
                    link(dve.tensor_tensor(sc[:, S1:W0], scoreP[:, 0, 64:96], tab[:, c_new + 32 * G:c_new + 32 * G + 32], ALU.add))
                    s3 = sc[:, S0:S1].rearrange("p (b n) -> p b n", b=16)
                    link(dve.tensor_tensor(s3, s3, drop[:, 1, :].unsqueeze(2).to_broadcast([P, 16, 64]), ALU.add))
                    done(dve.tensor_reduce(sm[:, 2:3], sc[:, S0:W0], AX, ALU.max, negate=True))
                    link(dve.tensor_tensor(sc[:, W0:W1], scoreP[:, 3, :], tab[:, c_win:c_win + WIN], ALU.add), wait=False)
                    link(dve.tensor_tensor(sc[:, W1:END], scoreP[:, 0, 96:128], tab[:, c_new + 32 * G:c_new + 32 * G + 32], ALU.add))
                    done(dve.tensor_reduce(sm[:, 4:5], sc[:, W0:END], AX, ALU.max, negate=True))
                    dve.wait_ge(e, 3 * G + 3)
                    done(dve.reciprocal(sm[:, 13:14], sm[:, 3:4]))
                    done(dve.reciprocal(sm[:, 14:15], sm[:, 5:6]))
                    settle()
                    done(dve.tensor_tensor(sm[:, 11:13], sm[:, 11:13], sm[:, 13:15], ALU.mult))
                    settle()
                    done(dve.tensor_scalar(sm[:, 16:19], sm[:, 10:13], tab[:, c_m:c_m + 1], None, ALU.mult))
                    done(dve.tensor_scalar(sm[:, 19:22], sm[:, 10:13], tab[:, c_m + 1:c_m + 2], None, ALU.mult))
                    settle()
                    dve.wait_ge(o_done, 2 * G + 1)
                    for c in range(3):
                        for g in range(2):
                            src, k = oP[:, c * P + g * HD:c * P + (g + 1) * HD], sm[:, 16 + 3 * g + c:17 + 3 * g + c]
                            if c == 0:
                                done(dve.tensor_scalar(oz[:, g, :], src, k, None, ALU.mult))
                            else:
                                done(dve.scalar_tensor_tensor(oz[:, g, :], src, k, oz[:, g, :], ALU.mult, ALU.add))
                        if c < 2:
                            settle()
                    dve.wait_ge(o_done, 2 * G + 2)
                    ot = miscP[:, P:2 * P].rearrange("p (b g j t) -> p g b j t", b=SG, g=2, j=NJ)
                    link(dve.tensor_copy(half_o[:], ot[:, 0]))
                    link(dve.tensor_tensor(half_o[:], half_o[:], ot[:, 1], ALU.add))
                    zs = zaT[:, :, SEQ + G * SG * NT:SEQ + (G + 1) * SG * NT].rearrange("p j (b t) -> p b j t", b=SG)
                    done(dve.tensor_tensor(zs, zs, half_o[:], ALU.mult))
                    assert n_v[0] == VG * (G + 1)
                    settle()


def stage_prompt_attention(nc, T):
    NPAIR = 2
    UN = 4 * NPAIR
    W_MAX = WIN + P

    def width(i):
        return min((i + 1) * P, W_MAX)

    def slots(i, kind):
        if kind == 0:
            return [(0, n * P, P, n) for n in range(i + 1)]
        k0 = (i + 1) - width(i) // P
        return [(1, n * P, P, k0 + n) for n in range(width(i) // P)] + [(2, W_MAX, NCMP, None)]

    def groups(i, kind):
        s = slots(i, kind)
        cut = 3 if len(s) == 5 and kind else 4
        return [x for x in (s[:cut], s[cut:8], s[8:]) if x]

    def each_step(eng, i, body):
        if i == 0:
            for s in range(2):
                body(s)
        else:
            with eng.Fori(0, 2) as s:
                body(s)

    def wait(eng, sem, count):
        if not isinstance(count, int) or count > 0:
            eng.wait_ge(sem, count)

    unit_kind = [0, 1, 0, 1] * NPAIR
    unit_g = [0, 0, 1, 1] * NPAIR
    NH = 2 * NPAIR
    with ExitStack() as ctx:
        sb = lambda n, s, d=F32: ctx.enter_context(nc.sbuf_tensor(n, s, d))
        sem = lambda n: ctx.enter_context(nc.semaphore(n))
        dist = sb("dist", [P, SEQ])
        dist_w = sb("dist_w", [P, P])
        dist_c = sb("dist_c", [P, QT, 64])
        slope = sb("slope", [P, H])
        gates = sb("gates", [P, QT, NJ, 2, 3])
        qb = [sb(f"qb{i}", [P, P]) for i in range(NH)]
        ss = [sb(f"ss{i}", [P, SEQ]) for i in range(4)]
        pT = [sb(f"ppT{i}", [P, 4, P]) for i in range(4)]
        nm = sb("nm", [P, 4, 2])
        sums = [sb(f"sums{i}", [P, 3]) for i in range(NH)]
        coef = sb("coef", [P, 3])
        tmp = sb("otmp", [P, 3, HD])
        ot = sb("ot", [P, NJ, P])
        sP = [ctx.enter_context(nc.psum_tensor(f"sP{i}", [P, 2, 512], F32)) for i in range(2)]
        tP = ctx.enter_context(nc.psum_tensor("tP", [P, 2, 512], F32))
        oP = ctx.enter_context(nc.psum_tensor("poP", [P, 2, 512], F32))
        ld_t, gate_ready, q_ready = sem("ld_d"), sem("gate_ready"), sem("q_ready")
        q_zero = sem("q_zero")
        score_prod, score_read, max_ready, p_ready = sem("score_prod"), sem("score_read"), sem("max_ready"), sem("p_ready")
        pt_ready, pt_out, pv_done = sem("ppt_ready"), sem("ppt_out"), sem("pv_done")
        o_read, o_ready, o_turned, z_done, dve_step = sem("o_read"), sem("o_ready"), sem("o_turned"), sem("z_done"), sem("dve_step3")
        kvt, kvT, kcT, vc, qT, zaT, ident = T["kvt"], T["kvT"], T["kcT"], T["vc"], T["qT"], T["zaT"], T["ident"]
        NPT = [sum(len(groups(i, k)) for k in unit_kind) for i in range(QT)]
        G0 = [2 * sum(NPT[:i]) for i in range(QT)]
        U0 = [2 * UN * i for i in range(QT)]

        with nc.Block() as block:
            @block.sync
            def _(sp):
                sp.dma_start(dist[:], T["in"]["dist"]).then_inc(ld_t, 16)
                sp.dma_start(dist_w[:], T["in"]["dist_w"]).then_inc(ld_t, 16)
                sp.dma_start(dist_c[:], T["in"]["dist_c"]).then_inc(ld_t, 16)
                sp.dma_start(slope[:], T["in"]["slope"]).then_inc(ld_t, 16)
                sp.wait_ge(ld_t, 64)

            @block.gpsimd
            def _(po):
                for q in qb:
                    x = po.memset(q[:], 0.0)
                x.then_inc(q_zero, 1)
                po.wait_ge(q_zero, 1)
                for i in range(QT):
                    def body(s, i=i):
                        for j in range(NPAIR):
                            wait(po, score_prod, s * UN + (U0[i] - UN + 4 * j + 4))
                            for g in range(2):
                                r = slice(g * HD, (g + 1) * HD)
                                x = po.tensor_copy(qb[2 * j + g][r, :], qT[r, bass.ds(s * NPAIR + j, 1), i * P:(i + 1) * P])
                            x.then_inc(q_ready, 1)
                    each_step(po, i, body)

            @block.tensor
            def _(pe):
                for i in range(QT):
                    def body(s, i=i):
                        def at(base):
                            return s * UN + base

                        def scores(u):
                            g, j, dst = unit_g[u], u // 4, sP[u % 2]
                            if u % 4 == 0:
                                pe.wait_ge(q_ready, s * NPAIR + 2 * NPAIR * i + j + 1)
                            wait(pe, score_read, at(U0[i] + u - 1))
                            n = (i + 1) * P if unit_kind[u] == 0 else width(i)
                            k0 = (i + 1) * P - n
                            for c in range(0, n, 512):
                                m = min(512, n - c)
                                mm = pe.matmul(dst[:, c // 512, 0:m], qb[2 * j + g][:], kvT[:, unit_kind[u], k0 + c:k0 + c + m])
                            if unit_kind[u]:
                                mm = pe.matmul(dst[:, 1, P:P + NCMP], qb[2 * j + g][:], kcT[:, NB, 0:NCMP])
                            mm.then_inc(score_prod, 1)

                        flat = [(u, n, grp) for u in range(UN) for n, grp in enumerate(groups(i, unit_kind[u]))]

                        def turn(k):
                            u, n, grp = flat[k]
                            if n == 0:
                                pe.wait_ge(p_ready, at(U0[i] + u + 1))
                            wait(pe, pt_out, s * NPT[i] + (G0[i] + k - 1))
                            for m, (_, c, keys, _) in enumerate(grp):
                                mm = pe.transpose(tP[0:keys, k % 2, m * P:(m + 1) * P], ss[u % 4][:, c:c + keys], ident[:])
                            mm.then_inc(pt_ready, 1)

                        def values(k):
                            u, n, grp = flat[k]
                            g, j = unit_g[u], u // 4
                            pe.wait_ge(pt_out, s * NPT[i] + (G0[i] + k + 1))
                            if u % 2 == 0 and n == 0:
                                wait(pe, o_read, s * NH + (2 * NH * i + 2 * j + g - 1))
                                if u == 0:
                                    wait(pe, z_done, i)
                            for m, (br, c, keys, tile) in enumerate(grp):
                                v = vc[:, NB, :] if br == 2 else kvt[:, tile, (3 + 2 * br) * P:(4 + 2 * br) * P]
                                first = br == 2 or c == 0
                                last = br == 2 or c == ((i + 1) * P if br == 0 else width(i)) - P
                                mm = pe.matmul(oP[:, g, br * P:(br + 1) * P], pT[k % 4][0:keys, m, :], v, start=first, stop=last)
                            mm.then_inc(pv_done, 1)

                        scores(0)
                        scores(1)
                        for k, (u, n, grp) in enumerate(flat):
                            if n == 0 and u + 2 < UN:
                                scores(u + 2)
                            turn(k)
                            if k:
                                values(k - 1)
                        values(len(flat) - 1)
                    each_step(pe, i, body)
                    pe.wait_ge(o_ready, H * (i + 1))
                    for j in range(NJ):
                        mm = pe.transpose(oP[:, 0, j * P:(j + 1) * P], ot[:, j, :], ident[:])
                    mm.then_inc(o_turned, 1)
                pe.wait_ge(z_done, QT)

            @block.scalar
            def _(act):
                for i in range(QT):
                    src = kvt[:, i, 6 * P:6 * P + 24].rearrange("p (g j c) -> p g j c", g=2, j=NJ)
                    dst = gates[:, i].rearrange("p j g c -> p g j c")
                    act.activation(dst[:, :, :, 2], src[:, :, :, 0], ACT.Sigmoid)
                    act.activation(dst[:, :, :, 0:2], src[:, :, :, 1:3], ACT.Sigmoid).then_inc(gate_ready, 1)
                for i in range(QT):
                    def body(s, i=i):
                        def exps(u):
                            g, j = unit_g[u], u // 4
                            act.wait_ge(max_ready, s * UN + (U0[i] + u + 1))
                            n = (i + 1) * P if unit_kind[u] == 0 else width(i)
                            b = unit_kind[u]
                            x = act.activation(ss[u % 4][:, 0:n], ss[u % 4][:, 0:n], ACT.Exp, bias=nm[:, u % 4, 0:1], accum_out=sums[2 * j + g][:, b:b + 1])
                            if b:
                                c = slice(W_MAX, W_MAX + NCMP)
                                x = act.activation(ss[u % 4][:, c], ss[u % 4][:, c], ACT.Exp, bias=nm[:, u % 4, 1:2], accum_out=sums[2 * j + g][:, 2:3])
                            x.then_inc(p_ready, 1)

                        exps(0)
                        k = 0
                        for u in range(UN):
                            if u + 1 < UN:
                                exps(u + 1)
                            for grp in groups(i, unit_kind[u]):
                                act.wait_ge(pt_ready, s * NPT[i] + (G0[i] + k + 1))
                                wait(act, pv_done, s * NPT[i] + (G0[i] + k - 3))
                                full = [x for x in grp if x[0] != 2]
                                if full:
                                    x = act.activation(pT[k % 4][:, 0:len(full), :], tP[:, k % 2, 0:len(full) * P].rearrange("p (n t) -> p n t", t=P), ACT.Copy)
                                if len(full) < len(grp):
                                    m = len(full)
                                    x = act.activation(pT[k % 4][0:NCMP, m, :], tP[0:NCMP, k % 2, m * P:(m + 1) * P], ACT.Copy)
                                x.then_inc(pt_out, 1)
                                k += 1
                    each_step(act, i, body)

            @block.vector
            def _(dve):
                LN = UN // 2 + 3 * NH
                ends = lambda i: [sum(len(groups(i, unit_kind[u])) for u in range(n + 1)) for n in range(UN)]
                dve.wait_ge(ld_t, 64)
                dve.wait_ge(gate_ready, QT)
                for i in range(QT):
                    def body(s, i=i):
                        linked = [0]

                        def link(ins, wait=True):
                            linked[0] += 1
                            ins.then_inc(dve_step, 1)
                            if wait:
                                dve.wait_ge(dve_step, s * LN + (2 * LN * i + linked[0]))

                        def biased(u):
                            g, j, src, dst = unit_g[u], u // 4, sP[u % 2], ss[u % 4]
                            U = U0[i] + u
                            dve.wait_ge(score_prod, s * UN + (U + 1))
                            if u >= 4:
                                wait(dve, pt_ready, s * NPT[i] + (G0[i] + ends(i)[u - 4]))
                            elif i == 0:
                                wait(dve, pt_ready, s * ends(i)[u + 4])
                            else:
                                gone = G0[i] - NPT[i - 1] + ends(i - 1)[u + 4]
                                dve.wait_ge(pt_ready, s * (G0[i] + ends(i)[u + 4] - gone) + gone)
                            k = slope[:, bass.ds(s * (2 * NPAIR) + (2 * j + g), 1)]
                            n = (i + 1) * P if unit_kind[u] == 0 else width(i)
                            flat = src[:].rearrange("p a b -> p (a b)")
                            first = P if unit_kind[u] and i >= 4 else 0
                            if first:
                                dve.scalar_tensor_tensor(dst[:, 0:P], dist_w[:], k, flat[:, 0:P], ALU.mult, ALU.add)
                            if unit_kind[u]:
                                dve.scalar_tensor_tensor(dst[:, W_MAX:W_MAX + NCMP], dist_c[:, i, 0:NCMP], k, flat[:, W_MAX:W_MAX + NCMP], ALU.mult, ALU.add)
                            dve.scalar_tensor_tensor(dst[:, first:n], dist[:, SEQ - n + first:SEQ], k, flat[:, first:n], ALU.mult, ALU.add).then_inc(score_read, 1)
                            dve.wait_ge(score_read, s * UN + (U + 1))
                            if unit_kind[u]:
                                link(dve.tensor_reduce(nm[:, u % 4, 1:2], dst[:, W_MAX:W_MAX + NCMP], AX, ALU.max, negate=True))
                                dve.tensor_scalar(nm[:, u % 4, 1:2], nm[:, u % 4, 1:2], GUARD, None, ALU.min)
                            dve.tensor_reduce(nm[:, u % 4, 0:1], dst[:, 0:n], AX, ALU.max, negate=True).then_inc(max_ready, 1)

                        def combine(h):
                            j, g = h // 2, h % 2
                            last = sum(len(groups(i, unit_kind[u])) for u in range(2 * h + 2))
                            dve.wait_ge(pv_done, s * NPT[i] + (G0[i] + last))
                            link(dve.tensor_scalar(coef[:], sums[h][:], 1e-30, None, ALU.max))
                            link(dve.reciprocal(coef[:], coef[:]))
                            link(dve.tensor_tensor(coef[:], coef[:], gates[:, i].rearrange("p j g c -> p (j g) c")[:, bass.ds(s * NH + h, 1), :].rearrange("p a c -> p (a c)"), ALU.mult))
                            o = oP[:, g, 0:3 * P].rearrange("p (c d) -> p c d", d=P)[:, :, g * HD:(g + 1) * HD]
                            dve.tensor_tensor(tmp[:], o, coef[:].unsqueeze(2).to_broadcast([P, 3, HD]), ALU.mult).then_inc(o_read, 1)
                            dve.wait_ge(o_read, s * NH + (2 * NH * i + h + 1))
                            dve.tensor_reduce(ot[:, bass.ds(s * NPAIR + j, 1), g * HD:(g + 1) * HD].rearrange("p a d -> p (a d)"), tmp[:].rearrange("p b d -> p d b"), AX, ALU.add).then_inc(o_ready, 1)

                        for u in range(UN):
                            biased(u)
                            if u >= 4 and u % 2 == 0:
                                combine((u - 4) // 2)
                        combine(NH - 2)
                        combine(NH - 1)
                        assert linked[0] == LN
                    each_step(dve, i, body)
                    dve.wait_ge(o_turned, i + 1)
                    z = zaT[:, :, i * P:(i + 1) * P]
                    dve.tensor_tensor(z, z, oP[:, 0, :].rearrange("p (j t) -> p j t", j=NJ), ALU.mult).then_inc(z_done, 1)


def stage_gdn_project(nc, T):
    with ExitStack() as ctx:
        sb = lambda n, s, d=F32: ctx.enter_context(nc.sbuf_tensor(n, s, d))
        sem = lambda n: ctx.enter_context(nc.semaphore(n))
        w = [sb(f"gw{i}", [P, KT, 256]) for i in range(2)]
        raw = [sb(f"raw{i}", [P, CW]) for i in range(2)]
        st = sb("cst", [P, 12, NB, 3])
        cwt = sb("cwt", [P, 12, 5])
        tail = sb("ctail", [P, 12, 3 + 3 * NB])
        fP = [ctx.enter_context(nc.psum_tensor(f"gfP{i}", [P, 3, 512], F32)) for i in range(2)]
        ld_w = [sem(f"gld_w{i}") for i in range(2)]
        ld_c, prod, raw_ready, st_ready = sem("gld_c"), sem("gprod"), sem("raw_ready"), sem("gst_ready")
        taps, conv_ready, tail_ready, st_out = sem("taps"), sem("conv_ready"), sem("tail_ready"), sem("gst_out")
        hT, uT = T["hT"], T["uT"]
        NF = 12
        samples = lambda r: r[:, SEQ + 3:CW].rearrange("p (b t) -> p b t", b=NB)

        with nc.Block() as block:
            @block.sync
            def _(sp):
                sp.dma_start(st[:], T["in"]["conv_state"]).then_inc(ld_c, 16)
                sp.dma_start(cwt[:], T["in"]["conv_w"]).then_inc(ld_c, 16)
                for n in range(NF // 2):
                    if n >= 2:
                        sp.wait_ge(prod, 2 * (n - 1))
                    sp.dma_start(w[n % 2][:], T["in"]["w_feat"][4 + n].rearrange("p (k n) -> p k n", k=KT)).then_inc(ld_w[n % 2], 16)
                sp.wait_ge(tail_ready, NF)
                sp.dma_start(T["out"]["conv_p"], tail[:, :, 0:3]).then_inc(st_out, 16)
                sp.dma_start(T["out"]["conv_s"], tail[:, :, 3:].rearrange("p f (b t) -> p f b t", b=NB)).then_inc(st_out, 16)
                sp.wait_ge(st_out, 32)

            @block.tensor
            def _(pe):
                for f in range(NF):
                    if f % 2 == 0:
                        pe.wait_ge(ld_w[f // 2 % 2], 16 * (f // 4 + 1))
                    if f >= 2:
                        pe.wait_ge(raw_ready, f - 1)
                    product_features(pe, fP[f % 2], w[f // 2 % 2], hT, f % 2).then_inc(prod, 1)

            @block.gpsimd
            def _(po):
                for r in raw:
                    po.memset(r[:, 0:3], 0.0)
                po.wait_ge(ld_c, 32)
                for f in range(NF):
                    if f >= 2:
                        po.wait_ge(conv_ready, f - 1)
                    po.tensor_copy(samples(raw[f % 2])[:, :, 0:3], st[:, f]).then_inc(st_ready, 1)
                    po.wait_ge(raw_ready, f + 1)
                    po.tensor_copy(tail[:, f, 0:3], raw[f % 2][:, SEQ:SEQ + 3])
                    po.tensor_copy(tail[:, f, 3:].rearrange("p (b t) -> p b t", b=NB), samples(raw[f % 2])[:, :, 4:7]).then_inc(tail_ready, 1)

            @block.scalar
            def _(act):
                def silu(f):
                    act.wait_ge(conv_ready, f + 1)
                    act.activation(uT[:, f, :], uT[:, f, :], ACT.Silu)
                for f in range(NF):
                    act.wait_ge(prod, f + 1)
                    if f >= 2:
                        act.wait_ge(conv_ready, f - 1)
                        act.wait_ge(tail_ready, f - 1)
                    r, p = raw[f % 2], fP[f % 2]
                    act.activation(r[:, 3:3 + 2 * TB].rearrange("p (b t) -> p b t", b=2), p[:, 0:2, 0:TB], ACT.Copy)
                    act.activation(r[:, 3 + 2 * TB:3 + SEQ], p[:, 2, 0:SEQ - 2 * TB], ACT.Copy)
                    act.activation(samples(r)[:, :, 3:7], p[:, 2, SEQ - 2 * TB:TB].rearrange("p (b t) -> p b t", b=NB), ACT.Copy).then_inc(raw_ready, 1)
                    if f:
                        silu(f - 1)
                silu(NF - 1)

            @block.vector
            def _(dve):
                dve.wait_ge(ld_c, 32)
                for f in range(NF):
                    dve.wait_ge(raw_ready, f + 1)
                    dve.wait_ge(st_ready, f + 1)
                    r, o = raw[f % 2], uT[:, f, :]
                    so, sr = o[:, SEQ:TOK].rearrange("p (b t) -> p b t", b=NB), samples(r)
                    for i in range(4):
                        if i == 0:
                            dve.tensor_scalar(o[:, 0:SEQ], r[:, 0:SEQ], cwt[:, f, 0:1], cwt[:, f, 4:5], ALU.mult, ALU.add)
                            x = dve.tensor_scalar(so, sr[:, :, 0:4], cwt[:, f, 0:1], cwt[:, f, 4:5], ALU.mult, ALU.add)
                        else:
                            k = cwt[:, f, i:i + 1]
                            dve.scalar_tensor_tensor(o[:, 0:SEQ], r[:, i:SEQ + i], k, o[:, 0:SEQ], ALU.mult, ALU.add)
                            x = dve.scalar_tensor_tensor(so, sr[:, :, i:i + 4], k, so, ALU.mult, ALU.add)
                        if i < 3:
                            x.then_inc(taps, 1)
                            dve.wait_ge(taps, 3 * f + i + 1)
                    x.then_inc(conv_ready, 1)


def stage_gdn_tokens(nc, T):
    with ExitStack() as ctx:
        sb = lambda n, s, d=F32: ctx.enter_context(nc.sbuf_tensor(n, s, d))
        sem = lambda n: ctx.enter_context(nc.semaphore(n))
        NTI = QT + 1
        sq = [sb(f"gsq{i}", [P, 2, 512]) for i in range(2)]
        ss = sb("gss", [P, NTI, 16])
        ab = sb("gab", [P, 2, H])
        ga = sb("ga", [P, 3, NTI, H])
        qP = [ctx.enter_context(nc.psum_tensor(f"gqP{i}", [P, 3, 512], F32)) for i in range(2)]
        ld, turned, copied, sq_ready, ss_ready, rt_ready = sem("gld"), sem("gturned"), sem("gcopied"), sem("gsq_ready"), sem("gss_ready"), sem("grt_ready")
        e, step, clear = sem("ge"), sem("gstep"), sem("gclear")
        uT, ident, qkv, ab_t = T["uT"], T["ident"], T["qkv"], T["ab_t"]
        rows = lambda t: P if t < QT else NS

        with nc.Block() as block:
            @block.sync
            def _(sp):
                sp.dma_start(ab[:], T["in"]["gdn_ab"]).then_inc(ld, 16)
                sp.wait_ge(ld, 16)

            @block.tensor
            def _(pe):
                for t in range(NTI):
                    m = rows(t)
                    if t >= 2:
                        pe.wait_ge(copied, t - 1)
                    for f in range(12):
                        mm = pe.transpose(qP[t % 2][0:m, f // 4, f % 4 * P:(f % 4 + 1) * P], uT[:, f, t * P:t * P + m], ident[:])
                    mm.then_inc(turned, 1)

            @block.scalar
            def _(act):
                for t in range(NTI):
                    m = rows(t)
                    act.wait_ge(copied, t + 1)
                    if t >= 2:
                        act.wait_ge(ss_ready, t - 1)
                    act.activation(sq[t % 2][0:m], qkv[0:m, t, 0:2], ACT.Square).then_inc(sq_ready, 1)
                act.wait_ge(step, 2)
                act.activation(ss[:], ss[:], ACT.Sqrt).then_inc(rt_ready, 1)
                act.wait_ge(ld, 16)
                act.activation(ab_t[:, :, H:2 * H], ab_t[:, :, H:2 * H], ACT.Sigmoid).then_inc(e, 1)
                act.activation(ab[:, 1, :], ab[:, 1, :], ACT.Exp).then_inc(e, 1)
                act.wait_ge(step, 3)
                act.activation(ga[:, 1], ga[:, 0], ACT.Abs).then_inc(e, 1)
                act.wait_ge(e, 3)
                act.activation(ga[:, 1], ga[:, 1], ACT.Exp, scale=-1.0).then_inc(e, 1)
                act.wait_ge(step, 4)
                act.activation(ga[:, 1], ga[:, 1], ACT.Ln).then_inc(e, 1)

            @block.vector
            def _(dve):
                dve.memset(ss[:], 1.0).then_inc(clear, 1)
                dve.wait_ge(clear, 1)
                for t in range(NTI):
                    m = rows(t)
                    dve.wait_ge(turned, t + 1)
                    dve.tensor_copy(qkv[0:m, t], qP[t % 2][0:m]).then_inc(copied, 1)
                    dve.wait_ge(sq_ready, t + 1)
                    dve.tensor_reduce(ss[0:m, t, :], sq[t % 2][0:m].rearrange("p a (h d) -> p (a h) d", d=HD), AX, ALU.add).then_inc(ss_ready, 1)
                dve.wait_ge(ss_ready, NTI)
                dve.tensor_scalar(ss[:], ss[:], EPS, None, ALU.add).then_inc(step, 1)
                dve.wait_ge(step, 1)
                dve.reciprocal(ss[:], ss[:]).then_inc(step, 1)
                dve.wait_ge(ld, 16)
                dve.tensor_tensor(ga[:, 0], ab_t[:, :, 0:H], ab[:, 0, :].unsqueeze(1).to_broadcast([P, NTI, H]), ALU.add).then_inc(step, 1)
                dve.wait_ge(e, 4)
                dve.tensor_scalar(ga[:, 1], ga[:, 1], 1.0, None, ALU.add).then_inc(step, 1)
                dve.tensor_scalar(ga[:, 2], ga[:, 0], 0.0, None, ALU.max).then_inc(step, 1)
                dve.wait_ge(e, 5)
                dve.wait_ge(step, 5)
                dve.tensor_tensor(ga[:, 2], ga[:, 2], ga[:, 1], ALU.add).then_inc(step, 1)
                dve.wait_ge(step, 6)
                dve.scalar_tensor_tensor(ab_t[:, :, 0:H], ga[:, 2], -1.0, ab[:, 1, :].unsqueeze(1).to_broadcast([P, NTI, H]), ALU.mult, ALU.mult)
                dve.wait_ge(rt_ready, 1)
                dve.tensor_scalar(ss[:, :, 0:H], ss[:, :, 0:H], HD ** -0.5, None, ALU.mult).then_inc(step, 1)
                dve.wait_ge(step, 7)
                for t in range(NTI):
                    m = rows(t)
                    x = qkv[0:m, t, 0:2].rearrange("p a (h d) -> p (a h) d", d=HD)
                    dve.tensor_tensor(x, x, ss[0:m, t].unsqueeze(2).to_broadcast([m, 16, HD]), ALU.mult)


def stage_gdn_scan(nc, T):
    with ExitStack() as ctx:
        sb = lambda n, s, d=F32: ctx.enter_context(nc.sbuf_tensor(n, s, d))
        sem = lambda n: ctx.enter_context(nc.semaphore(n))
        ps = lambda n, b: ctx.enter_context(nc.psum_tensor(n, [P, b, 512], F32))
        NTI = QT + 1
        tri = sb("tri", [P, 2, P])
        tot = sb("tot", [NS, P])
        seq = sb("seq", [NS, NB])
        msk = sb("msk", [P, P + NS])
        lvl = sb("lvl", [P, 7, P])
        src = sb("src", [P, 2, 512])
        ags = sb("ags", [P, 16])
        gst = sb("gst", [P, NTI, 3, H])
        gex = sb("gex", [P, NTI, 3, H])
        egc = sb("egc", [P, H])
        dec = sb("dec", [P, H, P])
        kb = sb("kb", [P, 4, 512])
        vb = sb("vb", [P, 512])
        kz = sb("kz", [P, H, P])
        kq = sb("kq", [P, NJ, 2, P])
        ke = sb("ke", [P, 2, NJ, P])
        lt = sb("lt", [P, H, P])
        at = sb("at", [P, H, P])
        x = sb("x", [P, H, P])
        xt = sb("xt", [P, H, P])
        yy = sb("yy", [P, H, P])
        vz = sb("vz", [P, NJ * 256 + P])
        r = sb("r", [P, 512])
        S = sb("S", [P, NJ, P])
        SS = sb("SS", [P, NJ, NB, P])
        eglS = sb("eglS", [P, NJ, NB])
        A, Bk = ps("psA", 4), ps("psB", 4)
        ld, clear, st_out = sem("sld"), sem("sclear"), sem("sst_out")
        g_prod, g_read, exp_ready = sem("g_prod"), sem("g_read"), sem("exp_ready")
        src_ready, scaled, scaled_late = sem("src_ready"), sem("scaled"), sem("scaled_late")
        row_prod, dec_part, dec_in, dec_ready = sem("row_prod"), sem("dec_part"), sem("dec_in"), sem("dec_ready")
        t_done, t_out, kk_done, lt_part, xt_part, lt_ready = (sem(n) for n in ("t_done", "t_out", "kk_done", "lt_part", "xt_part", "lt_ready"))
        mm_done, xt_out, dv_out, chain_mm, chain_ev, s_part = (sem(n) for n in ("mm_done", "xt_out", "dv_out", "chain_mm", "chain_ev", "s_part"))
        step, og_out, state_done, tile_done = sem("sstep"), sem("og_out"), sem("state_done"), sem("tile_done")
        qkv, ab_t, ident, ones, og = T["qkv"], T["ab_t"], T["ident"], T["ones"], T["og"]
        pair_rows = [slice(0, HD), slice(HD, P)]
        heads3 = lambda ap: ap.rearrange("p (h d) -> p h d", d=HD)
        one = lambda ap: ap.rearrange("p a h -> p (a h)")

        NL = 6

        def levels_of(smp):
            return 1 if smp else NL

        def count(t, per, n, ahead=0):
            return t * per + (ahead * per + n)

        def tiles(eng, prepare, body):
            prepare(0, 0, 0, P)
            body(0, 0, P, 0, P)
            with eng.Fori(1, QT - 1) as t:
                body(t, 0, P, 0, P)
            body(QT - 1, 0, P, 1, NS)
            body(QT, 1, NS, 0, 0)

        first_tile = lambda t: isinstance(t, int) and t == 0

        with nc.Block() as block:
            @block.sync
            def _(sp):
                for dst, name in ((tri, "tri"), (tot, "tot"), (seq, "seq"), (msk, "msk"), (lvl, "lvl")):
                    sp.dma_start(dst[:], T["in"][name]).then_inc(ld, 16)
                sp.wait_ge(clear, 4)
                for h2 in range(2):
                    for j in range(NJ):
                        sp.dma_start(SS[pair_rows[h2], j, :, h2 * HD:(h2 + 1) * HD], T["in"]["gdn_state"][pair_rows[h2], j]).then_inc(ld, 16)
                sp.wait_ge(tile_done, NTI)
                for h2 in range(2):
                    sp.dma_start(T["out"]["gdn_p"][pair_rows[h2]], S[pair_rows[h2], :, h2 * HD:(h2 + 1) * HD]).then_inc(st_out, 16)
                    for j in range(NJ):
                        sp.dma_start(T["out"]["gdn_s"][pair_rows[h2], j], SS[pair_rows[h2], j, :, h2 * HD:(h2 + 1) * HD]).then_inc(st_out, 16)
                sp.wait_ge(st_out, 16 * (2 + 2 * NJ))

            @block.gpsimd
            def _(po):
                for t_ in (S, kz, vz, SS):
                    po.memset(t_[:], 0.0).then_inc(clear, 1)
                po.wait_ge(exp_ready, 1)

                def operands(t, ahead, m):
                    i = bass.ds(t + ahead, 1)
                    bc = lambda ap: one(ap).unsqueeze(2).to_broadcast([m, H, HD])
                    k, v = (qkv[0:m, i, c, :].rearrange("p a (h d) -> p (a h) d", d=HD) for c in (1, 2))
                    return k, v, bc(ab_t[0:m, i, H:2 * H]), bc(gex[0:m, i, 2, :])

                def prepare(t, ahead, smp, m):
                    i = bass.ds(t + ahead, 1)
                    if ahead:
                        po.wait_ge(t_done, count(t, 5, 5))
                    po.tensor_copy(ags[0:m], one(ab_t[0:m, i, :])).then_inc(src_ready, 1)
                    po.tensor_copy(egc[0:m], one(gex[0:m, i, 0, :])).then_inc(src_ready, 1)
                    po.tensor_copy(src[0:m], qkv[0:m, i, 0:2, :].rearrange("p a c d -> p (a c) d")).then_inc(src_ready, 1)
                    k, v, beta, e_rest = operands(t, ahead, m)
                    e_gc = egc[0:m].unsqueeze(2).to_broadcast([m, H, HD])
                    po.tensor_tensor(heads3(kb[0:m, 0]), k, beta, ALU.mult).then_inc(scaled, 1)
                    po.wait_ge(src_ready, count(t, 3, 3, ahead))
                    po.tensor_tensor(heads3(kb[0:m, 2]), heads3(src[0:m, 0]), e_gc, ALU.mult).then_inc(scaled, 1)
                    po.wait_ge(scaled, count(t, 3, 1, ahead))
                    po.tensor_tensor(heads3(kb[0:m, 1]), heads3(kb[0:m, 0]), e_gc, ALU.mult).then_inc(scaled, 1)

                def body(t, smp, m, smp_next, m_next):
                    if m_next:
                        prepare(t, 1, smp_next, m_next)
                    if not first_tile(t):
                        po.wait_ge(tile_done, t)
                    k, v, beta, e_rest = operands(t, 0, m)
                    po.tensor_tensor(heads3(vb[0:m]), v, beta, ALU.mult).then_inc(scaled_late, 1)
                    po.tensor_tensor(heads3(kb[0:m, 3]), k, e_rest, ALU.mult).then_inc(scaled_late, 1)
                tiles(po, prepare, body)

            @block.tensor
            def _(pe):
                pe.wait_ge(ld, 16 * (5 + 2 * NJ))
                pe.wait_ge(clear, 4)
                pe.matmul(A[:, 0, 0:64], tri[:, 0, :], ab_t[:, 0:QT, 0:H])
                pe.matmul(A[:, 0, 64:128], ones[:], ab_t[:, 0:QT, 0:H])
                pe.matmul(A[0:NS, 0, 128:136], tri[0:NS, 1, 0:NS], ab_t[0:NS, QT, 0:H])
                pe.matmul(A[0:NS, 0, 136:144], tot[:, 0:NS], ab_t[0:NS, QT, 0:H])
                for h in range(H):
                    mm = pe.matmul(A[:, 0, 144 + 8 * h:152 + 8 * h], ab_t[0:NS, QT, h:h + 1].to_broadcast([NS, P]), seq[:, :])
                mm.then_inc(g_prod, 1)

                def rows(t, ahead, smp, m):
                    pe.wait_ge(src_ready, count(t, 3, 3, ahead))
                    for h in range(H):
                        mm = pe.matmul(Bk[0:m, 2 + h // 4, h % 4 * P:h % 4 * P + m], ags[0:m, h:h + 1].to_broadcast([m, m]), tri[0:m, smp, 0:m])
                    mm.then_inc(row_prod, 1)

                def turn(t, ahead, m, ns):
                    from_ = [src[0:m, 1], kb[0:m, 0], src[0:m, 0], kb[0:m, 1], kb[0:m, 2]]
                    for n in ns:
                        if n == 0:
                            pe.wait_ge(scaled, count(t, 3, 3, ahead))
                            pe.wait_ge(dec_in, count(t, 1, 1, ahead))
                        if n >= 2:
                            pe.wait_ge(t_out, count(t, 5, n - 1, ahead))
                        for j in range(NJ):
                            mm = pe.transpose(Bk[:, 2 + n % 2, j * P:j * P + m], from_[n][:, j * P:(j + 1) * P], ident[0:m, 0:m])
                        mm.then_inc(t_done, 1)

                def kk(t, ahead, m, a):
                    pe.wait_ge(t_out, count(t, 5, 5 if a else 3, ahead))
                    for h in range(4 * a, 4 * a + 4):
                        mm = pe.matmul(Bk[0:m, h // 2, h % 2 * 256:h % 2 * 256 + 2 * m], kz[:, h, 0:m], kq[:, h // 2, :, 0:m])
                    mm.then_inc(kk_done, 1)

                def prepare(t, ahead, smp, m):
                    rows(t, ahead, smp, m)
                    turn(t, ahead, m, range(5))
                    kk(t, ahead, m, 0)
                    kk(t, ahead, m, 1)

                def body(t, smp, m, smp_next, m_next):
                    hh = lambda a: range(4 * a, 4 * a + 4)
                    for a in range(2):
                        pe.wait_ge(lt_ready, count(t, 4, 2 + 2 * a))
                        for h in hh(a):
                            mm = pe.transpose(A[0:m, a, h % 4 * P:h % 4 * P + m], xt[0:m, h, 0:m], ident[0:m, 0:m])
                        mm.then_inc(mm_done, 1)
                    nl = levels_of(smp)
                    for li in range(nl):
                        for a in range(2):
                            pe.wait_ge(xt_out, count(t, 2 * NL, 2 * li + a + 1))
                            for h in hh(a):
                                mm = pe.matmul(A[0:m, 2 + a, h % 4 * P:h % 4 * P + m], lt[0:m, h, 0:m], x[0:m, h, 0:m])
                            mm.then_inc(mm_done, 1)
                        for a in range(2):
                            pe.wait_ge(dv_out, count(t, 4 * NL, 4 * li + a + 1))
                            for h in hh(a):
                                l_, r_ = (xt, yy) if li < nl - 1 else (yy, xt)
                                mm = pe.matmul(Bk[0:m, a, h % 4 * P:h % 4 * P + m], l_[0:m, h, 0:m], r_[0:m, h, 0:m])
                            mm.then_inc(mm_done, 1)
                        if m_next and li == 0:
                            rows(t, 1, smp_next, m_next)
                        if m_next and 2 <= li <= 4:
                            turn(t, 1, m_next, ((0, 1), (2,), (3, 4))[li - 2])
                        if li < nl - 1:
                            for a in range(2):
                                pe.wait_ge(dv_out, count(t, 4 * NL, 4 * li + 3 + a))
                                for h in hh(a):
                                    mm = pe.transpose(A[0:m, a, h % 4 * P:h % 4 * P + m], x[0:m, h, 0:m], ident[0:m, 0:m])
                                mm.then_inc(mm_done, 1)
                    if not smp:
                        if not first_tile(t):
                            pe.wait_ge(tile_done, t)
                        for c, bank in ((0, 0), (1, 3)):
                            pe.wait_ge(t_out, count(t, 5, 4 + c))
                            for j in range(NJ):
                                mm = pe.matmul(A[:, bank, j * P:(j + 1) * P], ke[:, c, j], S[:, j], start=(c == 0 or j == 0), stop=(c == 0), skip_group_check=True)
                            mm.then_inc(chain_mm, 1)
                    for a in range(2):
                        pe.wait_ge(dv_out, count(t, 4 * NL, 4 * nl - 1 + a))
                    if smp:
                        for c in range(2):
                            for j in range(NJ):
                                if c or j >= 2:
                                    pe.wait_ge(chain_ev, 2 * QT + 4 * c + j - 1)
                                for b in range(2):
                                    mm = pe.matmul(Bk[0:m, 2 * (j % 2) + b, :], ke[:, c, j, 0:m], SS[:, j, 4 * b:4 * b + 4, :].rearrange("p b e -> p (b e)"))
                                mm.then_inc(chain_mm, 1)
                    if m_next:
                        kk(t, 1, m_next, 0)
                    ev = t * 2 + (8 if smp else 0)
                    pe.wait_ge(chain_ev, ev + 1)
                    for h in range(H):
                        mm = pe.matmul(A[0:m, 1 + h // 4, h % 4 * P:(h % 4 + 1) * P], xt[0:m, h, 0:m], r[0:m, h // 2 * P:(h // 2 + 1) * P])
                    mm.then_inc(chain_mm, 1)
                    if m_next:
                        kk(t, 1, m_next, 1)
                    pe.wait_ge(chain_ev, ev + 2)
                    for h in range(H):
                        j = h // 2
                        mm = pe.matmul(A[0:m, 3, j * P:(j + 1) * P], at[0:m, h, 0:m], vz[0:m, h * P:(h + 1) * P],
                                       start=bool(smp and h == 0), stop=True, skip_group_check=True)
                    mm.then_inc(chain_mm, 1)
                    pe.wait_ge(scaled_late, count(t, 2, 2))
                    if not smp:
                        for j in range(NJ):
                            mm = pe.matmul(A[:, 0, j * P:(j + 1) * P], kb[:, 3, j * P:(j + 1) * P],
                                           vz[:, j * 256:j * 256 + 384].rearrange("p (a b) -> p a b", a=2)[:, :, 0:HD])
                        mm.then_inc(chain_mm, 1)
                    else:
                        for j in range(NJ):
                            if j >= 2:
                                pe.wait_ge(state_done, j - 1)
                            pe.wait_ge(chain_ev, 2 * QT + 11 + j)
                            for b in range(2):
                                mm = pe.matmul(Bk[:, 2 * (j % 2) + b, :], kb[0:m, 3, j * P:(j + 1) * P], yy[0:m, 4 * b:4 * b + 4, :].rearrange("p b e -> p (b e)"))
                            mm.then_inc(chain_mm, 1)
                pe.wait_ge(exp_ready, 1)
                tiles(pe, prepare, body)
                pe.wait_ge(tile_done, NTI)

            @block.scalar
            def _(act):
                act.wait_ge(g_read, 3)
                act.activation(gex[:, 0:QT], gst[:, 0:QT], ACT.Exp)
                act.activation(gex[0:NS, QT], gst[0:NS, QT], ACT.Exp)
                for h2 in range(2):
                    e_ = act.activation(eglS[pair_rows[h2]], A[pair_rows[h2], 0, 144:208].rearrange("p (j a b) -> p j a b", a=2, b=NB)[:, :, h2, :], ACT.Exp)
                e_.then_inc(exp_ready, 1)

                def decay(t, ahead, m):
                    act.wait_ge(dec_in, count(t, 1, 1, ahead))
                    act.activation(dec[0:m, :, 0:m], dec[0:m, :, 0:m], ACT.Exp).then_inc(dec_ready, 1)

                def turned(t, ahead, m, ns):
                    four = lambda n: Bk[:, 2 + n % 2, :].rearrange("p (j t) -> p j t", j=NJ)[:, :, 0:m]
                    for n in ns:
                        act.wait_ge(t_done, count(t, 5, n + 1, ahead))
                        if n == 0:
                            act.activation(kz[pair_rows[0], 0:H:2, 0:m], four(0)[pair_rows[0]], ACT.Copy)
                            act.activation(kz[pair_rows[1], 1:H:2, 0:m], four(0)[pair_rows[1]], ACT.Copy).then_inc(t_out, 1)
                            continue
                        dst = {1: kq[:, :, 0, 0:m], 2: kq[:, :, 1, 0:m], 3: ke[:, 0, :, 0:m], 4: ke[:, 1, :, 0:m]}[n]
                        if n >= 3 and ahead:
                            act.wait_ge(chain_mm, count(t, 5, n - 2))
                        act.activation(dst, four(n), ACT.Copy).then_inc(t_out, 1)

                def prepare(t, ahead, smp, m):
                    act.wait_ge(clear, 4)
                    decay(t, ahead, m)
                    turned(t, ahead, m, range(5))

                def body(t, smp, m, smp_next, m_next):
                    for li in range(levels_of(smp)):
                        for a in range(2):
                            act.wait_ge(mm_done, count(t, 6 * NL, 6 * li + a + 1))
                            act.activation((x if li == 0 else xt)[0:m, 4 * a:4 * a + 4, 0:m], A[0:m, a, :].rearrange("p (h t) -> p h t", h=4)[:, :, 0:m], ACT.Copy).then_inc(xt_out, 1)
                        if m_next and li == 1:
                            decay(t, 1, m_next)
                        if m_next and li in (2, 3):
                            turned(t, 1, m_next, ((0, 1), (2,))[li - 2])
                    if m_next:
                        turned(t, 1, m_next, (3, 4))
                    if not smp:
                        act.wait_ge(chain_mm, count(t, 5, 4))
                        act.activation(og[:, bass.ds(t, 1), :].rearrange("p a c -> p (a c)"), A[:, 3, :], ACT.Copy).then_inc(og_out, 1)
                tiles(act, prepare, body)

            @block.vector
            def _(dve):
                dve.wait_ge(g_prod, 1)
                g_of = lambda c: gst[:, 0:QT, c, :]
                dve.tensor_copy(g_of(0), A[:, 0, 0:64].rearrange("p (t h) -> p t h", h=H))
                dve.tensor_copy(g_of(1), A[:, 0, 64:128].rearrange("p (t h) -> p t h", h=H))
                dve.tensor_copy(gst[0:NS, QT, 0:2, :], A[0:NS, 0, 128:144].rearrange("p (c h) -> p c h", h=H)).then_inc(g_read, 1)
                dve.wait_ge(g_read, 1)
                dve.tensor_tensor(g_of(2), g_of(1), g_of(0), ALU.subtract).then_inc(g_read, 1)
                dve.tensor_tensor(gst[0:NS, QT, 2, :], gst[0:NS, QT, 1, :], gst[0:NS, QT, 0, :], ALU.subtract).then_inc(g_read, 1)
                dve.wait_ge(ld, 16 * (5 + 2 * NJ))
                dve.wait_ge(clear, 4)
                bch = lambda ap, m, n=4: ap.unsqueeze(1).to_broadcast([m, n, m])

                def decay(t, ahead, smp, m):
                    dve.wait_ge(row_prod, count(t, 1, 1, ahead))
                    for a in range(2):
                        p_ = Bk[0:m, 2 + a, :].rearrange("p (h t) -> p h t", h=4)[:, :, 0:m]
                        gc = one(gst[0:m, bass.ds(t + ahead, 1), 0, 4 * a:4 * a + 4])
                        dve.tensor_tensor(dec[0:m, 4 * a:4 * a + 4, 0:m], p_, gc.unsqueeze(2).to_broadcast([m, 4, m]), ALU.subtract).then_inc(dec_part, 1)
                    dve.wait_ge(dec_part, count(t, 2, 2, ahead))
                    dve.tensor_tensor(dec[0:m, :, 0:m], dec[0:m, :, 0:m], bch(msk[0:m, smp * P:smp * P + m], m, H), ALU.add).then_inc(dec_in, 1)

                def decayed(t, ahead, m):
                    dve.wait_ge(dec_ready, count(t, 1, 1, ahead))
                    for a in range(2):
                        hs = slice(4 * a, 4 * a + 4)
                        dve.wait_ge(kk_done, count(t, 2, a + 1, ahead))
                        p_ = Bk[0:m, 2 * a:2 * a + 2, :].rearrange("p b (h c) -> p (b h) c", h=2)
                        dve.tensor_tensor(lt[0:m, hs, 0:m], p_[:, :, 0:m], dec[0:m, hs, 0:m], ALU.mult).then_inc(lt_part, 1)
                        dve.tensor_tensor(at[0:m, hs, 0:m], p_[:, :, m:2 * m], dec[0:m, hs, 0:m], ALU.mult).then_inc(lt_ready, 1)
                        dve.wait_ge(lt_part, count(t, 2, a + 1, ahead))
                        dve.tensor_tensor(xt[0:m, hs, 0:m], lt[0:m, hs, 0:m], bch(lvl[0:m, 0, 0:m], m), ALU.mult).then_inc(xt_part, 1)
                        dve.wait_ge(xt_part, count(t, 2, a + 1, ahead))
                        dve.tensor_tensor(xt[0:m, hs, 0:m], bch(ident[0:m, 0:m], m), xt[0:m, hs, 0:m], ALU.subtract).then_inc(lt_ready, 1)

                def prepare(t, ahead, smp, m):
                    decay(t, ahead, smp, m)
                    decayed(t, ahead, m)

                def body(t, smp, m, smp_next, m_next):
                    linked = [0]
                    def link(ins, wait=True):
                        ins.then_inc(step, 1)
                        linked[0] += 1
                        if wait:
                            dve.wait_ge(step, linked[0])
                    nl = levels_of(smp)
                    for li in range(nl):
                        for a in range(2):
                            hs = slice(4 * a, 4 * a + 4)
                            dve.wait_ge(mm_done, count(t, 6 * NL, 6 * li + 3 + a))
                            p_ = A[0:m, 2 + a, :].rearrange("p (h t) -> p h t", h=4)[:, :, 0:m]
                            dve.tensor_tensor(yy[0:m, hs, 0:m], p_, bch(lvl[0:m, 1 + li, 0:m], m), ALU.mult).then_inc(dv_out, 1)
                        for a in range(2):
                            hs = slice(4 * a, 4 * a + 4)
                            dve.wait_ge(mm_done, count(t, 6 * NL, 6 * li + 5 + a))
                            p_ = Bk[0:m, a, :].rearrange("p (h t) -> p h t", h=4)[:, :, 0:m]
                            dst = x if li < nl - 1 else xt
                            dve.tensor_tensor(dst[0:m, hs, 0:m], dst[0:m, hs, 0:m], p_, ALU.subtract).then_inc(dv_out, 1)
                        if m_next and li == 0:
                            decay(t, 1, smp_next, m_next)
                    dve.wait_ge(scaled_late, count(t, 2, 1))
                    if not smp:
                        dve.wait_ge(chain_mm, count(t, 5, 1))
                        dve.tensor_tensor(r[:], vb[:], A[:, 0, :], ALU.subtract).then_inc(chain_ev, 1)
                        dve.wait_ge(chain_mm, count(t, 5, 2))
                        for h2 in range(2):
                            q_ = S[pair_rows[h2], :, h2 * HD:(h2 + 1) * HD]
                            e_ = one(gex[pair_rows[h2], bass.ds(t, 1), 1, h2:H:2])
                            dve.tensor_tensor(q_, q_, e_.unsqueeze(2).to_broadcast([HD, NJ, HD]), ALU.mult).then_inc(s_part, 1)
                        dve.wait_ge(chain_mm, count(t, 5, 3))
                    else:
                        for c in range(2):
                            for j in range(NJ):
                                dve.wait_ge(chain_mm, 5 * QT + 4 * c + j + 1)
                                p_ = Bk[0:m, 2 * (j % 2):2 * (j % 2) + 2, :].rearrange("p c (b e) -> p (c b) e", b=4)
                                dve.tensor_tensor(yy[0:m, 0:NB, :], p_, seq[:, :].unsqueeze(2).to_broadcast([m, NB, P]), ALU.mult).then_inc(chain_ev, 1)
                                dve.wait_ge(chain_ev, 2 * QT + 4 * c + j + 1)
                                dst = r[0:m] if c == 0 else dec[0:m, 0:4, :].rearrange("p a b -> p (a b)")
                                link(dve.tensor_reduce(dst[:, j * P:(j + 1) * P], yy[0:m, 0:NB, :].rearrange("p b e -> p e b"), AX, ALU.add))
                        dve.tensor_tensor(r[0:m], vb[0:m], r[0:m], ALU.subtract).then_inc(chain_ev, 1)
                        dve.wait_ge(chain_mm, 5 * QT + 9)
                    for h2 in range(2):
                        for bk in range(2):
                            p_ = A[0:m, 1 + bk, :].rearrange("p (j a e) -> p j a e", j=2, a=2)[:, :, h2, h2 * HD:(h2 + 1) * HD]
                            z = dve.tensor_copy(vz[0:m, 512 * bk:512 * bk + 512].rearrange("p (j c) -> p j c", j=2)[:, :, h2 * 192:h2 * 192 + HD], p_)
                    z.then_inc(chain_ev, 1)
                    if not smp:
                        dve.wait_ge(s_part, count(t, 2, 2))
                        dve.wait_ge(chain_mm, count(t, 5, 5))
                        dve.wait_ge(og_out, count(t, 1, 1))
                        for h2 in range(2):
                            q_ = S[pair_rows[h2], :, h2 * HD:(h2 + 1) * HD]
                            z = dve.tensor_tensor(q_, q_, A[pair_rows[h2], 0, :].rearrange("p (j e) -> p j e", j=NJ)[:, :, h2 * HD:(h2 + 1) * HD], ALU.add)
                        z.then_inc(tile_done, 1)
                        decayed(t, 1, m_next)
                    else:
                        dve.wait_ge(chain_mm, 5 * QT + 10)
                        link(dve.tensor_tensor(og[0:m, QT, :], dec[0:m, 0:4, :].rearrange("p a b -> p (a b)"), A[0:m, 3, :], ALU.add), wait=False)
                        for j in range(NJ):
                            if j:
                                dve.wait_ge(chain_mm, 5 * QT + 10 + j)
                            for a in range(2):
                                z = dve.tensor_tensor(yy[0:m, 0:NB, a * HD:(a + 1) * HD], vz[0:m, j * 256 + a * 192:j * 256 + a * 192 + HD].unsqueeze(1).to_broadcast([m, NB, HD]),
                                                      seq[:, :].unsqueeze(2).to_broadcast([m, NB, HD]), ALU.mult)
                            z.then_inc(chain_ev, 1)
                            for h2 in range(2):
                                q_ = SS[pair_rows[h2], j, :, h2 * HD:(h2 + 1) * HD]
                                link(dve.tensor_tensor(q_, q_, eglS[pair_rows[h2], j, :].unsqueeze(2).to_broadcast([HD, NB, HD]), ALU.mult), wait=(h2 == 1))
                            dve.wait_ge(chain_mm, 5 * QT + 11 + j)
                            for h2 in range(2):
                                q_ = SS[pair_rows[h2], j, :, h2 * HD:(h2 + 1) * HD]
                                p_ = Bk[pair_rows[h2], 2 * (j % 2):2 * (j % 2) + 2, :].rearrange("p c (b e) -> p (c b) e", b=4)[:, :, h2 * HD:(h2 + 1) * HD]
                                z = dve.tensor_tensor(q_, q_, p_, ALU.add)
                            z.then_inc(state_done, 1)
                        dve.wait_ge(state_done, NJ)
                        dve.sem_inc(tile_done, 1)
                tiles(dve, prepare, body)


def stage_gdn_norm(nc, T):
    with ExitStack() as ctx:
        sb = lambda n, s, d=F32: ctx.enter_context(nc.sbuf_tensor(n, s, d))
        sem = lambda n: ctx.enter_context(nc.semaphore(n))
        NTI = QT + 1
        sq = [sb(f"nsq{i}", [P, 512]) for i in range(2)]
        ss = sb("nss", [P, NTI, H])
        gn = sb("gn", [P, HD])
        tP = ctx.enter_context(nc.psum_tensor("ntP", [P, 2, 512], F32))
        ld, sq_ready, ss_ready, rt, sc, turned, done, step = (sem("n" + x) for x in ("ld", "sq_ready", "ss_ready", "rt", "sc", "turned", "done", "step"))
        og, zbT, ident = T["og"], T["zbT"], T["ident"]
        rows = lambda t: P if t < QT else NS
        with nc.Block() as block:
            @block.sync
            def _(sp):
                sp.dma_start(gn[:], T["in"]["gdn_norm"]).then_inc(ld, 16)
                sp.wait_ge(ld, 16)

            @block.scalar
            def _(act):
                for t in range(NTI):
                    m = rows(t)
                    if t >= 2:
                        act.wait_ge(ss_ready, t - 1)
                    act.activation(sq[t % 2][0:m], og[0:m, t, :], ACT.Square).then_inc(sq_ready, 1)
                act.wait_ge(step, 3)
                act.activation(ss[:], ss[:], ACT.Sqrt).then_inc(rt, 1)

            @block.vector
            def _(dve):
                def finish(dve, t):
                    m = rows(t)
                    dve.wait_ge(turned, t + 1)
                    z = zbT[:, :, t * P:t * P + m]
                    dve.tensor_tensor(z, z, tP[:, t % 2, :].rearrange("p (j t) -> p j t", j=NJ)[:, :, 0:m], ALU.mult).then_inc(done, 1)

                dve.memset(ss[:], 1.0).then_inc(step, 1)
                dve.wait_ge(step, 1)
                for t in range(NTI):
                    m = rows(t)
                    dve.wait_ge(sq_ready, t + 1)
                    dve.tensor_reduce(ss[0:m, t, :], sq[t % 2][0:m].rearrange("p (h d) -> p h d", d=HD), AX, ALU.add).then_inc(ss_ready, 1)
                dve.wait_ge(ss_ready, NTI)
                dve.tensor_scalar(ss[:], ss[:], 1.0 / HD, EPS, ALU.mult, ALU.add).then_inc(step, 1)
                dve.wait_ge(step, 2)
                dve.reciprocal(ss[:], ss[:]).then_inc(step, 1)
                dve.wait_ge(rt, 1)
                dve.wait_ge(ld, 16)
                for t in range(NTI):
                    m = rows(t)
                    x = og[0:m, t, :].rearrange("p (h d) -> p h d", d=HD)
                    dve.tensor_tensor(x, x, ss[0:m, t].unsqueeze(2).to_broadcast([m, H, HD]), ALU.mult).then_inc(step, 1)
                    dve.wait_ge(step, 4 + t)
                    dve.tensor_tensor(x, x, gn[0:m].unsqueeze(1).to_broadcast([m, H, HD]), ALU.mult).then_inc(sc, 1)
                    if t:
                        finish(dve, t - 1)
                finish(dve, NTI - 1)

            @block.tensor
            def _(pe):
                for t in range(NTI):
                    m = rows(t)
                    pe.wait_ge(sc, t + 1)
                    if t >= 2:
                        pe.wait_ge(done, t - 1)
                    for j in range(NJ):
                        mm = pe.transpose(tP[:, t % 2, j * P:j * P + m], og[0:m, t, j * P:(j + 1) * P], ident[0:m, 0:m])
                    mm.then_inc(turned, 1)


def stage_gdn(nc, T):
    with nc.sbuf_tensor("qkv", [P, QT + 1, 3, 512], F32) as qkv:
        T["qkv"] = qkv
        with nc.sbuf_tensor("uT", [P, 12, TOK], F32) as uT:
            T["uT"] = uT
            stage_gdn_project(nc, T)
            stage_gdn_tokens(nc, T)
        T["og"] = qkv[:, :, 0, :]
        stage_gdn_scan(nc, T)
        stage_gdn_norm(nc, T)


def stage_output(nc, T):
    with ExitStack() as ctx:
        sb = lambda n, s, d=F32: ctx.enter_context(nc.sbuf_tensor(n, s, d))
        sem = lambda n: ctx.enter_context(nc.semaphore(n))
        NTI = QT + 1
        wg = [sb(f"ow{i}", [P, KT, 256]) for i in range(2)]
        wo = [sb(f"oo{i}", [P, 2, NJ, P]) for i in range(2)]
        mT = sb("mT", [P, KT, TOK])
        sg = [sb(f"sg{i}", [P, TOK]) for i in range(2)]
        pr = sb("pr", [P, TOK])
        gP = ctx.enter_context(nc.psum_tensor("ogP", [P, 3, 512], F32))
        oP = ctx.enter_context(nc.psum_tensor("ooP", [P, 3, 512], F32))
        ld_w = [sem(f"old_w{i}") for i in range(2)]
        g_prod, g_out, o_prod, o_out, step = (sem("o" + n) for n in ("g_prod", "g_out", "o_prod", "o_out", "step"))
        hT, zaT, zbT = T["hT"], T["zaT"], T["zbT"]
        U = 2 * KT
        with nc.Block() as block:
            @block.sync
            def _(sp):
                for f in range(KT):
                    if f >= 2:
                        sp.wait_ge(o_prod, 2 * (f - 1))
                    sp.dma_start(wg[f % 2][:], T["in"]["w_gm"][f].rearrange("p (k n) -> p k n", k=KT)).then_inc(ld_w[f % 2], 16)
                    sp.dma_start(wo[f % 2][:], T["in"]["w_o"][f].rearrange("p (c k n) -> p c k n", c=2, k=NJ)).then_inc(ld_w[f % 2], 16)

            @block.tensor
            def _(pe):
                for u in range(U):
                    f, c = u // 2, u % 2
                    if c == 0:
                        pe.wait_ge(ld_w[f % 2], 32 * (f // 2 + 1))
                    if u:
                        pe.wait_ge(g_out, u)
                    product_features(pe, gP, wg[f % 2], hT, c).then_inc(g_prod, 1)
                    if u:
                        pe.wait_ge(o_out, u)
                    src = (zaT, zbT)[c]
                    for k in range(NJ):
                        for b in range(3):
                            mm = pe.matmul(oP[:, b, 0:TB], wo[f % 2][:, c, k, :], src[:, k, b * TB:(b + 1) * TB], start=(k == 0), stop=(k == NJ - 1))
                    mm.then_inc(o_prod, 1)

            @block.scalar
            def _(act):
                for u in range(U):
                    act.wait_ge(g_prod, u + 1)
                    if u >= 2:
                        act.wait_ge(o_out, u - 1)
                    act.activation(sg[u % 2][:].rearrange("p (b t) -> p b t", b=3), gP[:, :, 0:TB], ACT.Sigmoid).then_inc(g_out, 1)

            @block.vector
            def _(dve):
                for u in range(U):
                    f, c = u // 2, u % 2
                    dve.wait_ge(g_out, u + 1)
                    dve.wait_ge(o_prod, u + 1)
                    dst = mT[:, f, :] if c == 0 else pr[:]
                    dve.tensor_tensor(dst.rearrange("p (b t) -> p b t", b=3), oP[:, :, 0:TB], sg[u % 2][:].rearrange("p (b t) -> p b t", b=3), ALU.mult).then_inc(o_out, 1)
                    if c:
                        dve.wait_ge(o_out, u + 1)
                        dve.tensor_tensor(mT[:, f, :], mT[:, f, :], pr[:], ALU.add).then_inc(step, 1)
                        dve.wait_ge(step, f + 1)

        with ExitStack() as ctx2:
            sb = lambda n, s, d=F32: ctx2.enter_context(nc.sbuf_tensor(n, s, d))
            sem = lambda n: ctx2.enter_context(nc.semaphore(n))
            wf = sb("wf", [P, KT, D_MODEL])
            xr = [sb(f"xr{i}", [P, D_MODEL]) for i in range(2)]
            gt = sb("gt", [P, D_MODEL])
            gs = sb("gs", [NS, D_MODEL])
            fg = sb("fg", [P, D_MODEL])
            sel = sb("osel", [9, P + NS])
            rs = sb("ors", [P, NTI])
            ld, ld_x, y_prod, y_out, st_y, sel_p, gt_ready, st2, q_ready, root = (sem("y" + n) for n in ("ld", "ld_x", "prod", "out", "st", "sel_p", "gt_ready", "step", "sq", "root"))
            ld_xr = [ld_x, sem("yld_x1")]
            st_y = [st_y, sem("yst_1")]
            rows = lambda t: P if t < QT else NS
            y_dram = lambda t: T["out"]["y_prompt"][0, t * P:(t + 1) * P, :] if t < QT else T["out"]["y_sample"].rearrange("b t d -> (b t) d")
            bank = lambda t: (gP if t % 2 == 0 else oP)
            gate = T["gate"]
            with nc.Block() as block:
                @block.sync
                def _(sp):
                    sp.dma_start(sel[:], T["in"]["row_sel"]).then_inc(ld, 16)
                    sp.dma_start(fg[:], T["in"]["final_g"]).then_inc(ld, 16)
                    for n in range(2):
                        sp.dma_start(wf[:, :, n * 512:(n + 1) * 512], T["in"]["w_out"][n].rearrange("p (k n) -> p k n", k=KT)).then_inc(ld, 16)
                    for t in range(NTI):
                        if t >= 2:
                            sp.wait_ge(st_y[t % 2], 16 * (t // 2))
                        sp.dma_start(xr[t % 2][0:rows(t)], T["in"]["x"][t * P:t * P + rows(t), :]).then_inc(ld_xr[t % 2], 16)

                @block.scalar
                def _(act):
                    for t in range(NTI):
                        m = rows(t)
                        act.wait_ge(y_out, t + 1)
                        act.activation(pr[0:m, 0:D_MODEL], xr[t % 2][0:m], ACT.Square, accum_out=rs[0:m, t:t + 1]).then_inc(q_ready, 1)
                        act.wait_ge(st2, 4 * t + 2)
                        act.activation(rs[0:m, t:t + 1], rs[0:m, t:t + 1], ACT.Sqrt).then_inc(root, 1)
                        act.wait_ge(st2, 4 * t + 4)
                        act.dma_start(y_dram(t), xr[t % 2][0:m]).then_inc(st_y[t % 2], 16)
                    act.wait_ge(st_y[0], 16 * ((NTI + 1) // 2))
                    act.wait_ge(st_y[1], 16 * (NTI // 2))

                @block.tensor
                def _(pe):
                    pe.wait_ge(ld, 64)
                    for c in range(2):
                        pe.matmul(gP[:, c, :], sel[:, 0:P], gate[:, c * 512:(c + 1) * 512])
                        mm = pe.matmul(oP[0:NS, c, :], sel[:, P:P + NS], gate[:, c * 512:(c + 1) * 512])
                    mm.then_inc(sel_p, 1)
                    pe.wait_ge(gt_ready, 2)
                    for t in range(NTI):
                        m = rows(t)
                        if t >= 2:
                            pe.wait_ge(y_out, t - 1)
                        for c in range(2):
                            for k in range(KT):
                                mm = pe.matmul(bank(t)[0:m, c, :], mT[:, k, t * P:t * P + m], wf[:, k, c * 512:(c + 1) * 512], start=(k == 0), stop=(k == KT - 1))
                        mm.then_inc(y_prod, 1)

                @block.vector
                def _(dve):
                    dve.wait_ge(sel_p, 1)
                    dve.tensor_copy(gt[:].rearrange("p (c n) -> p c n", c=2), gP[:, 0:2, :]).then_inc(gt_ready, 1)
                    dve.tensor_copy(gs[:].rearrange("p (c n) -> p c n", c=2), oP[0:NS, 0:2, :]).then_inc(gt_ready, 1)
                    dve.wait_ge(gt_ready, 2)
                    dve.wait_ge(ld, 64)
                    for t in range(NTI):
                        m = rows(t)
                        x = xr[t % 2][0:m]
                        dve.wait_ge(y_prod, t + 1)
                        dve.wait_ge(ld_xr[t % 2], 16 * (t // 2 + 1))
                        gate_t = gt if t < QT else gs
                        tmp = sg[t % 2][0:m, 0:D_MODEL]
                        dve.tensor_tensor(tmp.rearrange("p (c n) -> p c n", c=2), bank(t)[0:m, 0:2, :], gate_t[0:m].rearrange("p (c n) -> p c n", c=2), ALU.mult).then_inc(st2, 1)
                        dve.wait_ge(st2, 4 * t + 1)
                        dve.tensor_tensor(x, x, tmp, ALU.add).then_inc(y_out, 1)
                        dve.wait_ge(q_ready, t + 1)
                        dve.tensor_scalar(rs[0:m, t:t + 1], rs[0:m, t:t + 1], 1.0 / D_MODEL, EPS, ALU.mult, ALU.add).then_inc(gt_ready, 1)
                        dve.wait_ge(gt_ready, 3 + t)
                        dve.reciprocal(rs[0:m, t:t + 1], rs[0:m, t:t + 1]).then_inc(st2, 1)
                        dve.wait_ge(root, t + 1)
                        dve.tensor_scalar(x, x, rs[0:m, t:t + 1], None, ALU.mult).then_inc(st2, 1)
                        dve.wait_ge(st2, 4 * t + 3)
                        dve.tensor_tensor(x, x, fg[0:m], ALU.mult).then_inc(st2, 1)


def build(nc, ins, outs):
    T = {"in": ins, "out": outs}
    with ExitStack() as ctx:
        def sb(name, shape, dt=F32):
            T[name] = ctx.enter_context(nc.sbuf_tensor(name, shape, dt))
        sb("hT", [P, KT, TOK])
        sb("gate", [9, D_MODEL])
        sb("ones", [P, P])
        sb("ident", [P, P])
        sb("zaT", [P, NJ, TOK])
        sb("zbT", [P, NJ, TOK])
        sb("ab_t", [P, QT + 1, 16])
        stage_input(nc, T)
        with nc.sbuf_tensor("qT", [P, NJ, TOK], F32) as qT, nc.sbuf_tensor("kvt", [P, QT + 1, KVG], F32) as kvt:
            T["qT"], T["kvt"] = qT, kvt
            stage_nsa_project(nc, T)
            with nc.sbuf_tensor("kvT", [P, 2, TOK], F32) as kvT, nc.sbuf_tensor("kcT", [P, NSEQ, 64], F32) as kcT, \
                    nc.sbuf_tensor("vc", [NCMP, NSEQ, P], F32) as vc:
                T["kvT"], T["kcT"], T["vc"] = kvT, kcT, vc
                stage_compress(nc, T)
                stage_sample_attention(nc, T)
                stage_prompt_attention(nc, T)
        stage_gdn(nc, T)
        stage_output(nc, T)


def layouts(inp):
    a = {k: np.asarray(v) for k, v in inp.items()}
    f = np.float32
    c = np.concatenate([a["c_sample"], a["c_prompt"]], 0)
    x = np.concatenate([a["x_prompt"][0], a["x_sample"].reshape(NS, D_MODEL)], 0)
    o = {}
    o["cT"] = np.ascontiguousarray(c.T.reshape(KT, P, 9).transpose(1, 0, 2))
    o["xT"] = np.ascontiguousarray(x.T.reshape(KT, P, TOK).transpose(1, 0, 2))
    o["x"] = x
    wt = lambda w, n: np.ascontiguousarray(w.reshape(-1, P, w.shape[1] // n, n).transpose(2, 1, 0, 3).reshape(w.shape[1] // n, P, -1))
    o["w_ada"] = wt(a["w_ada"][0], 512)
    o["b_ada"] = np.ascontiguousarray(np.broadcast_to(a["b_ada"][0], (9, 3072)))
    o["norm_gT"] = np.ascontiguousarray(a["norm_g"][0].reshape(KT, P).T)
    w = a["w_in"][0]
    pair = np.arange(512).reshape(2, NJ, HD).transpose(1, 0, 2).reshape(-1)
    q, kv, g = w[:, 0:512], w[:, 512:1280], w[:, 1280:1304]
    za, qkv, ab, zb, gm = w[:, 1304:1816], w[:, 1816:3352], w[:, 3352:3368], w[:, 3368:3880], w[:, 3880:5928]
    o["w_feat_full"] = np.concatenate([q[:, pair], za[:, pair], qkv, zb, gm], 1)
    o["w_tok"] = wt(np.concatenate([kv, g, ab], 1), KVH)
    o["ident"] = np.eye(P, dtype=f)
    extra_layouts(a, o, pair, f)
    return o


def extra_layouts(a, o, pair, f):
    cc = a["cache_cmp_kv"][0]
    o["cmp_pool"] = np.ascontiguousarray(cc.reshape(NPOOL, 8, 16, 2, 2, HD).transpose(0, 4, 5, 3, 2, 1).reshape(NPOOL, P, 256))
    cs = a["cache_sel_kv"][0].reshape(NPOOL, PAGE, 2, P)
    o["sel_k"] = np.ascontiguousarray(cs[:, :, 0].transpose(0, 2, 1))
    o["sel_v"] = np.ascontiguousarray(cs[:, :, 1])
    cw = a["cache_win_kv"][0].reshape(NB, WIN, 2, P)
    o["cache_win"] = cw.reshape(NB, WIN, 2 * P)
    o["win_k"] = np.ascontiguousarray(cw[:, :, 0].reshape(2, 4, WIN, P).transpose(0, 3, 1, 2).reshape(2, P, 4 * WIN))
    o["win_v"] = np.ascontiguousarray(cw[:, :, 1].reshape(2, 4, 4, P, P).transpose(0, 3, 1, 2, 4).reshape(2, P, 16 * P))
    o["pages"] = a["page_table"].reshape(1, NB * NPAGE)
    both = lambda n: np.stack([a[n + "_k"][0], a[n + "_v"][0]])
    o["cmp_w1"] = np.ascontiguousarray(both("cmp_w1").transpose(2, 0, 1, 3))
    o["cmp_w2"] = np.ascontiguousarray(both("cmp_w2").transpose(1, 0, 2))
    pe = both("cmp_pe").transpose(2, 0, 1)
    o["cmp_pe"] = np.ascontiguousarray(np.concatenate([pe, pe], 0))
    r = np.arange(P)
    g, j, t = (r // 16) % 2, (r // 4) % 4, r % 4
    h = g * NJ + j
    slope = (0.5 ** (h + 1.0))[:, None]
    end = np.arange(NCMP) * 16 + 31
    now = (1024 + t)[:, None]
    tab = np.zeros((P, 1840), f)
    tab[:, 0:63] = -slope * (now - end)
    tab[:, 63:1087] = -slope * (now - np.arange(1024))
    wpos = 512 + np.arange(512)
    tab[:, 1087:1599] = np.where(now - wpos < WIN, -slope * (now - wpos), NEG)
    for G in range(2):
        b = G * 4 + r // 32
        tok = np.arange(NS)
        ok = (tok // 4 == b[:, None]) & (tok % 4 <= t[:, None])
        tab[:, 1599 + 32 * G:1631 + 32 * G] = np.where(ok, -slope * (t[:, None] - tok % 4), NEG)
    i16, j64 = np.arange(NCMP)[:, None] * 16, np.arange(16)[None] * 64
    tab[:NCMP, 1663:1679] = np.clip(np.minimum(i16 + 32, j64 + 64) - np.maximum(i16, j64), 0, None) / 32
    same = (r[:, None] // 32 == r // 32) & (g[:, None] == g) & (t[:, None] == t)
    tab[:, 1679:1807] = same
    tab[:, 1807:1815] = h[:, None] == np.arange(H)
    tab[:, 1815:1831] = np.arange(16)
    tab[:, 1831], tab[:, 1832] = g == 0, g == 1
    o["sample_tab"] = tab
    o["token_sel"] = np.ascontiguousarray(np.stack([(np.arange(NS)[:, None] == (G * 4 + r // 32) * 4 + t) for G in range(2)], 1).astype(f))
    more_layouts(a, o, pair, f)


def more_layouts(a, o, pair, f):
    p, c = np.arange(P)[:, None], np.arange(SEQ)
    d = p - (c - (SEQ - P))
    o["dist"] = np.where(d >= 0, -d, NEG).astype(f)
    d = p - np.arange(P) + WIN
    o["dist_w"] = np.where(d < WIN, -d, NEG).astype(f)
    d = (np.arange(QT)[:, None] * P + np.arange(P))[:, :, None] - (np.arange(64) * 16 + 31)
    o["dist_c"] = np.ascontiguousarray(np.where(d >= 0, -d, NEG).astype(f).transpose(1, 0, 2))
    o["slope"] = np.ascontiguousarray(np.broadcast_to((0.5 ** (np.arange(2) * NJ + np.arange(NJ)[:, None] + 1.0)).reshape(-1), (P, H)).astype(f))
    gdn_layouts(a, o, pair, f)


def gdn_layouts(a, o, pair, f):
    w = o.pop("w_feat_full")
    wt = lambda w, n: np.ascontiguousarray(w.reshape(-1, P, w.shape[1] // n, n).transpose(2, 1, 0, 3).reshape(w.shape[1] // n, P, -1))
    o["w_feat"] = wt(w[:, 0:3072], 256)
    gm = w[:, 3072:].reshape(D_MODEL, 2, KT, P).transpose(0, 2, 1, 3).reshape(D_MODEL, 2048)
    o["w_gm"] = wt(gm, 256)
    o["conv_w"] = np.ascontiguousarray(np.concatenate([a["conv_w"][0], a["conv_b"]], 0).reshape(5, 12, P).transpose(2, 1, 0))
    o["conv_state"] = np.ascontiguousarray(a["state_conv"][0].reshape(NB, 3, 12, P).transpose(3, 2, 0, 1))
    o["gdn_state"] = np.ascontiguousarray(a["state_gdn"][0].reshape(NB, NJ, P, HD).transpose(2, 1, 0, 3))
    o["gdn_ab"] = np.ascontiguousarray(np.broadcast_to(np.stack([a["gdn_dt_bias"][0], a["gdn_a_log"][0]]), (P, 2, H)))
    o["gdn_norm"] = np.ascontiguousarray(np.broadcast_to(a["gdn_norm_g"][0], (P, HD)))
    i = np.arange(P)
    same = i[:, None] // NT == i // NT
    le = i[:, None] <= i
    o["tri"] = np.ascontiguousarray(np.stack([le, le & same], 1).astype(f))
    o["tot"] = np.ascontiguousarray(same[0:NS].astype(f))
    o["seq"] = np.ascontiguousarray((np.arange(NS)[:, None] // NT == np.arange(NB)).astype(f))
    o["msk"] = np.ascontiguousarray(np.where(np.concatenate([le, (le & same)[:, 0:NS]], 1), 0, NEG).astype(f))
    m = lambda s: (i[:, None] // s == i // s + 1) & (i[:, None] // s % 2 == 1)
    o["lvl"] = np.ascontiguousarray(np.stack([m(1).T] + [m(2 ** n) for n in range(1, 7)], 1).astype(f))
    wo = np.stack([a["w_o_nsa"][0][pair], a["w_o_gdn"][0]])
    o["w_o"] = np.ascontiguousarray(wo.reshape(2, NJ, P, KT, P).transpose(3, 2, 0, 1, 4).reshape(KT, P, -1))
    o["w_out"] = wt(a["w_out"][0], 512)
    o["final_g"] = np.ascontiguousarray(np.broadcast_to(a["final_g"], (P, D_MODEL)))
    o["row_sel"] = np.ascontiguousarray(np.concatenate([np.arange(9)[:, None] == np.full(P, 8), np.arange(9)[:, None] == np.arange(NS) // NT], 1).astype(f))


OUTS = [("y_prompt", (1, SEQ, D_MODEL)), ("y_sample", (NB, NT, D_MODEL)),
        ("cmp_p", (1, 1, SEQ, 2, 2, HD)), ("sel_p", (1, 1, SEQ, 2, 2, HD)), ("win_p", (1, 1, WIN, 2, 2, HD)),
        ("conv_p", (P, 12, 3)), ("gdn_p", (P, NJ, HD)),
        ("cmp_s", (1, NB, NT, 2, 2, HD)), ("sel_s", (1, NB, NT, 2, 2, HD)), ("win_s", (1, NB, WIN, 2, 2, HD)),
        ("conv_s", (P, 12, NB, 3)), ("gdn_s", (P, NJ, NB, HD))]


def kernel(**inputs):
    import concourse.bacc as bacc
    from concourse.bass_utils import run_bass_kernel_spmd

    arrays = layouts(inputs)
    nc = bacc.Bacc("TRN2", target_bir_lowering=False, num_devices=1)
    ins = {k: nc.dram_tensor(f"in_{k}", v.shape, mybir.dt.from_np(v.dtype), kind="ExternalInput").ap() for k, v in arrays.items()}
    outs = {k: nc.dram_tensor(f"out_{k}", s, F32, kind="ExternalOutput").ap() for k, s in OUTS}
    build(nc, ins, outs)
    r = run_bass_kernel_spmd(nc, [{f"in_{k}": v for k, v in arrays.items()}], core_ids=[0]).results[0]
    y = {k: r[f"out_{k}"] for k, _ in OUTS}
    conv_p = y["conv_p"].transpose(2, 1, 0).reshape(1, 1, 3, 1536)
    conv_s = y["conv_s"].transpose(2, 3, 1, 0).reshape(1, NB, 3, 1536)
    gdn_p = y["gdn_p"].reshape(2, HD, NJ, HD).transpose(2, 0, 1, 3).reshape(1, 1, H, HD, HD)
    gdn_s = y["gdn_s"].reshape(2, HD, NJ, NB, HD).transpose(3, 2, 0, 1, 4).reshape(1, NB, H, HD, HD)
    return (y["y_prompt"], y["y_sample"], y["cmp_p"], y["sel_p"], y["win_p"], conv_p, gdn_p,
            y["cmp_s"], y["sel_s"], y["win_s"], conv_s, gdn_s)
```

```python
from contextlib import ExitStack

import numpy as np

import concourse.bass as bass
from concourse import mybir

F32 = mybir.dt.float32
I32 = mybir.dt.int32
ALU = mybir.AluOpType
ACT = mybir.ActivationFunctionType
AX = mybir.AxisListType.X

P = 128
D_MODEL = 1024
SEQ = 1024
NB, NT = 8, 4
NS = NB * NT
TOK = SEQ + NS
KT = D_MODEL // P
TB = TOK // 3
QT = SEQ // P
H, HD = 8, 64
NJ = H // 2
PAGE = 128
NPAGE = 1024 // PAGE
NPOOL = NB * NPAGE * 5 // 4
NCMP = 63
NSEQ = NB + 1
WIN = 512
NG, SG = 2, 4
KVG = 6 * P + 24 + 16
KVH = KVG // 2
A_OFF, B_OFF = 6 * P + 24, 6 * P + 32
RS = 32
NEG = -1.0e30
GUARD = 1.0e25
TINY = 1.17549435e-38
EPS = 1e-6
CW = 1083


def stage_input(nc, T):
    with ExitStack() as ctx:
        sb = lambda n, s, d=F32: ctx.enter_context(nc.sbuf_tensor(n, s, d))
        sem = lambda n: ctx.enter_context(nc.semaphore(n))
        cT = sb("cT", [P, KT, 9])
        wa = [b[:].rearrange("p a k s n -> p (a k s n)").rearrange("p (k n) -> p k n", k=KT) for b in T["xc"]]
        wa.append(T["kvt"][:].rearrange("p t c -> p (t c)")[:, 0:KT * 512].rearrange("p (k n) -> p k n", k=KT))
        bada = sb("bada", [9, 3072])
        gT = sb("gT", [P, KT])
        sq = [T["qT"][:, n, :] for n in range(2)]
        rstd = T["qT"][:, 2, :]
        modA = sb("modA", [P, KT, 9])
        modB = sb("modB", [P, KT, 9])
        adaP = ctx.enter_context(nc.psum_tensor("adaP", [P, 2, 512], F32))
        sumP = ctx.enter_context(nc.psum_tensor("sumP", [P, 3, 512], F32))
        trP = ctx.enter_context(nc.psum_tensor("trP", [P, 512], F32))
        ld_c, ld_x, ld_b = sem("ld_c"), [sem("ld_x0"), sem("ld_x1")], sem("ld_b")
        ld_wa = [sem(f"ld_wa{i}") for i in range(3)]
        silu_ready, sq_ready, sq_used = sem("silu_ready"), sem("sq_ready"), sem("sq_used")
        ada_prod, ada_ready, ada_t, mod_ready = sem("ada_prod"), sem("ada_ready"), sem("ada_t"), sem("mod_ready")
        inv_ready, rstd_ready, dve_step = sem("inv_ready"), sem("rstd_ready"), sem("dve_step")
        shsc = T["zaT"][0:9].rearrange("p j t -> p (j t)")[:, 0:2 * D_MODEL]
        hT, gate, ones, ident = T["hT"], T["gate"], T["ones"], T["ident"]
        ada = [(shsc, n * 512) for n in range(4)] + [(gate, n * 512) for n in range(2)]

        with nc.Block() as block:
            @block.sync
            def _(sp):
                sp.dma_start(cT[:], T["in"]["cT"]).then_inc(ld_c, 16)
                for k in range(KT):
                    sp.dma_start(hT[:, k, :], T["in"]["xT"][:, k, :]).then_inc(ld_x[k % 2], 16)
                sp.dma_start(ident[:], T["in"]["ident"]).then_inc(ld_b, 16)
                sp.dma_start(bada[:], T["in"]["b_ada"]).then_inc(ld_b, 16)
                sp.dma_start(gT[:], T["in"]["norm_gT"]).then_inc(ld_b, 16)
                for n in range(6):
                    if n >= 3:
                        sp.wait_ge(ada_prod, n - 2)
                    sp.dma_start(wa[n % 3], T["in"]["w_ada"][n].rearrange("p (k n) -> p k n", k=KT)).then_inc(ld_wa[n % 3], 16)
                for n in range(2):
                    sp.dma_start(T["wt"][n], T["in"]["w_tok"][n].rearrange("p (k n) -> p k n", k=KT)).then_inc(T["ld_wt"], 16)
                sp.dma_start(T["pages"][:], T["in"]["pages"]).then_inc(T["ld_pg"], 16)
                sp.wait_ge(ld_b, 48)

            @block.scalar
            def _(act):
                act.wait_ge(ld_c, 16)
                act.activation(cT[:], cT[:], ACT.Silu).then_inc(silu_ready, 1)
                for n in range(2):
                    act.wait_ge(ld_x[n], 16 * KT // 2)
                for k in range(KT):
                    if k >= 2:
                        act.wait_ge(sq_used, k - 1)
                    act.activation(sq[k % 2], hT[:, k, :], ACT.Square).then_inc(sq_ready, 1)
                act.wait_ge(inv_ready, 1)
                act.activation(rstd, rstd, ACT.Sqrt).then_inc(rstd_ready, 1)

            @block.tensor
            def _(pe):
                pe.wait_ge(dve_step, 1)
                for k in range(KT):
                    pe.wait_ge(sq_ready, k + 1)
                    for b in range(3):
                        mm = pe.matmul(sumP[:, b, 0:TB], ones[:], sq[k % 2][:, b * TB:(b + 1) * TB],
                                       start=(k == 0), stop=(k == KT - 1))
                    mm.then_inc(sq_used, 1)
                pe.wait_ge(silu_ready, 1)
                for n in range(6):
                    if n == 4:
                        pe.wait_ge(ada_ready, 4)
                        pe.wait_ge(ld_b, 48)
                        for k in range(16):
                            mm = pe.transpose(trP[:, k * 9:k * 9 + 9], shsc[:, k * P:(k + 1) * P], ident[0:9, 0:9])
                        mm.then_inc(ada_t, 1)
                    pe.wait_ge(ld_wa[n % 3], 16 * (n // 3 + 1))
                    if n >= 2:
                        pe.wait_ge(ada_ready, n - 1)
                    for k in range(KT):
                        mm = pe.matmul(adaP[0:9, n % 2, :], cT[:, k, :], wa[n % 3][:, k, :],
                                       start=(k == 0), stop=(k == KT - 1))
                    mm.then_inc(ada_prod, 1)

            @block.vector
            def _(dve):
                dve.memset(ones[:], 1.0).then_inc(dve_step, 1)
                dve.wait_ge(sq_used, KT)
                dve.tensor_scalar(rstd.rearrange("p (b t) -> p b t", b=3), sumP[:, :, 0:TB], 1.0 / D_MODEL, EPS, ALU.mult, ALU.add).then_inc(dve_step, 1)
                dve.wait_ge(dve_step, 2)
                dve.reciprocal(rstd, rstd).then_inc(inv_ready, 1)
                dve.wait_ge(ld_b, 48)
                def ada_rows(n):
                    dve.wait_ge(ada_prod, n + 1)
                    dst, at = ada[n]
                    dve.tensor_tensor(dst[:, at:at + 512], adaP[0:9, n % 2, :],
                                      bada[:, n * 512:(n + 1) * 512], ALU.add).then_inc(ada_ready, 1)
                for n in range(4):
                    ada_rows(n)
                dve.wait_ge(ada_t, 1)
                dve.tensor_copy(modB[:], trP[:, 0:72].rearrange("p (k r) -> p k r", k=KT)).then_inc(mod_ready, 1)
                dve.tensor_scalar(modA[:], trP[:, 72:144].rearrange("p (k r) -> p k r", k=KT), 1.0, None, ALU.add).then_inc(mod_ready, 1)
                dve.wait_ge(mod_ready, 2)
                dve.tensor_tensor(modA[:], modA[:], gT[:].unsqueeze(2).to_broadcast([P, KT, 9]), ALU.mult).then_inc(mod_ready, 1)
                dve.wait_ge(rstd_ready, 1)
                dve.wait_ge(mod_ready, 3)
                for k in range(KT):
                    dve.tensor_tensor(hT[:, k, :], hT[:, k, :], rstd, ALU.mult).then_inc(dve_step, 1)
                dve.wait_ge(dve_step, 2 + KT)
                for k in range(KT):
                    dve.tensor_scalar(hT[:, k, 0:SEQ], hT[:, k, 0:SEQ], modA[:, k, 8:9], modB[:, k, 8:9], ALU.mult, ALU.add)
                    hs = hT[:, k, SEQ:TOK].rearrange("p (b t) -> p b t", b=NB)
                    dve.tensor_tensor(hs, hs, modA[:, k, 0:NB].unsqueeze(2).to_broadcast([P, NB, NT]), ALU.mult).then_inc(dve_step, 1)
                dve.wait_ge(dve_step, 2 + 2 * KT)
                for k in range(KT):
                    hs = hT[:, k, SEQ:TOK].rearrange("p (b t) -> p b t", b=NB)
                    dve.tensor_tensor(hs, hs, modB[:, k, 0:NB].unsqueeze(2).to_broadcast([P, NB, NT]), ALU.add)
                for n in (4, 5):
                    ada_rows(n)


def product_features(pe, out, w, x, ft):
    for k in range(KT):
        for b in range(3):
            mm = pe.matmul(out[:, b, 0:TB], w[:, k, ft * P:(ft + 1) * P], x[:, k, b * TB:(b + 1) * TB],
                           start=(k == 0), stop=(k == KT - 1))
    return mm


def load_pairs(eng, T, pair, half, pages):
    for p in pages:
        page = eng.value_load(T["pages"][0:1, bass.ds(pair * (2 * NPAGE) + p, 1)], min_val=0, max_val=NPOOL - 1)
        eng.dma_start(T["xc"][half][:, p], T["in"]["cmp_pool"][bass.ds(page, 1)].rearrange("a p (k s n) -> (a p) k s n", k=2, s=16)).then_inc(T["ld_x"][half], 16)


def load_pages(eng, T, G, first, count, dst, pool, loaded):
    with eng.Fori(first, first + count) as i:
        page = eng.value_load(T["pages"][0:1, bass.ds(i + G * SG * NPAGE, 1)], min_val=0, max_val=NPOOL - 1)
        eng.dma_start(dst[:].rearrange("p b n t -> p (b n) t")[:, bass.ds(i, 1), :], pool[bass.ds(page, 1)].rearrange("a p t -> p a t")).then_inc(loaded, 16)


def stage_nsa_project(nc, T):
    with ExitStack() as ctx:
        sb = lambda n, s, d=F32: ctx.enter_context(nc.sbuf_tensor(n, s, d))
        sem = lambda n: ctx.enter_context(nc.semaphore(n))
        w = [sb(f"w{i}", [P, KT, 256]) for i in range(2)]
        wt, ld_wt, ld_pg = T["wt"], T["ld_wt"], T["ld_pg"]
        featP = [ctx.enter_context(nc.psum_tensor(f"featP{i}", [P, 3, 512], F32)) for i in range(2)]
        tokP = ctx.enter_context(nc.psum_tensor("tokP", [P, 2, 512], F32))
        ld_w = [sem(f"ld_w{i}") for i in range(2)]
        feat_prod, feat_out = sem("feat_prod"), sem("feat_out")
        tok_prod, tok_out, ab_clear = sem("tok_prod"), sem("tok_out"), sem("ab_clear")
        hT, kvt = T["hT"], T["kvt"]
        dests = [(2 * blk + n, dst, 2 * n, fn, scale) for blk, dst, fn, scale in
                 ((0, T["qT"], ACT.Copy, HD ** -0.5), (1, T["zaT"], ACT.Silu, 1.0)) for n in range(2)]
        tiles = [(t, h) for t in range(QT + 1) for h in range(2)]

        with nc.Block() as block:
            @block.sync
            def _(sp):
                for n, (blk, _, _, _, _) in enumerate(dests):
                    if n == 2:
                        sp.wait_ge(tok_prod, len(tiles))
                        for kv in range(2):
                            sp.dma_start(T["w1"][:, kv], T["in"]["cmp_w1"][:, kv]).then_inc(T["ld_w1"], 16)
                        sp.wait_ge(ld_pg, 16)
                        for half in range(2):
                            load_pairs(sp, T, half, half, range(2 * NPAGE))
                    if n >= 2:
                        sp.wait_ge(feat_prod, 2 * (n - 1))
                    sp.dma_start(w[n % 2][:], T["in"]["w_feat"][blk].rearrange("p (k n) -> p k n", k=KT)).then_inc(ld_w[n % 2], 16)

            @block.tensor
            def _(pe):
                pe.wait_ge(ld_wt, 32)
                for n, (t, h) in enumerate(tiles):
                    m = P if t < QT else NS
                    if n >= 2:
                        pe.wait_ge(tok_out, n - 1)
                    for k in range(KT):
                        mm = pe.matmul(tokP[0:m, n % 2, 0:KVH], hT[:, k, t * P:t * P + m], wt[h][:, k, :],
                                       start=(k == 0), stop=(k == KT - 1))
                    mm.then_inc(tok_prod, 1)
                for n in range(len(dests)):
                    pe.wait_ge(ld_w[n % 2], 16 * (n // 2 + 1))
                    for ft in range(2):
                        u = 2 * n + ft
                        if u >= 2:
                            pe.wait_ge(feat_out, u - 1)
                        mm = product_features(pe, featP[u % 2], w[n % 2], hT, ft)
                        mm.then_inc(feat_prod, 1)

            @block.vector
            def _(dve):
                for n, (t, h) in enumerate(tiles):
                    m = P if t < QT else NS
                    dve.wait_ge(tok_prod, n + 1)
                    dve.tensor_copy(kvt[0:m, t, h * KVH:(h + 1) * KVH], tokP[0:m, n % 2, 0:KVH]).then_inc(tok_out, 1)
                dve.memset(T["ab_t"][:], 0.0).then_inc(ab_clear, 1)
                dve.wait_ge(ab_clear, 1)
                dve.wait_ge(tok_out, len(tiles))
                dve.tensor_copy(T["ab_t"][:, 0:QT, :], kvt[:, 0:QT, A_OFF:KVG])
                dve.tensor_copy(T["ab_t"][0:NS, QT, :], kvt[0:NS, QT, A_OFF:KVG])

            @block.scalar
            def _(act):
                for n, (_, dst, at, fn, scale) in enumerate(dests):
                    for ft in range(2):
                        u = 2 * n + ft
                        act.wait_ge(feat_prod, u + 1)
                        act.activation(dst[:, at + ft, :].rearrange("p (b t) -> p b t", b=3), featP[u % 2][:, :, 0:TB],
                                       fn, scale=scale).then_inc(feat_out, 1)


def stage_compress(nc, T):
    with ExitStack() as ctx:
        sb = lambda n, s, d=F32: ctx.enter_context(nc.sbuf_tensor(n, s, d))
        sem = lambda n: ctx.enter_context(nc.semaphore(n))
        w1 = T["w1"]
        w2 = sb("cw2", [P, 2, P])
        bias = sb("bias", [P, 2])
        hs = [sb(f"hs{i}", [P, 2, 127]) for i in range(2)]
        cmpT = sb("cmpT", [P, 2, SEQ + RS])
        trP = ctx.enter_context(nc.psum_tensor("trP2", [P, 2, 512], F32))
        preP = ctx.enter_context(nc.psum_tensor("preP", [P, 2, 512], F32))
        kvP = ctx.enter_context(nc.psum_tensor("kvP", [P, 2, 512], F32))
        ld_w = sem("ld_cw")
        xc, ld_x = T["xc"], T["ld_x"]
        kv_t, kv_copied, bias_ready = sem("kv_t"), sem("kv_copied"), sem("bias_ready")
        pre_prod, hs_ready, cmp_prod, cmp_ready = sem("pre_prod"), sem("hs_ready"), sem("cmp_prod"), sem("cmp_ready")
        kvt, kvT, kcT, vc, ident = T["kvt"], T["kvT"], T["kcT"], T["vc"], T["ident"]
        BLK = [0, 1, 2, 4]

        with nc.Block() as block:
            @block.sync
            def _(sp):
                sp.dma_start(w2[:], T["in"]["cmp_w2"]).then_inc(ld_w, 16)
                sp.dma_start(cmpT[:, :, SEQ:SEQ + RS], T["in"]["cmp_pe"]).then_inc(ld_w, 16)
                for half in range(2):
                    sp.wait_ge(pre_prod, half + 2)
                    load_pairs(sp, T, 2 + half, half, range(NPAGE))

            @block.tensor
            def _(pe):
                for t in range(QT + 1):
                    m = P if t < QT else NS
                    if t >= 2:
                        pe.wait_ge(kv_copied, t - 1)
                    for n, c in list(enumerate(BLK))[0 if t < QT else 2:]:
                        mm = pe.transpose(trP[:, t % 2, n * P:n * P + m], kvt[0:m, t, c * P:(c + 1) * P], ident[0:m, 0:m])
                    mm.then_inc(kv_t, 1)
                pe.wait_ge(ld_w, 32)
                pe.wait_ge(T["ld_w1"], 32)
                def conv(src, s, n):
                    for kv in range(2):
                        for r in range(2):
                            for t in range(16):
                                mm = pe.matmul(preP[:, s, kv * 256 + 1 - r:kv * 256 + n + 1 - r], w1[:, kv, r * 16 + t, :], src(kv, t),
                                               start=(r == 0 and t == 0), stop=(r == 1 and t == 15), skip_group_check=True)
                    return mm

                def up(s, seqs):
                    n = 64 * seqs - 1
                    pe.matmul(kvP[:, s, 0:n], w2[:, 0, :], hs[s][:, 0, 0:n])
                    for a in range(seqs):
                        mm = pe.matmul(kvP[0:NCMP, s, (a + 1) * 128:(a + 2) * 128], hs[s][:, 1, a * 64:a * 64 + NCMP], w2[:, 1, :])
                    return mm

                pe.wait_ge(kv_copied, QT + 1)
                conv(lambda kv, t: cmpT[:, kv, t:SEQ + RS:16], 0, 66).then_inc(pre_prod, 1)
                pe.wait_ge(hs_ready, 1)
                up(0, 1).then_inc(cmp_prod, 1)
                with pe.Fori(0, NB // 4) as i:
                    for half in range(2):
                        pe.wait_ge(ld_x[half], i * (32 * NPAGE) + 32 * NPAGE)
                        conv(lambda kv, t: xc[half][:, :, kv, t, :], 1 - half, 128).then_inc(pre_prod, 1)
                    pe.wait_ge(cmp_ready, i * 2 + 1)
                    for half in range(2):
                        pe.wait_ge(hs_ready, i * 2 + half + 2)
                        up(1 - half, 2).then_inc(cmp_prod, 1)

            @block.scalar
            def _(act):
                def silus(s, seqs):
                    n = 64 * seqs - 1
                    for kv in range(2):
                        ins = act.activation(hs[s][:, kv, 0:n], preP[:, s, kv * 256 + 1:kv * 256 + 1 + n], ACT.Silu, bias=bias[:, kv:kv + 1])
                    return ins
                act.wait_ge(pre_prod, 1)
                for kv in range(2):
                    b_ = act.activation(bias[:, kv:kv + 1], preP[:, 0, kv * 256 + 65:kv * 256 + 66], ACT.Copy)
                b_.then_inc(bias_ready, 1)
                act.wait_ge(bias_ready, 1)
                silus(0, 1).then_inc(hs_ready, 1)
                for u in range(1, NB // 2 + 1):
                    act.wait_ge(pre_prod, u + 1)
                    if u >= 2:
                        act.wait_ge(cmp_prod, u - 1)
                    silus(u % 2, 2).then_inc(hs_ready, 1)
                    if u <= 2:
                        load_pairs(act, T, u + 1, u - 1, range(NPAGE, 2 * NPAGE))

            @block.vector
            def _(dve):
                for t in range(QT + 1):
                    m = P if t < QT else NS
                    dve.wait_ge(kv_t, t + 1)
                    tr = trP[:, t % 2, :].rearrange("p (n t) -> p n t", n=4)
                    if t < QT:
                        dve.tensor_copy(cmpT[:, :, t * P:t * P + m], tr[:, 0:2, :])
                    dve.tensor_copy(kvT[:, :, t * P:t * P + m], tr[:, 2:4, 0:m]).then_inc(kv_copied, 1)
                dve.wait_ge(cmp_prod, 1)
                dve.tensor_copy(kcT[:, NB, 0:NCMP], kvP[:, 0, 0:NCMP])
                dve.tensor_copy(vc[:, NB, :], kvP[0:NCMP, 0, 128:256]).then_inc(cmp_ready, 1)
                with dve.Fori(0, NB // 4) as i:
                    for half in range(2):
                        dve.wait_ge(cmp_prod, i * 2 + half + 2)
                        b, p_ = i * 4 + 2 * half, kvP[:, 1 - half]
                        dve.tensor_copy(kcT[:, bass.ds(b, 2), 0:NCMP], p_[:, 0:128].rearrange("p (a n) -> p a n", a=2)[:, :, 0:NCMP])
                        dve.tensor_copy(vc[:, bass.ds(b, 2), :], p_[0:NCMP, 128:384].rearrange("p (a n) -> p a n", a=2)).then_inc(cmp_ready, 1)


def stage_sample_attention(nc, T):
    HALF = SG * NPAGE // 2
    NK = PAGE * NPAGE
    VG = 18
    with ExitStack() as ctx:
        sb = lambda n, s, d=F32: ctx.enter_context(nc.sbuf_tensor(n, s, d))
        sem = lambda n: ctx.enter_context(nc.semaphore(n))
        qs = sb("qs", [P, NB, 2, NJ, NT])
        tab = sb("tab", [P, 1840])
        sel = sb("sel", [NS, 2, P])
        kS, vS, ld_k, ld_v = T["kS"], T["vS"], T["ld_k"], T["ld_v"]
        kW = sb("kW", [P, SG, WIN])
        vW = sb("vW", [P, SG, 4, P])
        sc = sb("sc", [P, 63 + 1056 + 544])
        pT = sb("pT", [P, 15, P])
        sm = sb("sm", [P, 64])
        gts = sb("gts", [NS, 24])
        g3 = sb("g3", [P, 3, H])
        imp_r = sb("imp_r", [P, 16])
        drop = sb("drop", [P, 3, 16])
        oz = sb("oz", [P, 2, HD])
        half_o = sb("half_o", [P, SG, NJ, NT])
        scoreP = ctx.enter_context(nc.psum_tensor("scoreP", [P, 4, 512], F32))
        ptP = ctx.enter_context(nc.psum_tensor("ptP", [P, 2, 512], F32))
        oP = ctx.enter_context(nc.psum_tensor("oP", [P, 512], F32))
        miscP = ctx.enter_context(nc.psum_tensor("miscP", [P, 512], F32))
        qs_zero, qs_ready, ld_t = sem("qs_zero"), sem("qs_ready"), sem("ld_tab")
        ld_kw, ld_vw, ld_k2, ld_v2 = sem("ld_kw"), sem("ld_vw"), sem("ld_k2"), sem("ld_v2")
        gate_sig, gate_row, cmp_s, sel_s = sem("gate_sig"), sem("gate_row"), sem("cmp_s"), sem("sel_s")
        v, e, pt_ready, pt_out, o_done, imp_p = sem("v"), sem("e"), sem("pt_ready"), sem("pt_out"), sem("o_done"), sem("imp_p")
        dve_step = sem("dve_step2")
        ident, kvt, kvT, kcT, vc, zaT = T["ident"], T["kvt"], T["kvT"], T["kcT"], T["vc"], T["zaT"]
        qTs = T["qT"]
        c_cmp, c_sel, c_win, c_new, c_map, c_agg, c_hm, c_io, c_m = 0, 63, 1087, 1599, 1663, 1679, 1807, 1815, 1831
        C, S0, S1, W0, W1 = 0, 63, 63 + 1024, 63 + 1056, 63 + 1056 + 512
        END = W1 + 32

        with nc.Block() as block:
            @block.sync
            def _(sp):
                sp.dma_start(sel[:], T["in"]["token_sel"]).then_inc(ld_t, 16)
                sp.dma_start(tab[:], T["in"]["sample_tab"]).then_inc(ld_t, 16)
                for G in range(NG):
                    if G:
                        sp.wait_ge(sel_s, 1)
                        load_pages(sp, T, G, 0, HALF, kS, T["in"]["sel_k"], ld_k)
                    sp.dma_start(kW[:], T["in"]["win_k"][G].rearrange("p (b t) -> p b t", b=SG)).then_inc(ld_kw, 16)
                    if G:
                        sp.wait_ge(o_done, 1)
                        load_pages(sp, T, G, 0, HALF, vS, T["in"]["sel_v"], ld_v)
                sp.wait_ge(ld_t, 32)

            @block.gpsimd
            def _(po):
                po.memset(qs[:], 0.0).then_inc(qs_zero, 1)
                po.wait_ge(qs_zero, 1)
                for g in range(2):
                    r = slice(g * HD, (g + 1) * HD)
                    po.tensor_copy(qs[r, :, g].rearrange("p b j t -> p j b t"), qTs[r, :, SEQ:TOK].rearrange("p j (b t) -> p j b t", b=NB)).then_inc(qs_ready, 1)
                for G in range(NG):
                    if G:
                        po.wait_ge(sel_s, 1)
                        load_pages(po, T, G, HALF, HALF, kS, T["in"]["sel_k"], ld_k2)
                        po.wait_ge(o_done, 1)
                    po.dma_start(vW[:], T["in"]["win_v"][G].rearrange("p (b n c) -> p b n c", b=SG, n=4)).then_inc(ld_vw, 16)
                    if G:
                        load_pages(po, T, G, HALF, HALF, vS, T["in"]["sel_v"], ld_v2)

            @block.tensor
            def _(pe):
                npt = 0
                pe.wait_ge(qs_ready, 2)
                pe.wait_ge(ld_t, 32)
                for G in range(NG):
                    lhs = lambda b: qs[:, G * SG + b].rearrange("p g j t -> p (g j t)")
                    lhs_all = qs[:, G * SG:(G + 1) * SG].rearrange("p b g j t -> p (b g j t)")
                    pe.wait_ge(gate_sig, 1)
                    pe.matmul(miscP[:, 0:24], sel[:, G, :], gts[:, :]).then_inc(gate_row, 1)
                    for b in range(SG):
                        pe.matmul(scoreP[32 * b:32 * b + 32, 0, 0:NCMP], lhs(b), kcT[:, G * SG + b, 0:NCMP])
                    pe.matmul(scoreP[:, 0, 64:96], lhs_all, kvT[:, 0, SEQ:TOK])
                    pe.matmul(scoreP[:, 0, 96:128], lhs_all, kvT[:, 1, SEQ:TOK]).then_inc(cmp_s, 1)
                    pe.wait_ge(ld_k, 16 * (SG * NPAGE + G * HALF))
                    if G:
                        pe.wait_ge(ld_k2, 16 * HALF)
                    pe.wait_ge(ld_kw, (G + 1) * 16)
                    for b in range(SG):
                        for n in range(2):
                            pe.matmul(scoreP[32 * b:32 * b + 32, 1 + n, :], lhs(b), kS[:, b, 4 * n:4 * n + 4, :].rearrange("p n t -> p (n t)"))
                        mm = pe.matmul(scoreP[32 * b:32 * b + 32, 3, :], lhs(b), kW[:, b, :])
                    mm.then_inc(sel_s, 1)
                    pe.wait_ge(v, VG * G + 3)
                    pe.transpose(ptP[0:NCMP, 0, 0:P], sc[:, C:C + NCMP], ident[:]).then_inc(pt_ready, 1)
                    pe.wait_ge(pt_out, 5 * G + 1)
                    for b in range(SG):
                        pe.matmul(oP[32 * b:32 * b + 32, 0:P], pT[0:NCMP, 0, 32 * b:32 * b + 32], vc[:, G * SG + b, :])
                    pe.matmul(miscP[:, 32:48], pT[0:NCMP, 0, :], tab[0:NCMP, c_map:c_map + 16]).then_inc(imp_p, 1)
                    pe.wait_ge(v, VG * G + 4)
                    pe.matmul(miscP[:, 64:80], tab[:, c_agg:c_agg + P], imp_r[:]).then_inc(imp_p, 1)
                    pe.wait_ge(e, 3 * G + 2)
                    for grp in range(2):
                        for n in range(4):
                            mm = pe.transpose(ptP[:, 1 - grp, n * P:(n + 1) * P], sc[:, S0 + (4 * grp + n) * P:S0 + (4 * grp + n + 1) * P], ident[:])
                        mm.then_inc(pt_ready, 1)
                    pe.wait_ge(pt_out, 5 * G + 2)
                    pe.wait_ge(e, 3 * G + 3)
                    for n in range(4):
                        mm = pe.transpose(ptP[:, 1, n * P:(n + 1) * P], sc[:, W0 + n * P:W0 + (n + 1) * P], ident[:])
                    mm.then_inc(pt_ready, 1)
                    pe.wait_ge(pt_out, 5 * G + 3)
                    pe.transpose(ptP[0:NS, 0, 0:P], sc[:, S1:S1 + NS], ident[:])
                    pe.transpose(ptP[0:NS, 0, P:2 * P], sc[:, W1:W1 + NS], ident[:]).then_inc(pt_ready, 1)
                    pe.wait_ge(pt_out, 5 * G + 5)
                    pe.wait_ge(ld_v, 16 * (SG * NPAGE + G * HALF))
                    if G:
                        pe.wait_ge(ld_v2, 16 * HALF)
                    pe.wait_ge(ld_vw, (G + 1) * 16)
                    for b in range(SG):
                        c = slice(32 * b, 32 * b + 32)
                        for n in range(8):
                            pe.matmul(oP[c, P:2 * P], pT[:, 1 + n, c], vS[:, b, n, :], start=(n == 0), stop=False, skip_group_check=True)
                        pe.matmul(oP[c, P:2 * P], pT[0:NS, 9, c], kvt[0:NS, QT, 3 * P:4 * P], start=False, stop=True, skip_group_check=True)
                        for n in range(4):
                            pe.matmul(oP[c, 2 * P:3 * P], pT[:, 10 + n, c], vW[:, b, n, :], start=(n == 0), stop=False, skip_group_check=True)
                        mm = pe.matmul(oP[c, 2 * P:3 * P], pT[0:NS, 14, c], kvt[0:NS, QT, 5 * P:6 * P], start=False, stop=True, skip_group_check=True)
                    mm.then_inc(o_done, 1)
                    pe.wait_ge(v, VG * G + 17)
                    pe.transpose(miscP[:, P:2 * P], oz[:].rearrange("p g d -> p (g d)"), ident[:]).then_inc(o_done, 1)
                    pe.wait_ge(v, VG * G + 18)

            @block.scalar
            def _(act):
                act.activation(gts[:], kvt[0:NS, QT, 6 * P:6 * P + 24], ACT.Sigmoid).then_inc(gate_sig, 1)
                for G in range(NG):
                    act.wait_ge(v, VG * G + 1)
                    act.activation(sc[:, C:C + NCMP], sc[:, C:C + NCMP], ACT.Exp, bias=sm[:, 0:1], accum_out=sm[:, 1:2]).then_inc(e, 1)
                    act.wait_ge(v, VG * G + 5)
                    act.activation(sc[:, S0:W0], sc[:, S0:W0], ACT.Exp, bias=sm[:, 2:3], accum_out=sm[:, 3:4]).then_inc(e, 1)
                    act.wait_ge(v, VG * G + 6)
                    act.activation(sc[:, W0:END], sc[:, W0:END], ACT.Exp, bias=sm[:, 4:5], accum_out=sm[:, 5:6]).then_inc(e, 1)
                    for k, (m, dst, src) in enumerate([
                            (P, pT[:, 1:5, :], ptP[:, 1, :].rearrange("p (n t) -> p n t", n=4)),
                            (P, pT[:, 5:9, :], ptP[:, 0, :].rearrange("p (n t) -> p n t", n=4)),
                            (P, pT[:, 10:14, :], ptP[:, 1, :].rearrange("p (n t) -> p n t", n=4)),
                            (NS, pT[0:NS, 9:15:5, :], ptP[0:NS, 0, 0:2 * P].rearrange("p (n t) -> p n t", n=2))]):
                        act.wait_ge(pt_ready, 5 * G + 2 + k)
                        act.activation(dst, src, ACT.Copy).then_inc(pt_out, 1)

            @block.vector
            def _(dve):
                linked = [0]
                def link(ins, wait=True):
                    ins.then_inc(dve_step, 1)
                    linked[0] += 1
                    if wait:
                        dve.wait_ge(dve_step, linked[0])
                dve.wait_ge(ld_t, 32)
                for G in range(NG):
                    n_v = [VG * G]
                    def done(ins):
                        ins.then_inc(v, 1)
                        n_v[0] += 1
                    def settle():
                        dve.wait_ge(v, n_v[0])
                    dve.wait_ge(cmp_s, G + 1)
                    dve.wait_ge(gate_row, G + 1)
                    link(dve.tensor_tensor(sc[:, C:C + NCMP], scoreP[:, 0, 0:NCMP], tab[:, c_cmp:c_cmp + NCMP], ALU.add))
                    done(dve.tensor_reduce(sm[:, 0:1], sc[:, C:C + NCMP], AX, ALU.max, negate=True))
                    link(dve.tensor_tensor(g3[:], miscP[:, 0:24].rearrange("p (h c) -> p c h", c=3), tab[:, c_hm:c_hm + H].unsqueeze(1).to_broadcast([P, 3, H]), ALU.mult))
                    link(dve.tensor_reduce(sm[:, 10:13], g3[:], AX, ALU.add))
                    dve.wait_ge(e, 3 * G + 1)
                    done(dve.reciprocal(sm[:, 6:7], sm[:, 1:2]))
                    settle()
                    link(dve.tensor_scalar(sc[:, C:C + NCMP], sc[:, C:C + NCMP], sm[:, 6:7], None, ALU.mult))
                    done(dve.scalar_tensor_tensor(sc[:, C:C + NCMP], sc[:, C:C + NCMP], TINY, sc[:, C:C + NCMP], ALU.is_ge, ALU.mult))
                    dve.wait_ge(pt_ready, 5 * G + 1)
                    dve.tensor_copy(pT[0:NCMP, 0, :], ptP[0:NCMP, 0, 0:P]).then_inc(pt_out, 1)
                    dve.wait_ge(imp_p, 2 * G + 1)
                    done(dve.tensor_copy(imp_r[:], miscP[:, 32:48]))
                    dve.wait_ge(imp_p, 2 * G + 2)
                    imp = miscP[:, 65:79]
                    link(dve.tensor_reduce(sm[:, 7:8], imp, AX, ALU.min))
                    link(dve.scalar_tensor_tensor(drop[:, 0, 0:14], imp, sm[:, 7:8], tab[:, c_io + 1:c_io + 15], ALU.is_equal, ALU.mult))
                    link(dve.tensor_reduce(sm[:, 8:9], drop[:, 0, 0:14], AX, ALU.max))
                    link(dve.tensor_scalar(drop[:, 1, :], tab[:, c_io:c_io + 16], sm[:, 8:9], NEG, ALU.is_equal, ALU.mult))
                    dve.wait_ge(sel_s, G + 1)
                    link(dve.tensor_tensor(sc[:, S0:S1].rearrange("p (b n) -> p b n", b=2), scoreP[:, 1:3, :], tab[:, c_sel:c_sel + NK].rearrange("p (b n) -> p b n", b=2), ALU.add), wait=False)
                    link(dve.tensor_tensor(sc[:, S1:W0], scoreP[:, 0, 64:96], tab[:, c_new + 32 * G:c_new + 32 * G + 32], ALU.add))
                    s3 = sc[:, S0:S1].rearrange("p (b n) -> p b n", b=16)
                    link(dve.tensor_tensor(s3, s3, drop[:, 1, :].unsqueeze(2).to_broadcast([P, 16, 64]), ALU.add))
                    done(dve.tensor_reduce(sm[:, 2:3], sc[:, S0:W0], AX, ALU.max, negate=True))
                    link(dve.tensor_tensor(sc[:, W0:W1], scoreP[:, 3, :], tab[:, c_win:c_win + WIN], ALU.add), wait=False)
                    link(dve.tensor_tensor(sc[:, W1:END], scoreP[:, 0, 96:128], tab[:, c_new + 32 * G:c_new + 32 * G + 32], ALU.add))
                    done(dve.tensor_reduce(sm[:, 4:5], sc[:, W0:END], AX, ALU.max, negate=True))
                    dve.wait_ge(e, 3 * G + 3)
                    done(dve.reciprocal(sm[:, 13:14], sm[:, 3:4]))
                    done(dve.reciprocal(sm[:, 14:15], sm[:, 5:6]))
                    settle()
                    done(dve.tensor_tensor(sm[:, 11:13], sm[:, 11:13], sm[:, 13:15], ALU.mult))
                    settle()
                    done(dve.tensor_scalar(sm[:, 16:19], sm[:, 10:13], tab[:, c_m:c_m + 1], None, ALU.mult))
                    done(dve.tensor_scalar(sm[:, 19:22], sm[:, 10:13], tab[:, c_m + 1:c_m + 2], None, ALU.mult))
                    settle()
                    dve.wait_ge(o_done, 2 * G + 1)
                    for c in range(3):
                        for g in range(2):
                            src, k = oP[:, c * P + g * HD:c * P + (g + 1) * HD], sm[:, 16 + 3 * g + c:17 + 3 * g + c]
                            if c == 0:
                                done(dve.tensor_scalar(oz[:, g, :], src, k, None, ALU.mult))
                            else:
                                done(dve.scalar_tensor_tensor(oz[:, g, :], src, k, oz[:, g, :], ALU.mult, ALU.add))
                        if c < 2:
                            settle()
                    dve.wait_ge(o_done, 2 * G + 2)
                    ot = miscP[:, P:2 * P].rearrange("p (b g j t) -> p g b j t", b=SG, g=2, j=NJ)
                    link(dve.tensor_copy(half_o[:], ot[:, 0]))
                    link(dve.tensor_tensor(half_o[:], half_o[:], ot[:, 1], ALU.add))
                    zs = zaT[:, :, SEQ + G * SG * NT:SEQ + (G + 1) * SG * NT].rearrange("p j (b t) -> p b j t", b=SG)
                    done(dve.tensor_tensor(zs, zs, half_o[:], ALU.mult))
                    assert n_v[0] == VG * (G + 1)
                    settle()


def stage_prompt_attention(nc, T):
    UN = 4
    W_MAX = WIN + P
    unit_kind = [0, 1, 0, 1]
    unit_g = [0, 0, 1, 1]

    def width(i):
        return min((i + 1) * P, W_MAX)

    def slots(i, kind):
        if kind == 0:
            return [(0, n * P, P, n) for n in range(i + 1)]
        k0 = (i + 1) - width(i) // P
        return [(1, n * P, P, k0 + n) for n in range(width(i) // P)] + [(2, W_MAX, NCMP, None)]

    def groups(i, kind):
        s = slots(i, kind)
        cut = 3 if len(s) == 5 and kind else 2 if len(s) == 4 and not kind else 4
        return [x for x in (s[:cut], s[cut:8], s[8:]) if x]

    flats = [[(u, n, grp) for u in range(UN) for n, grp in enumerate(groups(i, unit_kind[u]))] for i in range(QT)]
    NPT = [len(f) for f in flats]
    assert all(n % 4 == 0 for n in NPT)
    G0 = [NJ * sum(NPT[:i]) for i in range(QT + 1)]

    def through(i, u):
        return sum(1 for v, _, _ in flats[i] if v <= u)

    def count(q, per, n):
        i, s, a = q
        return s * per + (per * (NJ * i + a) + n)

    def group(q, k):
        i, s, a = q
        return G0[i] + k if i == QT else s * NPT[i] + (G0[i] + a * NPT[i] + k)

    def following(q):
        i, s, a = q
        if isinstance(s, int) and s + a == NJ - 1:
            return (i + 1, 0, 0) if i + 1 < QT else None
        return (i, s, a + 1)

    def wait(eng, sem, n):
        if not isinstance(n, int) or n > 0:
            eng.wait_ge(sem, n)

    def each_pair(eng, body, tile_end=lambda i: None):
        for i in range(QT):
            if i == 0:
                for s in range(NJ - 1):
                    body((i, s, 0))
            else:
                with eng.Fori(0, NJ - 1) as s:
                    body((i, s, 0))
            body((i, NJ - 1, 0))
            tile_end(i)

    first = lambda q: q[0] == 0 and q[1] + q[2] == 0

    with ExitStack() as ctx:
        sb = lambda n, s, d=F32: ctx.enter_context(nc.sbuf_tensor(n, s, d))
        sem = lambda n: ctx.enter_context(nc.semaphore(n))
        dist = sb("dist", [P, SEQ])
        dist_w = sb("dist_w", [P, P])
        dist_c = sb("dist_c", [P, QT, 64])
        slope = sb("slope", [P, H])
        gates = sb("gates", [P, QT, NJ, 2, 3])
        qb = [sb(f"qb{g}", [P, P]) for g in range(2)]
        ss = [sb(f"ss{i}", [P, SEQ]) for i in range(UN)]
        pT = [sb(f"ppT{i}", [P, 4, P]) for i in range(4)]
        nm = sb("nm", [P, UN, 2])
        sums = [sb(f"sums{g}", [P, 3]) for g in range(2)]
        coef = [sb(f"coef{g}", [P, 3]) for g in range(2)]
        tmp = sb("otmp", [P, 3, HD])
        ot = sb("ot", [P, P])
        oz = sb("ozt", [P, NJ, P])
        sP = [ctx.enter_context(nc.psum_tensor(f"sP{i}", [P, 2, 512], F32)) for i in range(2)]
        tP = ctx.enter_context(nc.psum_tensor("tP", [P, 2, 512], F32))
        oP = ctx.enter_context(nc.psum_tensor("poP", [P, 2, 512], F32))
        ld_t, gate_ready, q_ready, q_zero, st_kv = sem("ld_d"), sem("gate_ready"), sem("q_ready"), sem("q_zero"), sem("st_kv")
        score_prod, score_read, max_ready, p_ready = sem("score_prod"), sem("score_read"), sem("max_ready"), sem("p_ready")
        pt_ready, pt_out, pv_done = sem("ppt_ready"), sem("ppt_out"), sem("pv_done")
        o_read, o_ready, o_turned, z_done = sem("o_read"), sem("o_ready"), sem("o_turned"), sem("z_done")
        guard, coef_step = sem("guard"), sem("coef_step")
        kvt, kvT, kcT, vc, qT, zaT, ident = T["kvt"], T["kvT"], T["kcT"], T["vc"], T["qT"], T["zaT"], T["ident"]

        with nc.Block() as block:
            @block.sync
            def _(sp):
                sp.dma_start(dist[:], T["in"]["dist"]).then_inc(ld_t, 16)
                sp.dma_start(dist_w[:], T["in"]["dist_w"]).then_inc(ld_t, 16)
                sp.dma_start(dist_c[:], T["in"]["dist_c"]).then_inc(ld_t, 16)
                sp.dma_start(slope[:], T["in"]["slope"]).then_inc(ld_t, 16)
                load_pages(sp, T, 0, 0, SG * NPAGE, T["kS"], T["in"]["sel_k"], T["ld_k"])
                load_pages(sp, T, 0, 0, SG * NPAGE, T["vS"], T["in"]["sel_v"], T["ld_v"])
                o, sel = T["out"], lambda c: slice(c * 2 * P, (c + 1) * 2 * P)
                rows = lambda ap: ap.rearrange("a b t k g d -> (a b t) (k g d)")
                sp.dma_start(rows(o["cmp_p"]).rearrange("(n p) c -> p n c", p=P), kvt[:, 0:QT, sel(0)]).then_inc(st_kv, 16)
                sp.dma_start(rows(o["sel_p"]).rearrange("(n p) c -> p n c", p=P), kvt[:, 0:QT, sel(1)]).then_inc(st_kv, 16)
                sp.dma_start(rows(o["win_p"]).rearrange("(n p) c -> p n c", p=P), kvt[:, QT // 2:QT, sel(2)]).then_inc(st_kv, 16)
                sp.dma_start(rows(o["cmp_s"]), kvt[0:NS, QT, sel(0)]).then_inc(st_kv, 16)
                sp.dma_start(rows(o["sel_s"]), kvt[0:NS, QT, sel(1)]).then_inc(st_kv, 16)
                win = o["win_s"].rearrange("a b t k g d -> (a b) t (k g d)")
                for b in range(NB):
                    sp.dma_start(win[b, WIN - NT:WIN, :], kvt[b * NT:(b + 1) * NT, QT, sel(2)]).then_inc(st_kv, 16)
                sp.dma_start(win[:, 0:WIN - NT, :], T["in"]["cache_win"][:, NT:WIN, :]).then_inc(st_kv, 16)
                sp.wait_ge(st_kv, 16 * (6 + NB))
                sp.wait_ge(ld_t, 64)

            @block.gpsimd
            def _(po):
                for q_ in qb:
                    x = po.memset(q_[:], 0.0)
                x.then_inc(q_zero, 1)
                po.wait_ge(q_zero, 1)
                def body(q):
                    i, s, a = q
                    for g in range(2):
                        r = slice(g * HD, (g + 1) * HD)
                        wait(po, score_prod, count(q, UN, 2 * g + 2 - UN))
                        po.tensor_copy(qb[g][r, :], qT[r, bass.ds(s + a, 1), i * P:(i + 1) * P]).then_inc(q_ready, 1)
                each_pair(po, body)

            @block.tensor
            def _(pe):
                def scores(q, u):
                    i = q[0]
                    g, dst = unit_g[u], sP[u % 2]
                    if u % 2 == 0:
                        pe.wait_ge(q_ready, count(q, 2, g + 1))
                    wait(pe, score_read, count(q, UN, u - 1))
                    n = (i + 1) * P if unit_kind[u] == 0 else width(i)
                    k0 = (i + 1) * P - n
                    for c in range(0, n, 512):
                        m = min(512, n - c)
                        mm = pe.matmul(dst[:, c // 512, 0:m], qb[g][:], kvT[:, unit_kind[u], k0 + c:k0 + c + m])
                    if unit_kind[u]:
                        mm = pe.matmul(dst[:, 1, P:P + NCMP], qb[g][:], kcT[:, NB, 0:NCMP])
                    mm.then_inc(score_prod, 1)

                def turn(q, k):
                    u, n, grp = flats[q[0]][k]
                    if n == 0:
                        pe.wait_ge(p_ready, count(q, UN, u + 1))
                    wait(pe, pt_out, group(q, k - 1))
                    for m, (_, c, keys, _) in enumerate(grp):
                        mm = pe.transpose(tP[0:keys, k % 2, m * P:(m + 1) * P], ss[u][:, c:c + keys], ident[:])
                    mm.then_inc(pt_ready, 1)

                def values(q, k):
                    i = q[0]
                    u, n, grp = flats[i][k]
                    g = unit_g[u]
                    pe.wait_ge(pt_out, group(q, k + 1))
                    if u % 2 == 0 and n == 0:
                        wait(pe, o_read, count(q, 2, g - 1))
                        if g:
                            wait(pe, z_done, count(q, 1, 0))
                    for m, (br, c, keys, tile) in enumerate(grp):
                        v = vc[:, NB, :] if br == 2 else kvt[:, tile, (3 + 2 * br) * P:(4 + 2 * br) * P]
                        start = br == 2 or c == 0
                        stop = br == 2 or c == ((i + 1) * P if br == 0 else width(i)) - P
                        mm = pe.matmul(oP[:, g, br * P:(br + 1) * P], pT[k % 4][0:keys, m, :], v, start=start, stop=stop)
                    mm.then_inc(pv_done, 1)

                def turn_outputs(ready):
                    pe.wait_ge(o_ready, ready)
                    pe.transpose(oP[:, 1, 3 * P:4 * P], ot[:], ident[:]).then_inc(o_turned, 1)

                def body(q):
                    nxt = following(q)
                    flat = flats[q[0]]
                    for k, (u, n, grp) in enumerate(flat):
                        if n == 0 and u < 2:
                            scores(q, u + 2)
                        elif n == 0 and nxt:
                            scores(nxt, u - 2)
                        turn(q, k)
                        if k:
                            values(q, k - 1)
                        if u == 1 and k + 1 == through(q[0], 1) and not first(q):
                            turn_outputs(count(q, 2, 0))
                    values(q, len(flat) - 1)

                scores((0, 0, 0), 0)
                scores((0, 0, 0), 1)
                each_pair(pe, body)
                turn_outputs(2 * NJ * QT)
                pe.wait_ge(z_done, NJ * QT)

            @block.scalar
            def _(act):
                for i in range(QT):
                    src = kvt[:, i, 6 * P:6 * P + 24].rearrange("p (g j c) -> p g j c", g=2, j=NJ)
                    dst = gates[:, i].rearrange("p j g c -> p g j c")
                    act.activation(dst[:, :, :, 2], src[:, :, :, 0], ACT.Sigmoid)
                    act.activation(dst[:, :, :, 0:2], src[:, :, :, 1:3], ACT.Sigmoid).then_inc(gate_ready, 1)

                def exps(q, u):
                    i, g, b = q[0], unit_g[u], unit_kind[u]
                    act.wait_ge(max_ready, count(q, UN, u + 1))
                    n = (i + 1) * P if b == 0 else width(i)
                    x = act.activation(ss[u][:, 0:n], ss[u][:, 0:n], ACT.Exp, bias=nm[:, u, 0:1], accum_out=sums[g][:, b:b + 1])
                    if b:
                        c = slice(W_MAX, W_MAX + NCMP)
                        x = act.activation(ss[u][:, c], ss[u][:, c], ACT.Exp, bias=nm[:, u, 1:2], accum_out=sums[g][:, 2:3])
                    x.then_inc(p_ready, 1)

                def body(q):
                    nxt = following(q)
                    for k, (u, n, grp) in enumerate(flats[q[0]]):
                        if n == 0 and u < 3:
                            exps(q, u + 1)
                        elif n == 0 and nxt:
                            exps(nxt, 0)
                        act.wait_ge(pt_ready, group(q, k + 1))
                        wait(act, pv_done, group(q, k - 3))
                        full = [x for x in grp if x[0] != 2]
                        if full:
                            x = act.activation(pT[k % 4][:, 0:len(full), :], tP[:, k % 2, 0:len(full) * P].rearrange("p (n t) -> p n t", t=P), ACT.Copy)
                        if len(full) < len(grp):
                            m = len(full)
                            x = act.activation(pT[k % 4][0:NCMP, m, :], tP[0:NCMP, k % 2, m * P:(m + 1) * P], ACT.Copy)
                        x.then_inc(pt_out, 1)
                exps((0, 0, 0), 0)
                each_pair(act, body)

            @block.vector
            def _(dve):
                dve.wait_ge(ld_t, 64)
                dve.wait_ge(gate_ready, QT)

                def biased(q, u):
                    i, s, a = q
                    g, src, dst = unit_g[u], sP[u % 2], ss[u]
                    dve.wait_ge(score_prod, count(q, UN, u + 1))
                    k = slope[:, bass.ds(s * 2 + (2 * a + g), 1)]
                    n = (i + 1) * P if unit_kind[u] == 0 else width(i)
                    flat = src[:].rearrange("p a b -> p (a b)")
                    lo = P if unit_kind[u] and i >= 4 else 0
                    if lo:
                        dve.scalar_tensor_tensor(dst[:, 0:P], dist_w[:], k, flat[:, 0:P], ALU.mult, ALU.add)
                    if unit_kind[u]:
                        dve.scalar_tensor_tensor(dst[:, W_MAX:W_MAX + NCMP], dist_c[:, i, 0:NCMP], k, flat[:, W_MAX:W_MAX + NCMP], ALU.mult, ALU.add)
                    dve.scalar_tensor_tensor(dst[:, lo:n], dist[:, SEQ - n + lo:SEQ], k, flat[:, lo:n], ALU.mult, ALU.add).then_inc(score_read, 1)
                    dve.wait_ge(score_read, count(q, UN, u + 1))
                    if unit_kind[u]:
                        dve.tensor_reduce(nm[:, u, 1:2], dst[:, W_MAX:W_MAX + NCMP], AX, ALU.max, negate=True).then_inc(guard, 1)
                        dve.wait_ge(guard, count(q, 2, g + 1))
                        dve.tensor_scalar(nm[:, u, 1:2], nm[:, u, 1:2], GUARD, None, ALU.min)
                    dve.tensor_reduce(nm[:, u, 0:1], dst[:, 0:n], AX, ALU.max, negate=True).then_inc(max_ready, 1)

                def head(q, g, back, per, n):
                    return count(q, 2 * per, per * (g - 2 * back) + n)

                def weigh(q, g, back):
                    i, s, a = q
                    dve.wait_ge(p_ready, count(q, UN, 2 * g + 2 - UN * back))
                    dve.tensor_scalar(coef[g][:], sums[g][:], 1e-30, None, ALU.max).then_inc(coef_step, 1)
                    dve.wait_ge(coef_step, head(q, g, back, 3, 1))
                    dve.reciprocal(coef[g][:], coef[g][:]).then_inc(coef_step, 1)
                    dve.wait_ge(coef_step, head(q, g, back, 3, 2))
                    gate = gates[:].rearrange("p t j g c -> p (t j) g c")[:, bass.ds(s + (NJ * i + a - back), 1), g, :].rearrange("p a c -> p (a c)")
                    dve.tensor_tensor(coef[g][:], coef[g][:], gate, ALU.mult).then_inc(coef_step, 1)

                def combine(q, g, back):
                    dve.wait_ge(pv_done, group(q, 0 if back else through(q[0], 2 * g + 1)))
                    dve.wait_ge(coef_step, head(q, g, back, 3, 3))
                    o = oP[:, g, 0:3 * P].rearrange("p (c d) -> p c d", d=P)[:, :, g * HD:(g + 1) * HD]
                    dve.tensor_tensor(tmp[:], o, coef[g][:].unsqueeze(2).to_broadcast([P, 3, HD]), ALU.mult).then_inc(o_read, 1)
                    dve.wait_ge(o_read, head(q, g, back, 1, 1))
                    dve.tensor_reduce(ot[:, g * HD:(g + 1) * HD], tmp[:].rearrange("p b d -> p d b"), AX, ALU.add).then_inc(o_ready, 1)

                def body(q):
                    i, s, a = q
                    nxt = following(q)
                    if not first(q):
                        weigh(q, 1, 1)
                        dve.wait_ge(pt_ready, group(q, 0))
                    biased(q, 2)
                    if not first(q):
                        combine(q, 1, 1)
                    biased(q, 3)
                    if not first(q):
                        dve.wait_ge(o_turned, count(q, 1, 0))
                        dve.tensor_copy(oz[:, bass.ds(s + a, 1), :].rearrange("p a c -> p (a c)"), oP[:, 1, 3 * P:4 * P]).then_inc(z_done, 1)
                    weigh(q, 0, 0)
                    if nxt:
                        for u in range(2):
                            dve.wait_ge(pt_ready, group(q, through(i, u)))
                            biased(nxt, u)
                    combine(q, 0, 0)

                def gate_outputs(i):
                    dve.wait_ge(z_done, NJ * (i + 1) - 1)
                    if i:
                        z = zaT[:, NJ - 1, (i - 1) * P:i * P]
                        dve.tensor_tensor(z, z, oz[:, 0, :], ALU.mult)
                    z = zaT[:, 0:NJ - 1, i * P:(i + 1) * P]
                    dve.tensor_tensor(z, z, oz[:, 1:NJ, :], ALU.mult)

                biased((0, 0, 0), 0)
                biased((0, 0, 0), 1)
                each_pair(dve, body, gate_outputs)
                weigh((QT, 0, 0), 1, 1)
                combine((QT, 0, 0), 1, 1)
                dve.wait_ge(o_turned, NJ * QT)
                z = zaT[:, NJ - 1, (QT - 1) * P:QT * P]
                dve.tensor_tensor(z, z, oP[:, 1, 3 * P:4 * P], ALU.mult).then_inc(z_done, 1)


def stage_gdn_project(nc, T):
    with ExitStack() as ctx:
        sb = lambda n, s, d=F32: ctx.enter_context(nc.sbuf_tensor(n, s, d))
        sem = lambda n: ctx.enter_context(nc.semaphore(n))
        NTI = QT + 1
        w = [sb(f"gw{i}", [P, KT, 256]) for i in range(2)]
        raw = [sb(f"raw{i}", [P, CW]) for i in range(2)]
        st = sb("cst", [P, 12, NB, 3])
        cwt = sb("cwt", [P, 12, 5])
        tail = sb("ctail", [P, 12, 3 + 3 * NB])
        sq = sb("gsq", [P, 512])
        ss = sb("gss", [P, NTI, 16])
        ab = sb("gab", [P, 2, H])
        ga = sb("ga", [P, 3, NTI, H])
        fP = [ctx.enter_context(nc.psum_tensor(f"gfP{i}", [P, 3, 512], F32)) for i in range(2)]
        qP = ctx.enter_context(nc.psum_tensor("gqP", [P, 2, 512], F32))
        ld_w, ld_first = [sem(f"gld_w{i}") for i in range(2)], sem("gld_first")
        ld_c, ld_g, prod, z_read, raw_ready, st_ready = sem("gld_c"), sem("gld_g"), sem("gprod"), sem("gz_read"), sem("raw_ready"), sem("gst_ready")
        taps, conv_ready, tail_ready, u_ready, st_out = sem("taps"), sem("conv_ready"), sem("tail_ready"), sem("u_ready"), sem("gst_out")
        turned, copied, sq_ready, ss_ready, root_ready, clear = sem("gturned"), sem("gcopied"), sem("gsq_ready"), sem("gss_ready"), sem("groot"), sem("gclear")
        e, step, norm_step = sem("ge"), sem("gstep"), sem("gnorm_step")
        hT, uT, zbT, ident, qkv, ab_t = T["hT"], T["uT"], T["zbT"], T["ident"], T["qkv"], T["ab_t"]
        NZ, NF = NJ, 12
        blocks = [10, 11] + list(range(4, 10))
        TURN_AFTER = {5: 0, 9: 1}
        rows = lambda t: P if t < QT else NS
        samples = lambda r: r[:, SEQ + 3:CW].rearrange("p (b t) -> p b t", b=NB)

        with nc.Block() as block:
            @block.sync
            def _(sp):
                for n, blk in enumerate(blocks):
                    if n >= 2:
                        sp.wait_ge(prod, 2 * (n - 1))
                    src = T["in"]["w_feat"][blk].rearrange("p (k n) -> p k n", k=KT)
                    if n == 0:
                        sp.dma_start(w[0][:, :, 0:P], src[:, :, 0:P]).then_inc(ld_first, 16)
                        sp.dma_start(w[0][:, :, P:2 * P], src[:, :, P:2 * P]).then_inc(ld_w[0], 16)
                    else:
                        sp.dma_start(w[n % 2][:], src).then_inc(ld_w[n % 2], 16)
                    if n == 1:
                        sp.dma_start(st[:], T["in"]["conv_state"]).then_inc(ld_c, 16)
                        sp.dma_start(cwt[:], T["in"]["conv_w"]).then_inc(ld_c, 16)
                        sp.dma_start(ab[:], T["in"]["gdn_ab"]).then_inc(ld_g, 16)
                sp.wait_ge(tail_ready, NF)
                sp.dma_start(T["out"]["conv_p"], tail[:, :, 0:3]).then_inc(st_out, 16)
                sp.dma_start(T["out"]["conv_s"], tail[:, :, 3:].rearrange("p f (b t) -> p f b t", b=NB)).then_inc(st_out, 16)
                sp.wait_ge(st_out, 32)

            @block.tensor
            def _(pe):
                def turn(c):
                    pe.wait_ge(u_ready, 4 * (c + 1))
                    for t in range(NTI):
                        n, m = NTI * c + t, rows(t)
                        if n >= 2:
                            pe.wait_ge(copied, n - 1)
                        for f in range(4):
                            mm = pe.transpose(qP[0:m, n % 2, f * P:(f + 1) * P], uT[:, 4 * c + f, t * P:t * P + m], ident[:])
                        mm.then_inc(turned, 1)

                for g in range(NZ + NF):
                    if g == 0:
                        pe.wait_ge(ld_first, 16)
                    elif g == 1 or g % 2 == 0:
                        pe.wait_ge(ld_w[g // 2 % 2], 16 * (g // 4 + 1))
                    if g >= NZ + 2:
                        pe.wait_ge(raw_ready, g - NZ - 1)
                    elif g >= 2:
                        pe.wait_ge(z_read, g - 1)
                    product_features(pe, fP[g % 2], w[g // 2 % 2], hT, g % 2).then_inc(prod, 1)
                    if g - NZ in TURN_AFTER:
                        turn(TURN_AFTER[g - NZ])
                turn(2)

            @block.gpsimd
            def _(po):
                for r in raw:
                    po.memset(r[:, 0:3], 0.0)
                po.wait_ge(ld_c, 32)
                for f in range(NF):
                    if f >= 2:
                        po.wait_ge(conv_ready, f - 1)
                    po.tensor_copy(samples(raw[f % 2])[:, :, 0:3], st[:, f]).then_inc(st_ready, 1)
                    po.wait_ge(raw_ready, f + 1)
                    po.tensor_copy(tail[:, f, 0:3], raw[f % 2][:, SEQ:SEQ + 3])
                    po.tensor_copy(tail[:, f, 3:].rearrange("p (b t) -> p b t", b=NB), samples(raw[f % 2])[:, :, 4:7]).then_inc(tail_ready, 1)

            @block.scalar
            def _(act):
                act.wait_ge(ld_g, 16)
                act.activation(ab_t[:, :, H:2 * H], ab_t[:, :, H:2 * H], ACT.Sigmoid).then_inc(e, 1)
                act.activation(ab[:, 1, :], ab[:, 1, :], ACT.Exp).then_inc(e, 1)
                act.wait_ge(step, 1)
                act.activation(ga[:, 1], ga[:, 0], ACT.Abs).then_inc(e, 1)
                act.wait_ge(e, 3)
                act.activation(ga[:, 1], ga[:, 1], ACT.Exp, scale=-1.0).then_inc(e, 1)
                act.wait_ge(step, 2)
                act.activation(ga[:, 1], ga[:, 1], ACT.Ln).then_inc(e, 1)
                for g in range(NZ):
                    act.wait_ge(prod, g + 1)
                    act.activation(zbT[:, g, :].rearrange("p (b t) -> p b t", b=3), fP[g % 2][:, :, 0:TB], ACT.Silu).then_inc(z_read, 1)

                def silu(f):
                    act.wait_ge(conv_ready, f + 1)
                    act.activation(uT[:, f, :], uT[:, f, :], ACT.Silu).then_inc(u_ready, 1)

                def copy_out(c, tiles):
                    for t in tiles:
                        n, m = NTI * c + t, rows(t)
                        act.wait_ge(turned, n + 1)
                        act.activation(qkv[0:m, t, c, :], qP[0:m, n % 2, :], ACT.Copy).then_inc(copied, 1)

                def root(c):
                    act.wait_ge(norm_step, 2 if c == 0 else 5)
                    act.activation(ss[:, :, H * c:H * (c + 1)], ss[:, :, H * c:H * (c + 1)], ACT.Sqrt).then_inc(root_ready, 1)

                for f in range(NF):
                    act.wait_ge(prod, NZ + f + 1)
                    if f >= 2:
                        act.wait_ge(conv_ready, f - 1)
                        act.wait_ge(tail_ready, f - 1)
                    r, p = raw[f % 2], fP[f % 2]
                    act.activation(r[:, 3:3 + 2 * TB].rearrange("p (b t) -> p b t", b=2), p[:, 0:2, 0:TB], ACT.Copy)
                    act.activation(r[:, 3 + 2 * TB:3 + SEQ], p[:, 2, 0:SEQ - 2 * TB], ACT.Copy)
                    act.activation(samples(r)[:, :, 3:7], p[:, 2, SEQ - 2 * TB:TB].rearrange("p (b t) -> p b t", b=NB), ACT.Copy).then_inc(raw_ready, 1)
                    if f:
                        silu(f - 1)
                    if f == 9:
                        root(0)
                    if f in TURN_AFTER:
                        copy_out(TURN_AFTER[f], range(NTI))
                silu(NF - 1)
                copy_out(2, range(6))
                root(1)
                copy_out(2, range(6, NTI))

            @block.vector
            def _(dve):
                dve.memset(ss[:], 1.0).then_inc(clear, 1)
                dve.wait_ge(ld_g, 16)
                dt_bias, a_exp = (ab[:, n, :].unsqueeze(1).to_broadcast([P, NTI, H]) for n in range(2))
                dve.tensor_tensor(ga[:, 0], ab_t[:, :, 0:H], dt_bias, ALU.add).then_inc(step, 1)
                dve.wait_ge(e, 4)
                dve.tensor_scalar(ga[:, 1], ga[:, 1], 1.0, None, ALU.add).then_inc(step, 1)
                dve.tensor_scalar(ga[:, 2], ga[:, 0], 0.0, None, ALU.max).then_inc(step, 1)
                dve.wait_ge(e, 5)
                dve.wait_ge(step, 3)
                dve.tensor_tensor(ga[:, 2], ga[:, 2], ga[:, 1], ALU.add).then_inc(step, 1)
                dve.wait_ge(step, 4)
                dve.scalar_tensor_tensor(ab_t[:, :, 0:H], ga[:, 2], -1.0, a_exp, ALU.mult, ALU.mult)
                dve.wait_ge(clear, 1)
                dve.wait_ge(ld_c, 32)

                def convolve(f):
                    dve.wait_ge(raw_ready, f + 1)
                    dve.wait_ge(st_ready, f + 1)
                    r, o = raw[f % 2], uT[:, f, :]
                    so, sr = o[:, SEQ:TOK].rearrange("p (b t) -> p b t", b=NB), samples(r)
                    for i in range(4):
                        if i == 0:
                            dve.tensor_scalar(o[:, 0:SEQ], r[:, 0:SEQ], cwt[:, f, 0:1], cwt[:, f, 4:5], ALU.mult, ALU.add)
                            x = dve.tensor_scalar(so, sr[:, :, 0:4], cwt[:, f, 0:1], cwt[:, f, 4:5], ALU.mult, ALU.add)
                        else:
                            k = cwt[:, f, i:i + 1]
                            dve.scalar_tensor_tensor(o[:, 0:SEQ], r[:, i:SEQ + i], k, o[:, 0:SEQ], ALU.mult, ALU.add)
                            x = dve.scalar_tensor_tensor(so, sr[:, :, i:i + 4], k, so, ALU.mult, ALU.add)
                        if i < 3:
                            x.then_inc(taps, 1)
                            dve.wait_ge(taps, 3 * f + i + 1)
                    x.then_inc(conv_ready, 1)

                def square_sums(c, t):
                    n, m = NTI * c + t, rows(t)
                    x = qkv[0:m, t, c, :]
                    dve.wait_ge(copied, n + 1)
                    if n:
                        dve.wait_ge(ss_ready, n)
                    dve.tensor_tensor(sq[0:m], x, x, ALU.mult).then_inc(sq_ready, 1)
                    dve.wait_ge(sq_ready, n + 1)
                    dve.tensor_reduce(ss[0:m, t, H * c:H * (c + 1)], sq[0:m].rearrange("p (h d) -> p h d", d=HD), AX, ALU.add).then_inc(ss_ready, 1)

                sums_after = {6: [(0, t) for t in range(3)], 7: [(0, t) for t in range(3, 6)], 8: [(0, t) for t in range(6, NTI)],
                              10: [(1, t) for t in range(6)], 11: [(1, t) for t in range(6, NTI)]}
                def inverse_squares(c):
                    part = ss[:, :, H * c:H * (c + 1)]
                    done = 3 * c
                    dve.wait_ge(ss_ready, (c + 1) * NTI)
                    dve.tensor_scalar(part, part, EPS, None, ALU.add).then_inc(norm_step, 1)
                    dve.wait_ge(norm_step, done + 1)
                    dve.reciprocal(part, part).then_inc(norm_step, 1)

                def normalise(c):
                    dve.wait_ge(root_ready, c + 1)
                    if c == 0:
                        dve.tensor_scalar(ss[:, :, 0:H], ss[:, :, 0:H], HD ** -0.5, None, ALU.mult).then_inc(norm_step, 1)
                        dve.wait_ge(norm_step, 3)
                    for t in range(NTI):
                        m = rows(t)
                        x = qkv[0:m, t, c].rearrange("p (h d) -> p h d", d=HD)
                        dve.tensor_tensor(x, x, ss[0:m, t, H * c:H * (c + 1)].unsqueeze(2).to_broadcast([m, H, HD]), ALU.mult)

                for f in range(NF):
                    convolve(f)
                    if f == 9:
                        normalise(0)
                    for c, t in sums_after.get(f, []):
                        square_sums(c, t)
                    if f == 8:
                        inverse_squares(0)
                inverse_squares(1)
                normalise(1)


def stage_gdn_scan(nc, T):
    with ExitStack() as ctx:
        sb = lambda n, s, d=F32: ctx.enter_context(nc.sbuf_tensor(n, s, d))
        sem = lambda n: ctx.enter_context(nc.semaphore(n))
        ps = lambda n, b: ctx.enter_context(nc.psum_tensor(n, [P, b, 512], F32))
        NTI = QT + 1
        tri = sb("tri", [P, P + NS])
        tot = sb("tot", [NS, P])
        seq = sb("seq", [NS, NB])
        msk = sb("msk", [P, P + NS])
        lvl = sb("lvl", [P, 7, P])
        src = sb("src", [P, 2, 512])
        ags = sb("ags", [P, 16])
        gst = sb("gst", [P, NTI, 3, H])
        gex = sb("gex", [P, NTI, 3, H])
        egc = sb("egc", [P, H])
        dec = sb("dec", [P, H, P])
        kb = sb("kb", [P, 4, 512])
        vb = sb("vb", [P, 512])
        kz = sb("kz", [P, H, P])
        kq = sb("kq", [P, NJ, 2, P])
        ke = sb("ke", [P, 2, NJ, P])
        lt = sb("lt", [P, H, P])
        at = sb("at", [P, H, P])
        x = sb("x", [P, H, P])
        xt = sb("xt", [P, H, P])
        yy = sb("yy", [P, H, P])
        vz = sb("vz", [P, NJ * 256 + P])
        r = sb("r", [P, 512])
        S = sb("S", [P, NJ, P])
        SS = sb("SS", [P, NJ, NB, P])
        eglS = sb("eglS", [P, NJ, NB])
        spreads = [yy, x]
        A, Bk = ps("psA", 4), ps("psB", 4)
        ld, ld_s, clear, st_out = sem("sld"), sem("sld_s"), sem("sclear"), sem("sst_out")
        g_prod, g_read, exp_ready = sem("g_prod"), sem("g_read"), sem("exp_ready")
        src_ready, scaled, scaled_late = sem("src_ready"), sem("scaled"), sem("scaled_late")
        row_prod, dec_part, dec_in, dec_ready = sem("row_prod"), sem("dec_part"), sem("dec_in"), sem("dec_ready")
        t_done, t_out, kk_done, lt_part, lt_ready = (sem(n) for n in ("t_done", "t_out", "kk_done", "lt_part", "lt_ready"))
        mm_done, xt_out, dv_out, chain_mm, chain_ev, s_part = (sem(n) for n in ("mm_done", "xt_out", "dv_out", "chain_mm", "chain_ev", "s_part"))
        step, og_out, state_done, tile_done, at_ready = sem("sstep"), sem("og_out"), sem("state_done"), sem("tile_done"), sem("at_ready")
        qkv, ab_t, ident, ones, og = T["qkv"], T["ab_t"], T["ident"], T["ones"], T["og"]
        pair_rows = [slice(0, HD), slice(HD, P)]
        heads3 = lambda ap: ap.rearrange("p (h d) -> p h d", d=HD)
        one = lambda ap: ap.rearrange("p a h -> p (a h)")

        NL = 6

        def levels_of(smp):
            return 1 if smp else NL

        turn_bank = lambda li, a: a if li else 1 + a
        product_bank = lambda li, a: 2 + a if li else (3, 0)[a]

        def count(t, per, n, ahead=0):
            return t * per + (ahead * per + n)

        def tiles(eng, prepare, body):
            prepare(0, 0, 0, P)
            body(0, 0, P, 0, P)
            with eng.Fori(1, QT - 1) as t:
                body(t, 0, P, 0, P)
            body(QT - 1, 0, P, 1, NS)
            body(QT, 1, NS, 0, 0)

        first_tile = lambda t: isinstance(t, int) and t == 0

        with nc.Block() as block:
            @block.sync
            def _(sp):
                for dst, name in ((tri, "tri"), (tot, "tot"), (seq, "seq"), (msk, "msk"), (lvl, "lvl")):
                    sp.dma_start(dst[:], T["in"][name]).then_inc(ld, 16)
                sp.wait_ge(clear, 4)
                for h2 in range(2):
                    for j in range(NJ):
                        sp.dma_start(SS[pair_rows[h2], j, :, h2 * HD:(h2 + 1) * HD], T["in"]["gdn_state"][pair_rows[h2], j]).then_inc(ld_s, 16)
                sp.wait_ge(tile_done, QT)
                for h2 in range(2):
                    sp.dma_start(T["out"]["gdn_p"][pair_rows[h2]], S[pair_rows[h2], :, h2 * HD:(h2 + 1) * HD]).then_inc(st_out, 16)
                for j in range(NJ):
                    sp.wait_ge(state_done, j + 1)
                    for h2 in range(2):
                        sp.dma_start(T["out"]["gdn_s"][pair_rows[h2], j], SS[pair_rows[h2], j, :, h2 * HD:(h2 + 1) * HD]).then_inc(st_out, 16)
                sp.wait_ge(st_out, 16 * (2 + 2 * NJ))

            @block.gpsimd
            def _(po):
                for t_ in (kz, S, vz):
                    po.memset(t_[:], 0.0).then_inc(clear, 1)
                po.wait_ge(exp_ready, 1)

                def operands(t, ahead, m):
                    i = bass.ds(t + ahead, 1)
                    bc = lambda ap: one(ap).unsqueeze(2).to_broadcast([m, H, HD])
                    k, v = (qkv[0:m, i, c, :].rearrange("p a (h d) -> p (a h) d", d=HD) for c in (1, 2))
                    return k, v, bc(ab_t[0:m, i, H:2 * H]), bc(gex[0:m, i, 2, :])

                def prepare(t, ahead, smp, m):
                    i = bass.ds(t + ahead, 1)
                    if ahead:
                        po.wait_ge(t_done, count(t, 5, 5))
                    po.tensor_copy(ags[0:m], one(ab_t[0:m, i, :])).then_inc(src_ready, 1)
                    po.tensor_copy(egc[0:m], one(gex[0:m, i, 0, :])).then_inc(src_ready, 1)
                    po.tensor_copy(src[0:m], qkv[0:m, i, 0:2, :].rearrange("p a c d -> p (a c) d")).then_inc(src_ready, 1)
                    k, v, beta, e_rest = operands(t, ahead, m)
                    e_gc = egc[0:m].unsqueeze(2).to_broadcast([m, H, HD])
                    po.tensor_tensor(heads3(kb[0:m, 0]), k, beta, ALU.mult).then_inc(scaled, 1)
                    po.wait_ge(src_ready, count(t, 3, 3, ahead))
                    po.tensor_tensor(heads3(kb[0:m, 2]), heads3(src[0:m, 0]), e_gc, ALU.mult).then_inc(scaled, 1)
                    po.wait_ge(scaled, count(t, 3, 1, ahead))
                    po.tensor_tensor(heads3(kb[0:m, 1]), heads3(kb[0:m, 0]), e_gc, ALU.mult).then_inc(scaled, 1)
                    if not ahead:
                        po.memset(SS[:], 0.0).then_inc(clear, 1)

                def body(t, smp, m, smp_next, m_next):
                    if m_next:
                        prepare(t, 1, smp_next, m_next)
                    if not first_tile(t):
                        po.wait_ge(tile_done, t)
                    k, v, beta, e_rest = operands(t, 0, m)
                    po.tensor_tensor(heads3(vb[0:m]), v, beta, ALU.mult).then_inc(scaled_late, 1)
                    po.tensor_tensor(heads3(kb[0:m, 3]), k, e_rest, ALU.mult).then_inc(scaled_late, 1)
                tiles(po, prepare, body)

            @block.tensor
            def _(pe):
                pe.wait_ge(ld, 16 * 5)
                pe.matmul(A[:, 0, 0:64], tri[:, 0:P], ab_t[:, 0:QT, 0:H])
                pe.matmul(A[:, 0, 64:128], ones[:], ab_t[:, 0:QT, 0:H])
                pe.matmul(A[0:NS, 0, 128:136], tri[0:NS, P:P + NS], ab_t[0:NS, QT, 0:H])
                pe.matmul(A[0:NS, 0, 136:144], tot[:, 0:NS], ab_t[0:NS, QT, 0:H])
                for h in range(H):
                    mm = pe.matmul(A[:, 0, 144 + 8 * h:152 + 8 * h], ab_t[0:NS, QT, h:h + 1].to_broadcast([NS, P]), seq[:, :])
                mm.then_inc(g_prod, 1)

                def rows(t, ahead, smp, m):
                    pe.wait_ge(src_ready, count(t, 3, 3, ahead))
                    for h in range(H):
                        mm = pe.matmul(Bk[0:m, 2 + h // 4, h % 4 * P:h % 4 * P + m], ags[0:m, h:h + 1].to_broadcast([m, m]), tri[0:m, smp * P:smp * P + m])
                    mm.then_inc(row_prod, 1)

                def turn(t, ahead, m, ns):
                    from_ = [src[0:m, 1], kb[0:m, 0], src[0:m, 0], kb[0:m, 1], kb[0:m, 2]]
                    for n in ns:
                        if n == 0:
                            pe.wait_ge(scaled, count(t, 3, 3, ahead))
                            pe.wait_ge(dec_in, count(t, 1, 1, ahead))
                        if n >= 2:
                            pe.wait_ge(t_out, count(t, 5, n - 1, ahead))
                        for j in range(NJ):
                            mm = pe.transpose(Bk[:, 2 + n % 2, j * P:j * P + m], from_[n][:, j * P:(j + 1) * P], ident[0:m, 0:m])
                        mm.then_inc(t_done, 1)

                def kk(t, ahead, m, a):
                    pe.wait_ge(t_out, count(t, 5, 5 if a else 3, ahead))
                    for h in range(4 * a, 4 * a + 4):
                        mm = pe.matmul(Bk[0:m, h // 2, h % 2 * 256:h % 2 * 256 + 2 * m], kz[:, h, 0:m], kq[:, h // 2, :, 0:m])
                    mm.then_inc(kk_done, 1)

                def prepare(t, ahead, smp, m):
                    rows(t, ahead, smp, m)
                    turn(t, ahead, m, range(5))
                    kk(t, ahead, m, 0)
                    kk(t, ahead, m, 1)

                def body(t, smp, m, smp_next, m_next):
                    hh = lambda a: range(4 * a, 4 * a + 4)
                    for a in range(2):
                        pe.wait_ge(lt_ready, count(t, 2, 1 + a))
                        for h in hh(a):
                            mm = pe.transpose(A[0:m, turn_bank(0, a), h % 4 * P:h % 4 * P + m], xt[0:m, h, 0:m], ident[0:m, 0:m])
                        mm.then_inc(mm_done, 1)
                    nl = levels_of(smp)
                    for li in range(nl):
                        if li == 0 and not first_tile(t):
                            pe.wait_ge(tile_done, t)
                        for a in range(2):
                            pe.wait_ge(xt_out, count(t, 2 * NL, 2 * li + a + 1))
                            for h in hh(a):
                                mm = pe.matmul(A[0:m, product_bank(li, a), h % 4 * P:h % 4 * P + m], lt[0:m, h, 0:m], x[0:m, h, 0:m])
                            mm.then_inc(mm_done, 1)
                        if li == 0:
                            pe.wait_ge(at_ready, count(t, 2, 2))
                        for a in range(2):
                            pe.wait_ge(dv_out, count(t, 4 * NL, 4 * li + a + 1))
                            for h in hh(a):
                                l_, r_ = (xt, yy) if li < nl - 1 else (yy, xt)
                                mm = pe.matmul(Bk[0:m, a, h % 4 * P:h % 4 * P + m], l_[0:m, h, 0:m], r_[0:m, h, 0:m])
                            mm.then_inc(mm_done, 1)
                        if m_next and li == 0:
                            rows(t, 1, smp_next, m_next)
                        if m_next and 2 <= li <= 4:
                            turn(t, 1, m_next, ((0, 1), (2,), (3, 4))[li - 2])
                        if li < nl - 1:
                            for a in range(2):
                                pe.wait_ge(dv_out, count(t, 4 * NL, 4 * li + 3 + a))
                                for h in hh(a):
                                    mm = pe.transpose(A[0:m, a, h % 4 * P:h % 4 * P + m], x[0:m, h, 0:m], ident[0:m, 0:m])
                                mm.then_inc(mm_done, 1)
                    if not smp:
                        if first_tile(t):
                            pe.wait_ge(clear, 3)
                        else:
                            pe.wait_ge(tile_done, t)
                        for c, bank in ((0, 0), (1, 3)):
                            pe.wait_ge(t_out, count(t, 5, 4 + c))
                            for j in range(NJ):
                                mm = pe.matmul(A[:, bank, j * P:(j + 1) * P], ke[:, c, j], S[:, j], start=(c == 0 or j == 0), stop=(c == 0), skip_group_check=True)
                            mm.then_inc(chain_mm, 1)
                    for a in range(2):
                        pe.wait_ge(dv_out, count(t, 4 * NL, 4 * nl - 1 + a))
                    if smp:
                        pe.wait_ge(clear, 4)
                        pe.wait_ge(ld_s, 16 * 2 * NJ)
                        for c in range(2):
                            for j in range(NJ):
                                if c or j >= 2:
                                    pe.wait_ge(chain_ev, 2 * QT + 4 * c + j - 1)
                                for b in range(2):
                                    mm = pe.matmul(Bk[0:m, 2 * (j % 2) + b, :], ke[:, c, j, 0:m], SS[:, j, 4 * b:4 * b + 4, :].rearrange("p b e -> p (b e)"))
                                mm.then_inc(chain_mm, 1)
                    if m_next:
                        kk(t, 1, m_next, 0)
                    ev = t * 2 + (8 if smp else 0)
                    pe.wait_ge(chain_ev, ev + 1)
                    for h in range(H):
                        mm = pe.matmul(A[0:m, 1 + h // 4, h % 4 * P:(h % 4 + 1) * P], xt[0:m, h, 0:m], r[0:m, h // 2 * P:(h // 2 + 1) * P])
                    mm.then_inc(chain_mm, 1)
                    if m_next:
                        kk(t, 1, m_next, 1)
                    pe.wait_ge(chain_ev, ev + 2)
                    for h in range(H):
                        j = h // 2
                        mm = pe.matmul(A[0:m, 3, j * P:(j + 1) * P], at[0:m, h, 0:m], vz[0:m, h * P:(h + 1) * P],
                                       start=bool(smp and h == 0), stop=True, skip_group_check=True)
                    mm.then_inc(chain_mm, 1)
                    pe.wait_ge(scaled_late, count(t, 2, 2))
                    if not smp:
                        for j in range(NJ):
                            mm = pe.matmul(A[:, 0, j * P:(j + 1) * P], kb[:, 3, j * P:(j + 1) * P],
                                           vz[:, j * 256:j * 256 + 384].rearrange("p (a b) -> p a b", a=2)[:, :, 0:HD])
                        mm.then_inc(chain_mm, 1)
                    else:
                        for j in range(NJ):
                            if j >= 2:
                                pe.wait_ge(state_done, j - 1)
                            pe.wait_ge(chain_ev, 2 * QT + 11 + j)
                            for b in range(2):
                                mm = pe.matmul(Bk[:, 2 * (j % 2) + b, :], kb[0:m, 3, j * P:(j + 1) * P], spreads[j % 2][0:m, 4 * b:4 * b + 4, :].rearrange("p b e -> p (b e)"))
                            mm.then_inc(chain_mm, 1)
                pe.wait_ge(exp_ready, 1)
                tiles(pe, prepare, body)
                pe.wait_ge(tile_done, NTI)

            @block.scalar
            def _(act):
                act.wait_ge(g_read, 3)
                act.activation(gex[:, 0:QT], gst[:, 0:QT], ACT.Exp)
                act.activation(gex[0:NS, QT], gst[0:NS, QT], ACT.Exp)
                for h2 in range(2):
                    e_ = act.activation(eglS[pair_rows[h2]], A[pair_rows[h2], 0, 144:208].rearrange("p (j a b) -> p j a b", a=2, b=NB)[:, :, h2, :], ACT.Exp)
                e_.then_inc(exp_ready, 1)

                def decay(t, ahead, m):
                    act.wait_ge(dec_in, count(t, 1, 1, ahead))
                    act.activation(dec[0:m, :, 0:m], dec[0:m, :, 0:m], ACT.Exp).then_inc(dec_ready, 1)

                def turned(t, ahead, m, ns):
                    four = lambda n: Bk[:, 2 + n % 2, :].rearrange("p (j t) -> p j t", j=NJ)[:, :, 0:m]
                    for n in ns:
                        act.wait_ge(t_done, count(t, 5, n + 1, ahead))
                        if n == 0:
                            act.activation(kz[pair_rows[0], 0:H:2, 0:m], four(0)[pair_rows[0]], ACT.Copy)
                            act.activation(kz[pair_rows[1], 1:H:2, 0:m], four(0)[pair_rows[1]], ACT.Copy).then_inc(t_out, 1)
                            continue
                        dst = {1: kq[:, :, 0, 0:m], 2: kq[:, :, 1, 0:m], 3: ke[:, 0, :, 0:m], 4: ke[:, 1, :, 0:m]}[n]
                        if n >= 3 and ahead:
                            act.wait_ge(chain_mm, count(t, 5, n - 2))
                        act.activation(dst, four(n), ACT.Copy).then_inc(t_out, 1)

                def prepare(t, ahead, smp, m):
                    act.wait_ge(clear, 1)
                    decay(t, ahead, m)
                    turned(t, ahead, m, range(5))

                def body(t, smp, m, smp_next, m_next):
                    for li in range(levels_of(smp)):
                        for a in range(2):
                            act.wait_ge(mm_done, count(t, 6 * NL, 6 * li + a + 1))
                            act.activation((x if li == 0 else xt)[0:m, 4 * a:4 * a + 4, 0:m], A[0:m, turn_bank(li, a), :].rearrange("p (h t) -> p h t", h=4)[:, :, 0:m], ACT.Copy).then_inc(xt_out, 1)
                        if m_next and li == 1:
                            decay(t, 1, m_next)
                        if m_next and li in (2, 3):
                            turned(t, 1, m_next, ((0, 1), (2,))[li - 2])
                    if m_next:
                        turned(t, 1, m_next, (3, 4))
                    if not smp:
                        act.wait_ge(chain_mm, count(t, 5, 4))
                        act.activation(og[:, bass.ds(t, 1), :].rearrange("p a c -> p (a c)"), A[:, 3, :], ACT.Copy).then_inc(og_out, 1)
                tiles(act, prepare, body)

            @block.vector
            def _(dve):
                dve.wait_ge(g_prod, 1)
                g_of = lambda c: gst[:, 0:QT, c, :]
                dve.tensor_copy(g_of(0), A[:, 0, 0:64].rearrange("p (t h) -> p t h", h=H))
                dve.tensor_copy(g_of(1), A[:, 0, 64:128].rearrange("p (t h) -> p t h", h=H))
                dve.tensor_copy(gst[0:NS, QT, 0:2, :], A[0:NS, 0, 128:144].rearrange("p (c h) -> p c h", h=H)).then_inc(g_read, 1)
                dve.wait_ge(g_read, 1)
                dve.tensor_tensor(g_of(2), g_of(1), g_of(0), ALU.subtract).then_inc(g_read, 1)
                dve.tensor_tensor(gst[0:NS, QT, 2, :], gst[0:NS, QT, 1, :], gst[0:NS, QT, 0, :], ALU.subtract).then_inc(g_read, 1)
                dve.wait_ge(ld, 16 * 5)
                dve.wait_ge(clear, 3)
                bch = lambda ap, m, n=4: ap.unsqueeze(1).to_broadcast([m, n, m])

                def decay(t, ahead, smp, m):
                    dve.wait_ge(row_prod, count(t, 1, 1, ahead))
                    for a in range(2):
                        p_ = Bk[0:m, 2 + a, :].rearrange("p (h t) -> p h t", h=4)[:, :, 0:m]
                        gc = one(gst[0:m, bass.ds(t + ahead, 1), 0, 4 * a:4 * a + 4])
                        dve.tensor_tensor(dec[0:m, 4 * a:4 * a + 4, 0:m], p_, gc.unsqueeze(2).to_broadcast([m, 4, m]), ALU.subtract).then_inc(dec_part, 1)
                    dve.wait_ge(dec_part, count(t, 2, 2, ahead))
                    dve.tensor_tensor(dec[0:m, :, 0:m], dec[0:m, :, 0:m], bch(msk[0:m, smp * P:smp * P + m], m, H), ALU.add).then_inc(dec_in, 1)

                def lower(t, ahead, m):
                    dve.wait_ge(dec_ready, count(t, 1, 1, ahead))
                    for a in range(2):
                        hs = slice(4 * a, 4 * a + 4)
                        dve.wait_ge(kk_done, count(t, 2, a + 1, ahead))
                        p_ = Bk[0:m, 2 * a:2 * a + 2, :].rearrange("p b (h c) -> p (b h) c", h=2)
                        dve.tensor_tensor(lt[0:m, hs, 0:m], p_[:, :, 0:m], dec[0:m, hs, 0:m], ALU.mult).then_inc(lt_part, 1)
                        dve.wait_ge(lt_part, count(t, 4, 2 * a + 1, ahead))
                        dve.tensor_tensor(xt[0:m, hs, 0:m], lt[0:m, hs, 0:m], bch(lvl[0:m, 0, 0:m], m), ALU.mult).then_inc(lt_part, 1)
                        dve.wait_ge(lt_part, count(t, 4, 2 * a + 2, ahead))
                        dve.tensor_tensor(xt[0:m, hs, 0:m], bch(ident[0:m, 0:m], m), xt[0:m, hs, 0:m], ALU.subtract).then_inc(lt_ready, 1)

                def attention(t, ahead, m):
                    for a in range(2):
                        hs = slice(4 * a, 4 * a + 4)
                        p_ = Bk[0:m, 2 * a:2 * a + 2, :].rearrange("p b (h c) -> p (b h) c", h=2)
                        dve.tensor_tensor(at[0:m, hs, 0:m], p_[:, :, m:2 * m], dec[0:m, hs, 0:m], ALU.mult).then_inc(at_ready, 1)

                def prepare(t, ahead, smp, m):
                    decay(t, ahead, smp, m)
                    lower(t, ahead, m)
                    attention(t, ahead, m)

                def body(t, smp, m, smp_next, m_next):
                    linked = [0]
                    def link(ins, wait=True):
                        ins.then_inc(step, 1)
                        linked[0] += 1
                        if wait:
                            dve.wait_ge(step, linked[0])
                    nl = levels_of(smp)
                    for li in range(nl):
                        for a in range(2):
                            hs = slice(4 * a, 4 * a + 4)
                            dve.wait_ge(mm_done, count(t, 6 * NL, 6 * li + 3 + a))
                            p_ = A[0:m, product_bank(li, a), :].rearrange("p (h t) -> p h t", h=4)[:, :, 0:m]
                            dve.tensor_tensor(yy[0:m, hs, 0:m], p_, bch(lvl[0:m, 1 + li, 0:m], m), ALU.mult).then_inc(dv_out, 1)
                        for a in range(2):
                            hs = slice(4 * a, 4 * a + 4)
                            dve.wait_ge(mm_done, count(t, 6 * NL, 6 * li + 5 + a))
                            p_ = Bk[0:m, a, :].rearrange("p (h t) -> p h t", h=4)[:, :, 0:m]
                            dst = x if li < nl - 1 else xt
                            dve.tensor_tensor(dst[0:m, hs, 0:m], dst[0:m, hs, 0:m], p_, ALU.subtract).then_inc(dv_out, 1)
                        if m_next and li == 0:
                            decay(t, 1, smp_next, m_next)
                    dve.wait_ge(scaled_late, count(t, 2, 1))
                    if not smp:
                        dve.wait_ge(chain_mm, count(t, 5, 1))
                        dve.tensor_tensor(r[:], vb[:], A[:, 0, :], ALU.subtract).then_inc(chain_ev, 1)
                        dve.wait_ge(chain_mm, count(t, 5, 2))
                        for h2 in range(2):
                            q_ = S[pair_rows[h2], :, h2 * HD:(h2 + 1) * HD]
                            e_ = one(gex[pair_rows[h2], bass.ds(t, 1), 1, h2:H:2])
                            dve.tensor_tensor(q_, q_, e_.unsqueeze(2).to_broadcast([HD, NJ, HD]), ALU.mult).then_inc(s_part, 1)
                        dve.wait_ge(chain_mm, count(t, 5, 3))
                    else:
                        for c in range(2):
                            for j in range(NJ):
                                dve.wait_ge(chain_mm, 5 * QT + 4 * c + j + 1)
                                p_ = Bk[0:m, 2 * (j % 2):2 * (j % 2) + 2, :].rearrange("p c (b e) -> p (c b) e", b=4)
                                dve.tensor_tensor(yy[0:m, 0:NB, :], p_, seq[:, :].unsqueeze(2).to_broadcast([m, NB, P]), ALU.mult).then_inc(chain_ev, 1)
                                dve.wait_ge(chain_ev, 2 * QT + 4 * c + j + 1)
                                dst = r[0:m] if c == 0 else dec[0:m, 0:4, :].rearrange("p a b -> p (a b)")
                                link(dve.tensor_reduce(dst[:, j * P:(j + 1) * P], yy[0:m, 0:NB, :].rearrange("p b e -> p e b"), AX, ALU.add))
                        dve.tensor_tensor(r[0:m], vb[0:m], r[0:m], ALU.subtract).then_inc(chain_ev, 1)
                        dve.wait_ge(chain_mm, 5 * QT + 9)
                    for h2 in range(2):
                        for bk in range(2):
                            p_ = A[0:m, 1 + bk, :].rearrange("p (j a e) -> p j a e", j=2, a=2)[:, :, h2, h2 * HD:(h2 + 1) * HD]
                            z = dve.tensor_copy(vz[0:m, 512 * bk:512 * bk + 512].rearrange("p (j c) -> p j c", j=2)[:, :, h2 * 192:h2 * 192 + HD], p_)
                    z.then_inc(chain_ev, 1)
                    if not smp:
                        lower(t, 1, m_next)
                        dve.wait_ge(s_part, count(t, 2, 2))
                        dve.wait_ge(chain_mm, count(t, 5, 5))
                        dve.wait_ge(og_out, count(t, 1, 1))
                        for h2 in range(2):
                            q_ = S[pair_rows[h2], :, h2 * HD:(h2 + 1) * HD]
                            z = dve.tensor_tensor(q_, q_, A[pair_rows[h2], 0, :].rearrange("p (j e) -> p j e", j=NJ)[:, :, h2 * HD:(h2 + 1) * HD], ALU.add)
                        z.then_inc(tile_done, 1)
                        attention(t, 1, m_next)
                    else:
                        dve.wait_ge(clear, 4)
                        dve.wait_ge(ld_s, 16 * 2 * NJ)
                        dve.wait_ge(chain_mm, 5 * QT + 10)
                        link(dve.tensor_tensor(og[0:m, QT, :], dec[0:m, 0:4, :].rearrange("p a b -> p (a b)"), A[0:m, 3, :], ALU.add), wait=False)
                        def spread(j):
                            if j >= 2:
                                dve.wait_ge(chain_mm, 5 * QT + 9 + j)
                            for a in range(2):
                                z = dve.tensor_tensor(spreads[j % 2][0:m, 0:NB, a * HD:(a + 1) * HD], vz[0:m, j * 256 + a * 192:j * 256 + a * 192 + HD].unsqueeze(1).to_broadcast([m, NB, HD]),
                                                      seq[:, :].unsqueeze(2).to_broadcast([m, NB, HD]), ALU.mult)
                            z.then_inc(chain_ev, 1)
                        spread(0)
                        for j in range(NJ):
                            for h2 in range(2):
                                q_ = SS[pair_rows[h2], j, :, h2 * HD:(h2 + 1) * HD]
                                link(dve.tensor_tensor(q_, q_, eglS[pair_rows[h2], j, :].unsqueeze(2).to_broadcast([HD, NB, HD]), ALU.mult), wait=(h2 == 1))
                            if j + 1 < NJ:
                                spread(j + 1)
                            dve.wait_ge(chain_mm, 5 * QT + 11 + j)
                            for h2 in range(2):
                                q_ = SS[pair_rows[h2], j, :, h2 * HD:(h2 + 1) * HD]
                                p_ = Bk[pair_rows[h2], 2 * (j % 2):2 * (j % 2) + 2, :].rearrange("p c (b e) -> p (c b) e", b=4)[:, :, h2 * HD:(h2 + 1) * HD]
                                z = dve.tensor_tensor(q_, q_, p_, ALU.add)
                            z.then_inc(state_done, 1)
                        dve.wait_ge(state_done, NJ)
                        dve.sem_inc(tile_done, 1)
                tiles(dve, prepare, body)


def stage_gdn_and_output(nc, T):
    with nc.sbuf_tensor("qkv", [P, QT + 1, 3, 512], F32) as qkv:
        T["qkv"] = qkv
        with nc.sbuf_tensor("uT", [P, 12, TOK], F32) as uT:
            T["uT"] = uT
            stage_gdn_project(nc, T)
        T["og"] = qkv[:, :, 0, :]
        stage_gdn_scan(nc, T)
        stage_output(nc, T)


def stage_output(nc, T):
    with ExitStack() as ctx:
        sb = lambda n, s, d=F32: ctx.enter_context(nc.sbuf_tensor(n, s, d))
        sem = lambda n: ctx.enter_context(nc.semaphore(n))
        NTI = QT + 1
        wg = [sb(f"ow{i}", [P, KT, 256]) for i in range(2)]
        wo = [sb(f"oo{i}", [P, 2, NJ, P]) for i in range(2)]
        mT = sb("mT", [P, KT, TOK])
        sg = [sb(f"sg{i}", [P, TOK]) for i in range(2)]
        pr = sb("pr", [P, TOK])
        gP = ctx.enter_context(nc.psum_tensor("ogP", [P, 3, 512], F32))
        oP = ctx.enter_context(nc.psum_tensor("ooP", [P, 3, 512], F32))
        ld_w = [sem(f"old_w{i}") for i in range(2)]
        g_prod, g_out, o_prod, o_out, step = (sem("o" + n) for n in ("g_prod", "g_out", "o_prod", "o_out", "step"))
        hT, zaT, zbT = T["hT"], T["zaT"], T["zbT"]
        nsq = [sb(f"nsq{i}", [P, 512]) for i in range(2)]
        nss = sb("nss", [P, NTI, H])
        gn = sb("gn", [P, HD])
        turnP = ctx.enter_context(nc.psum_tensor("turnP", [P, 2, 512], F32))
        ld_n, sq_ready, ss_ready, root_ready, normed, turned, z_done, norm_step = (sem("n" + x) for x in ("ld", "sq_ready", "ss_ready", "root", "normed", "turned", "z_done", "step"))
        ld_wf = sem("ld_wf")
        og, ident = T["og"], T["ident"]
        freed = T["qkv"][:].rearrange("p t c n -> p (t c n)")
        wf = freed[:, 0:KT * D_MODEL].rearrange("p (k n) -> p k n", k=KT)
        gt, fg, gs, *xr = (freed[:, (KT + n) * D_MODEL:(KT + n + 1) * D_MODEL] for n in range(5))
        gs = gs[0:NS]
        sel = sb("osel", [9, P + NS])
        gate, gate_prod, gate_ready = T["gate"], sem("gate_prod"), sem("ogate_ready")
        ld_first, ld_xr = sem("old_first"), [sem("ld_xr0"), sem("ld_xr1")]
        rows = lambda t: P if t < QT else NS
        U = 2 * KT
        with nc.Block() as block:
            @block.sync
            def _(sp):
                for f in range(KT):
                    if f == 1:
                        sp.dma_start(gn[:], T["in"]["gdn_norm"]).then_inc(ld_n, 16)
                        sp.dma_start(sel[:], T["in"]["row_sel"]).then_inc(ld_n, 16)
                    if f == 2:
                        sp.wait_ge(ld_n, 32)
                        sp.wait_ge(turned, NTI)
                        for n in range(2):
                            sp.dma_start(wf[:, :, n * 512:(n + 1) * 512], T["in"]["w_out"][n].rearrange("p (k n) -> p k n", k=KT)).then_inc(ld_wf, 16)
                        sp.dma_start(fg, T["in"]["final_g"]).then_inc(ld_wf, 16)
                        for t in range(2):
                            sp.dma_start(xr[t], T["in"]["x"][t * P:(t + 1) * P, :]).then_inc(ld_xr[t], 16)
                    if f >= 2:
                        sp.wait_ge(o_prod, 2 * (f - 1))
                    g_src = T["in"]["w_gm"][f].rearrange("p (k n) -> p k n", k=KT)
                    o_src = T["in"]["w_o"][f].rearrange("p (c k n) -> p c k n", c=2, k=NJ)
                    if f == 0:
                        for c, loaded in ((0, ld_first), (1, ld_w[0])):
                            sp.dma_start(wg[0][:, :, c * P:(c + 1) * P], g_src[:, :, c * P:(c + 1) * P]).then_inc(loaded, 16)
                            sp.dma_start(wo[0][:, c], o_src[:, c]).then_inc(loaded, 16)
                    else:
                        sp.dma_start(wg[f % 2][:], g_src).then_inc(ld_w[f % 2], 16)
                        sp.dma_start(wo[f % 2][:], o_src).then_inc(ld_w[f % 2], 16)

            @block.tensor
            def _(pe):
                def turn_outputs():
                    for t in range(NTI):
                        m = rows(t)
                        pe.wait_ge(normed, t + 1)
                        if t >= 2:
                            pe.wait_ge(z_done, t - 1)
                        for j in range(NJ):
                            mm = pe.transpose(turnP[:, t % 2, j * P:j * P + m], og[0:m, t, j * P:(j + 1) * P], ident[0:m, 0:m])
                        mm.then_inc(turned, 1)
                    pe.wait_ge(z_done, NTI)

                for u in range(U):
                    f, c = u // 2, u % 2
                    if u == 0:
                        pe.wait_ge(ld_first, 32)
                    elif u == 1 or c == 0:
                        pe.wait_ge(ld_w[f % 2], 32 * (f // 2 + 1))
                    if u:
                        pe.wait_ge(g_out, u)
                    product_features(pe, gP, wg[f % 2], hT, c).then_inc(g_prod, 1)
                    if u == 1:
                        turn_outputs()
                    if u in (4, 6):
                        m, at = ((P, 0), (NS, P))[u // 2 - 2]
                        if u == 4:
                            pe.wait_ge(ld_n, 32)
                        else:
                            pe.wait_ge(gate_ready, 1)
                        for c_ in range(2):
                            mm = pe.matmul(turnP[0:m, c_, :], sel[:, at:at + m], gate[:, c_ * 512:(c_ + 1) * 512])
                        mm.then_inc(gate_prod, 1)
                    if u:
                        pe.wait_ge(o_out, u)
                    src = (zaT, zbT)[c]
                    for k in range(NJ):
                        for b in range(3):
                            mm = pe.matmul(oP[:, b, 0:TB], wo[f % 2][:, c, k, :], src[:, k, b * TB:(b + 1) * TB], start=(k == 0), stop=(k == NJ - 1))
                    mm.then_inc(o_prod, 1)

            @block.scalar
            def _(act):
                for t in range(NTI):
                    m = rows(t)
                    if t >= 2:
                        act.wait_ge(ss_ready, t - 1)
                    act.activation(nsq[t % 2][0:m], og[0:m, t, :], ACT.Square).then_inc(sq_ready, 1)
                act.wait_ge(norm_step, 3)
                act.activation(nss[:], nss[:], ACT.Sqrt).then_inc(root_ready, 1)
                for u in range(U):
                    act.wait_ge(g_prod, u + 1)
                    if u >= 2:
                        act.wait_ge(o_out, u - 1)
                    act.activation(sg[u % 2][:].rearrange("p (b t) -> p b t", b=3), gP[:, :, 0:TB], ACT.Sigmoid).then_inc(g_out, 1)

            @block.vector
            def _(dve):
                def finish(t):
                    m = rows(t)
                    dve.wait_ge(turned, t + 1)
                    z = zbT[:, :, t * P:t * P + m]
                    dve.tensor_tensor(z, z, turnP[:, t % 2, :].rearrange("p (j t) -> p j t", j=NJ)[:, :, 0:m], ALU.mult).then_inc(z_done, 1)

                dve.memset(nss[:], 1.0).then_inc(norm_step, 1)
                dve.wait_ge(norm_step, 1)
                for t in range(NTI):
                    m = rows(t)
                    dve.wait_ge(sq_ready, t + 1)
                    dve.tensor_reduce(nss[0:m, t, :], nsq[t % 2][0:m].rearrange("p (h d) -> p h d", d=HD), AX, ALU.add).then_inc(ss_ready, 1)
                dve.wait_ge(ss_ready, NTI)
                dve.tensor_scalar(nss[:], nss[:], 1.0 / HD, EPS, ALU.mult, ALU.add).then_inc(norm_step, 1)
                dve.wait_ge(norm_step, 2)
                dve.reciprocal(nss[:], nss[:]).then_inc(norm_step, 1)
                dve.wait_ge(root_ready, 1)
                dve.wait_ge(ld_n, 32)
                for t in range(NTI):
                    m = rows(t)
                    x = og[0:m, t, :].rearrange("p (h d) -> p h d", d=HD)
                    dve.tensor_tensor(x, x, nss[0:m, t].unsqueeze(2).to_broadcast([m, H, HD]), ALU.mult).then_inc(norm_step, 1)
                    dve.wait_ge(norm_step, 4 + t)
                    dve.tensor_tensor(x, x, gn[0:m].unsqueeze(1).to_broadcast([m, H, HD]), ALU.mult).then_inc(normed, 1)

                for u in range(U):
                    f, c = u // 2, u % 2
                    if u == 1:
                        for t in range(NTI):
                            finish(t)
                    dve.wait_ge(g_out, u + 1)
                    dve.wait_ge(o_prod, u + 1)
                    if u in (5, 7):
                        m, dst = ((P, gt), (NS, gs))[u // 2 - 2]
                        dve.wait_ge(gate_prod, u // 2 - 1)
                        dve.tensor_copy(dst.rearrange("p (c n) -> p c n", c=2), turnP[0:m, 0:2, :]).then_inc(gate_ready, 1)
                    dst = mT[:, f, :] if c == 0 else pr[:]
                    dve.tensor_tensor(dst.rearrange("p (b t) -> p b t", b=3), oP[:, :, 0:TB], sg[u % 2][:].rearrange("p (b t) -> p b t", b=3), ALU.mult).then_inc(o_out, 1)
                    if c:
                        dve.wait_ge(o_out, u + 1)
                        dve.tensor_tensor(mT[:, f, :], mT[:, f, :], pr[:], ALU.add).then_inc(step, 1)
                        dve.wait_ge(step, f + 1)

        with ExitStack() as ctx2:
            sb = lambda n, s, d=F32: ctx2.enter_context(nc.sbuf_tensor(n, s, d))
            sem = lambda n: ctx2.enter_context(nc.semaphore(n))
            rs = sb("ors", [P, NTI])
            y_prod, y_out, ms_ready, st2, q_ready, root = (sem("y" + n) for n in ("prod", "out", "ms", "step", "sq", "root"))
            st_y = [sem("yst_0"), sem("yst_1")]
            y_dram = lambda t: T["out"]["y_prompt"][0, t * P:(t + 1) * P, :] if t < QT else T["out"]["y_sample"].rearrange("b t d -> (b t) d")
            bank = lambda t: (gP if t % 2 == 0 else oP)
            with nc.Block() as block:
                @block.sync
                def _(sp):
                    for t in range(2, NTI):
                        sp.wait_ge(st_y[t % 2], 16 * (t // 2))
                        sp.dma_start(xr[t % 2][0:rows(t)], T["in"]["x"][t * P:t * P + rows(t), :]).then_inc(ld_xr[t % 2], 16)

                @block.scalar
                def _(act):
                    for t in range(NTI):
                        m = rows(t)
                        act.wait_ge(y_out, t + 1)
                        act.activation(pr[0:m, 0:D_MODEL], xr[t % 2][0:m], ACT.Square, accum_out=rs[0:m, t:t + 1]).then_inc(q_ready, 1)
                        act.wait_ge(st2, 4 * t + 2)
                        act.activation(rs[0:m, t:t + 1], rs[0:m, t:t + 1], ACT.Sqrt).then_inc(root, 1)
                        act.wait_ge(st2, 4 * t + 4)
                        act.dma_start(y_dram(t), xr[t % 2][0:m]).then_inc(st_y[t % 2], 16)
                    act.wait_ge(st_y[0], 16 * ((NTI + 1) // 2))
                    act.wait_ge(st_y[1], 16 * (NTI // 2))

                @block.tensor
                def _(pe):
                    pe.wait_ge(ld_wf, 48)
                    for t in range(NTI):
                        m = rows(t)
                        if t >= 2:
                            pe.wait_ge(y_out, t - 1)
                        for c in range(2):
                            for k in range(KT):
                                mm = pe.matmul(bank(t)[0:m, c, :], mT[:, k, t * P:t * P + m], wf[:, k, c * 512:(c + 1) * 512], start=(k == 0), stop=(k == KT - 1))
                        mm.then_inc(y_prod, 1)

                @block.vector
                def _(dve):
                    dve.wait_ge(ld_wf, 48)
                    for t in range(NTI):
                        m = rows(t)
                        x = xr[t % 2][0:m]
                        dve.wait_ge(y_prod, t + 1)
                        dve.wait_ge(ld_xr[t % 2], 16 * (t // 2 + 1))
                        gate_t = gt if t < QT else gs
                        tmp = sg[t % 2][0:m, 0:D_MODEL]
                        dve.tensor_tensor(tmp.rearrange("p (c n) -> p c n", c=2), bank(t)[0:m, 0:2, :], gate_t[0:m].rearrange("p (c n) -> p c n", c=2), ALU.mult).then_inc(st2, 1)
                        dve.wait_ge(st2, 4 * t + 1)
                        dve.tensor_tensor(x, x, tmp, ALU.add).then_inc(y_out, 1)
                        dve.wait_ge(q_ready, t + 1)
                        dve.tensor_scalar(rs[0:m, t:t + 1], rs[0:m, t:t + 1], 1.0 / D_MODEL, EPS, ALU.mult, ALU.add).then_inc(ms_ready, 1)
                        dve.wait_ge(ms_ready, t + 1)
                        dve.reciprocal(rs[0:m, t:t + 1], rs[0:m, t:t + 1]).then_inc(st2, 1)
                        dve.wait_ge(root, t + 1)
                        dve.tensor_scalar(x, x, rs[0:m, t:t + 1], None, ALU.mult).then_inc(st2, 1)
                        dve.wait_ge(st2, 4 * t + 3)
                        dve.tensor_tensor(x, x, fg[0:m], ALU.mult).then_inc(st2, 1)


def build(nc, ins, outs):
    T = {"in": ins, "out": outs}
    with ExitStack() as ctx:
        def sb(name, shape, dt=F32):
            T[name] = ctx.enter_context(nc.sbuf_tensor(name, shape, dt))
        sb("hT", [P, KT, TOK])
        sb("pages", [1, NB * NPAGE], I32)
        sb("gate", [9, D_MODEL])
        sb("ones", [P, P])
        sb("ident", [P, P])
        sb("zaT", [P, NJ, TOK])
        sb("zbT", [P, NJ, TOK])
        sb("ab_t", [P, QT + 1, 16])
        with ExitStack() as nsa:
            for name, shape in (("qT", [P, NJ, TOK]), ("kvt", [P, QT + 1, KVG])):
                T[name] = nsa.enter_context(nc.sbuf_tensor(name, shape, F32))
            place = T["zbT"][:].rearrange("p j t -> p (j t)")
            T["kvT"] = place[:, 0:2 * TOK].rearrange("p (c t) -> p c t", c=2)
            T["kcT"] = place[:, 2 * TOK:2 * TOK + NSEQ * 64].rearrange("p (b n) -> p b n", b=NSEQ)
            T["vc"] = place[0:NCMP, 2 * TOK + NSEQ * 64:2 * TOK + NSEQ * (64 + P)].rearrange("p (b n) -> p b n", b=NSEQ)
            with ExitStack() as part:
                T["xc"] = [part.enter_context(nc.sbuf_tensor(f"xc{i}", [P, 2 * NPAGE, 2, 16, 8], F32)) for i in range(2)]
                T["ld_x"] = [part.enter_context(nc.semaphore(f"ld_xc{i}")) for i in range(2)]
                T["ld_wt"], T["ld_pg"] = (part.enter_context(nc.semaphore(n)) for n in ("ld_wt", "ld_pg"))
                T["w1"] = part.enter_context(nc.sbuf_tensor("cmp_w1", [P, 2, RS, P], F32))
                T["ld_w1"] = part.enter_context(nc.semaphore("ld_cmp_w1"))
                place = T["w1"][:].rearrange("p a r n -> p (a r n)")
                T["wt"] = [place[:, i * KT * KVH:(i + 1) * KT * KVH].rearrange("p (k n) -> p k n", k=KT) for i in range(2)]
                stage_input(nc, T)
                stage_nsa_project(nc, T)
                stage_compress(nc, T)
            with ExitStack() as part:
                T["kS"] = part.enter_context(nc.sbuf_tensor("kS", [P, SG, NPAGE, PAGE], F32))
                T["vS"] = part.enter_context(nc.sbuf_tensor("vS", [P, SG, NPAGE, P], F32))
                T["ld_k"], T["ld_v"] = (part.enter_context(nc.semaphore(n)) for n in ("ld_k", "ld_v"))
                stage_prompt_attention(nc, T)
                stage_sample_attention(nc, T)
        stage_gdn_and_output(nc, T)


def layouts(inp):
    a = {k: np.asarray(v) for k, v in inp.items()}
    f = np.float32
    c = np.concatenate([a["c_sample"], a["c_prompt"]], 0)
    x = np.concatenate([a["x_prompt"][0], a["x_sample"].reshape(NS, D_MODEL)], 0)
    o = {}
    o["cT"] = np.ascontiguousarray(c.T.reshape(KT, P, 9).transpose(1, 0, 2))
    o["xT"] = np.ascontiguousarray(x.T.reshape(KT, P, TOK).transpose(1, 0, 2))
    o["x"] = x
    wt = lambda w, n: np.ascontiguousarray(w.reshape(-1, P, w.shape[1] // n, n).transpose(2, 1, 0, 3).reshape(w.shape[1] // n, P, -1))
    o["w_ada"] = wt(a["w_ada"][0], 512)
    o["b_ada"] = np.ascontiguousarray(np.broadcast_to(a["b_ada"][0], (9, 3072)))
    o["norm_gT"] = np.ascontiguousarray(a["norm_g"][0].reshape(KT, P).T)
    w = a["w_in"][0]
    pair = np.arange(512).reshape(2, NJ, HD).transpose(1, 0, 2).reshape(-1)
    q, kv, g = w[:, 0:512], w[:, 512:1280], w[:, 1280:1304]
    za, qkv, ab, zb, gm = w[:, 1304:1816], w[:, 1816:3352], w[:, 3352:3368], w[:, 3368:3880], w[:, 3880:5928]
    o["w_feat_full"] = np.concatenate([q[:, pair], za[:, pair], qkv, zb, gm], 1)
    o["w_tok"] = wt(np.concatenate([kv, g, ab], 1), KVH)
    o["ident"] = np.eye(P, dtype=f)
    extra_layouts(a, o, pair, f)
    return o


def extra_layouts(a, o, pair, f):
    cc = a["cache_cmp_kv"][0]
    o["cmp_pool"] = np.ascontiguousarray(cc.reshape(NPOOL, 8, 16, 2, 2, HD).transpose(0, 4, 5, 3, 2, 1).reshape(NPOOL, P, 256))
    cs = a["cache_sel_kv"][0].reshape(NPOOL, PAGE, 2, P)
    o["sel_k"] = np.ascontiguousarray(cs[:, :, 0].transpose(0, 2, 1))
    o["sel_v"] = np.ascontiguousarray(cs[:, :, 1])
    cw = a["cache_win_kv"][0].reshape(NB, WIN, 2, P)
    o["cache_win"] = cw.reshape(NB, WIN, 2 * P)
    o["win_k"] = np.ascontiguousarray(cw[:, :, 0].reshape(2, 4, WIN, P).transpose(0, 3, 1, 2).reshape(2, P, 4 * WIN))
    o["win_v"] = np.ascontiguousarray(cw[:, :, 1].reshape(2, 4, 4, P, P).transpose(0, 3, 1, 2, 4).reshape(2, P, 16 * P))
    o["pages"] = a["page_table"].reshape(1, NB * NPAGE)
    both = lambda n: np.stack([a[n + "_k"][0], a[n + "_v"][0]])
    blocks = lambda w: np.concatenate([np.pad(w, [(0, 0)] * (w.ndim - 1) + [(g * HD, (1 - g) * HD)]) for g in range(2)], 0)
    o["cmp_w1"] = np.ascontiguousarray(blocks(both("cmp_w1").transpose(2, 0, 1, 3)))
    o["cmp_w2"] = np.ascontiguousarray(blocks(both("cmp_w2").transpose(1, 0, 2)))
    pe = both("cmp_pe").transpose(2, 0, 1)
    o["cmp_pe"] = np.ascontiguousarray(np.concatenate([pe, pe], 0))
    r = np.arange(P)
    g, j, t = (r // 16) % 2, (r // 4) % 4, r % 4
    h = g * NJ + j
    slope = (0.5 ** (h + 1.0))[:, None]
    end = np.arange(NCMP) * 16 + 31
    now = (1024 + t)[:, None]
    tab = np.zeros((P, 1840), f)
    tab[:, 0:63] = -slope * (now - end)
    tab[:, 63:1087] = -slope * (now - np.arange(1024))
    wpos = 512 + np.arange(512)
    tab[:, 1087:1599] = np.where(now - wpos < WIN, -slope * (now - wpos), NEG)
    for G in range(2):
        b = G * 4 + r // 32
        tok = np.arange(NS)
        ok = (tok // 4 == b[:, None]) & (tok % 4 <= t[:, None])
        tab[:, 1599 + 32 * G:1631 + 32 * G] = np.where(ok, -slope * (t[:, None] - tok % 4), NEG)
    i16, j64 = np.arange(NCMP)[:, None] * 16, np.arange(16)[None] * 64
    tab[:NCMP, 1663:1679] = np.clip(np.minimum(i16 + 32, j64 + 64) - np.maximum(i16, j64), 0, None) / 32
    same = (r[:, None] // 32 == r // 32) & (g[:, None] == g) & (t[:, None] == t)
    tab[:, 1679:1807] = same
    tab[:, 1807:1815] = h[:, None] == np.arange(H)
    tab[:, 1815:1831] = np.arange(16)
    tab[:, 1831], tab[:, 1832] = g == 0, g == 1
    o["sample_tab"] = tab
    o["token_sel"] = np.ascontiguousarray(np.stack([(np.arange(NS)[:, None] == (G * 4 + r // 32) * 4 + t) for G in range(2)], 1).astype(f))
    more_layouts(a, o, pair, f)


def more_layouts(a, o, pair, f):
    p, c = np.arange(P)[:, None], np.arange(SEQ)
    d = p - (c - (SEQ - P))
    o["dist"] = np.where(d >= 0, -d, NEG).astype(f)
    d = p - np.arange(P) + WIN
    o["dist_w"] = np.where(d < WIN, -d, NEG).astype(f)
    d = (np.arange(QT)[:, None] * P + np.arange(P))[:, :, None] - (np.arange(64) * 16 + 31)
    o["dist_c"] = np.ascontiguousarray(np.where(d >= 0, -d, NEG).astype(f).transpose(1, 0, 2))
    o["slope"] = np.ascontiguousarray(np.broadcast_to((0.5 ** (np.arange(2) * NJ + np.arange(NJ)[:, None] + 1.0)).reshape(-1), (P, H)).astype(f))
    gdn_layouts(a, o, pair, f)


def gdn_layouts(a, o, pair, f):
    w = o.pop("w_feat_full")
    wt = lambda w, n: np.ascontiguousarray(w.reshape(-1, P, w.shape[1] // n, n).transpose(2, 1, 0, 3).reshape(w.shape[1] // n, P, -1))
    o["w_feat"] = wt(w[:, 0:3072], 256)
    gm = w[:, 3072:].reshape(D_MODEL, 2, KT, P).transpose(0, 2, 1, 3).reshape(D_MODEL, 2048)
    o["w_gm"] = wt(gm, 256)
    o["conv_w"] = np.ascontiguousarray(np.concatenate([a["conv_w"][0], a["conv_b"]], 0).reshape(5, 12, P).transpose(2, 1, 0))
    o["conv_state"] = np.ascontiguousarray(a["state_conv"][0].reshape(NB, 3, 12, P).transpose(3, 2, 0, 1))
    o["gdn_state"] = np.ascontiguousarray(a["state_gdn"][0].reshape(NB, NJ, P, HD).transpose(2, 1, 0, 3))
    o["gdn_ab"] = np.ascontiguousarray(np.broadcast_to(np.stack([a["gdn_dt_bias"][0], a["gdn_a_log"][0]]), (P, 2, H)))
    o["gdn_norm"] = np.ascontiguousarray(np.broadcast_to(a["gdn_norm_g"][0], (P, HD)))
    i = np.arange(P)
    same = i[:, None] // NT == i // NT
    le = i[:, None] <= i
    o["tri"] = np.ascontiguousarray(np.concatenate([le, (le & same)[:, 0:NS]], 1).astype(f))
    o["tot"] = np.ascontiguousarray(same[0:NS].astype(f))
    o["seq"] = np.ascontiguousarray((np.arange(NS)[:, None] // NT == np.arange(NB)).astype(f))
    o["msk"] = np.ascontiguousarray(np.where(np.concatenate([le, (le & same)[:, 0:NS]], 1), 0, NEG).astype(f))
    m = lambda s: (i[:, None] // s == i // s + 1) & (i[:, None] // s % 2 == 1)
    o["lvl"] = np.ascontiguousarray(np.stack([m(1).T] + [m(2 ** n) for n in range(1, 7)], 1).astype(f))
    wo = np.stack([a["w_o_nsa"][0][pair], a["w_o_gdn"][0]])
    o["w_o"] = np.ascontiguousarray(wo.reshape(2, NJ, P, KT, P).transpose(3, 2, 0, 1, 4).reshape(KT, P, -1))
    o["w_out"] = wt(a["w_out"][0], 512)
    o["final_g"] = np.ascontiguousarray(np.broadcast_to(a["final_g"], (P, D_MODEL)))
    o["row_sel"] = np.ascontiguousarray(np.concatenate([np.arange(9)[:, None] == np.full(P, 8), np.arange(9)[:, None] == np.arange(NS) // NT], 1).astype(f))


OUTS = [("y_prompt", (1, SEQ, D_MODEL)), ("y_sample", (NB, NT, D_MODEL)),
        ("cmp_p", (1, 1, SEQ, 2, 2, HD)), ("sel_p", (1, 1, SEQ, 2, 2, HD)), ("win_p", (1, 1, WIN, 2, 2, HD)),
        ("conv_p", (P, 12, 3)), ("gdn_p", (P, NJ, HD)),
        ("cmp_s", (1, NB, NT, 2, 2, HD)), ("sel_s", (1, NB, NT, 2, 2, HD)), ("win_s", (1, NB, WIN, 2, 2, HD)),
        ("conv_s", (P, 12, NB, 3)), ("gdn_s", (P, NJ, NB, HD))]


def kernel(**inputs):
    import concourse.bacc as bacc
    from concourse.bass_utils import run_bass_kernel_spmd

    arrays = layouts(inputs)
    nc = bacc.Bacc("TRN2", target_bir_lowering=False, num_devices=1)
    ins = {k: nc.dram_tensor(f"in_{k}", v.shape, mybir.dt.from_np(v.dtype), kind="ExternalInput").ap() for k, v in arrays.items()}
    outs = {k: nc.dram_tensor(f"out_{k}", s, F32, kind="ExternalOutput").ap() for k, s in OUTS}
    build(nc, ins, outs)
    r = run_bass_kernel_spmd(nc, [{f"in_{k}": v for k, v in arrays.items()}], core_ids=[0]).results[0]
    y = {k: r[f"out_{k}"] for k, _ in OUTS}
    conv_p = y["conv_p"].transpose(2, 1, 0).reshape(1, 1, 3, 1536)
    conv_s = y["conv_s"].transpose(2, 3, 1, 0).reshape(1, NB, 3, 1536)
    gdn_p = y["gdn_p"].reshape(2, HD, NJ, HD).transpose(2, 0, 1, 3).reshape(1, 1, H, HD, HD)
    gdn_s = y["gdn_s"].reshape(2, HD, NJ, NB, HD).transpose(3, 2, 0, 1, 4).reshape(1, NB, H, HD, HD)
    return (y["y_prompt"], y["y_sample"], y["cmp_p"], y["sel_p"], y["win_p"], conv_p, gdn_p,
            y["cmp_s"], y["sel_s"], y["win_s"], conv_s, gdn_s)
```
